# Optimizing a Trainium2 kernel written in Bass

```python
import jax, jax.numpy as jnp
from jax import lax
import numpy as np

D_MODEL = 1024
BATCH = 1
SEQ = 512
DEPTH = 1

N_META = 16
D_SSD = D_MODEL
D_CONF = D_MODEL
D_MIX = D_SSD + D_CONF
SSD_HEADDIM = 64
SSD_HEADS = D_SSD // SSD_HEADDIM
SSD_GROUPS = 4
SSD_HPG = SSD_HEADS // SSD_GROUPS
SSD_STATE = 128
SSD_CONV = 4
SSD_CHUNK = 128
D_XBC = D_SSD + 2 * SSD_GROUPS * SSD_STATE
CONF_KERNEL = 31
D_IN = D_SSD + D_XBC + SSD_HEADS + 2 * D_CONF
PEER_HEADS = 8
PEER_NKEYS = 128
PEER_EXPERTS = PEER_NKEYS * PEER_NKEYS
PEER_DKEY = 256
PEER_TOPK = 16
PEER_BLOCK = 256
EPS = 1e-5


def rmsnorm(x, w):
    xf = x.astype(jnp.float32)
    y = xf * lax.rsqrt(jnp.mean(xf * xf, axis=-1, keepdims=True) + EPS)
    return (y * w.astype(jnp.float32)).astype(x.dtype)

def causal_depthwise_conv(x, w, b):
    k = w.shape[0]
    y = lax.conv_general_dilated(x, w[:, None, :].astype(x.dtype), window_strides=(1,),
                                 padding=[(k - 1, 0)],
                                 dimension_numbers=("NWC", "WIO", "NWC"),
                                 feature_group_count=x.shape[-1])
    return y + b.astype(x.dtype)

def segsum(a):
    t = a.shape[-1]
    cs = jnp.cumsum(a, axis=-1)
    diff = cs[..., :, None] - cs[..., None, :]
    mask = jnp.tril(jnp.ones((t, t), dtype=bool))
    return jnp.where(mask, diff, -jnp.inf)

def ssd_chunked(xh, dt, a_neg, bm, cm):
    b, lp = xh.shape[0], xh.shape[1]
    nc = lp // SSD_CHUNK
    xh = xh.reshape(b, nc, SSD_CHUNK, SSD_GROUPS, SSD_HPG, SSD_HEADDIM)
    dtc = dt.reshape(b, nc, SSD_CHUNK, SSD_GROUPS, SSD_HPG)
    xdt = xh * dtc[..., None]
    bm = bm.reshape(b, nc, SSD_CHUNK, SSD_GROUPS, SSD_STATE)
    cm = cm.reshape(b, nc, SSD_CHUNK, SSD_GROUPS, SSD_STATE)
    dta = jnp.moveaxis(dtc * a_neg.reshape(SSD_GROUPS, SSD_HPG), 2, -1)
    a_cs = jnp.cumsum(dta, axis=-1)
    lmat = jnp.exp(segsum(dta))
    cb = jnp.einsum("bclgn,bcsgn->bcgls", cm, bm)
    y_diag = jnp.einsum("bcgls,bcgrls,bcsgrp->bclgrp", cb, lmat, xdt)
    decay_states = jnp.exp(a_cs[..., -1:] - a_cs)
    states = jnp.einsum("bclgn,bcgrl,bclgrp->bcgrpn", bm, decay_states, xdt)
    chunk_decay = jnp.exp(a_cs[..., -1])

    def step(h, inp):
        s, d = inp
        return h * d[..., None, None] + s, h

    h0 = jnp.zeros((b, SSD_GROUPS, SSD_HPG, SSD_HEADDIM, SSD_STATE), states.dtype)
    _, prev = lax.scan(step, h0, (jnp.moveaxis(states, 1, 0), jnp.moveaxis(chunk_decay, 1, 0)))
    prev = jnp.moveaxis(prev, 0, 1)
    y_off = jnp.einsum("bclgn,bcgrpn,bcgrl->bclgrp", cm, prev, jnp.exp(a_cs))
    return (y_diag + y_off).reshape(b, lp, SSD_HEADS, SSD_HEADDIM)

def ssd_mixer(z, xbc, dt_raw, conv_w, conv_b, dt_bias, a_log, d_skip, norm_w):
    b, l = z.shape[0], z.shape[1]
    xbc = jax.nn.silu(causal_depthwise_conv(xbc, conv_w, conv_b))
    xs, bm, cm = jnp.split(xbc, [D_SSD, D_SSD + SSD_GROUPS * SSD_STATE], axis=-1)
    f32 = jnp.float32
    dt = jax.nn.softplus(dt_raw.astype(f32) + dt_bias.astype(f32))
    a_neg = -jnp.exp(a_log.astype(f32))
    xh = xs.astype(f32).reshape(b, l, SSD_HEADS, SSD_HEADDIM)
    bm = bm.astype(f32).reshape(b, l, SSD_GROUPS, SSD_STATE)
    cm = cm.astype(f32).reshape(b, l, SSD_GROUPS, SSD_STATE)
    pad = (-N_META) % SSD_CHUNK
    padw = lambda t: jnp.pad(t, [(0, 0), (pad, 0)] + [(0, 0)] * (t.ndim - 2))
    y = ssd_chunked(padw(xh), padw(dt), a_neg, padw(bm), padw(cm))[:, pad:]
    y = y + d_skip.astype(f32)[:, None] * xh
    y = y.reshape(b, l, D_SSD) * jax.nn.silu(z.astype(f32))
    yg = y.reshape(b, l, SSD_GROUPS, D_SSD // SSD_GROUPS)
    yg = yg * lax.rsqrt(jnp.mean(yg * yg, axis=-1, keepdims=True) + EPS)
    return (yg.reshape(b, l, D_SSD) * norm_w.astype(f32)).astype(z.dtype)

def conformer_conv(u, conv_w, conv_b, ln_g, ln_b):
    a, g = jnp.split(u, 2, axis=-1)
    h = causal_depthwise_conv(a * jax.nn.sigmoid(g), conv_w, conv_b)
    hf = h.astype(jnp.float32)
    mu = jnp.mean(hf, axis=-1, keepdims=True)
    var = jnp.mean(jnp.square(hf - mu), axis=-1, keepdims=True)
    hn = (hf - mu) * lax.rsqrt(var + EPS) * ln_g.astype(jnp.float32) + ln_b.astype(jnp.float32)
    return jax.nn.silu(hn).astype(u.dtype)

def peer_ffn(x, w_query, sub_keys_1, sub_keys_2, w_down, w_up):
    b, l, d = x.shape
    t = b * l
    xt = x.reshape(t, d)
    q = (xt @ w_query).reshape(t, PEER_HEADS, PEER_DKEY)
    q1, q2 = jnp.split(q, 2, axis=-1)
    s1 = jnp.einsum("thd,hkd->thk", q1, sub_keys_1).astype(jnp.float32)
    s2 = jnp.einsum("thd,hkd->thk", q2, sub_keys_2).astype(jnp.float32)
    v1, i1 = lax.top_k(s1, PEER_TOPK)
    v2, i2 = lax.top_k(s2, PEER_TOPK)
    cand = (v1[..., :, None] + v2[..., None, :]).reshape(t, PEER_HEADS, PEER_TOPK * PEER_TOPK)
    cand_idx = (i1[..., :, None] * PEER_NKEYS + i2[..., None, :]).reshape(t, PEER_HEADS, PEER_TOPK * PEER_TOPK)
    top_s, pos = lax.top_k(cand, PEER_TOPK)
    expert_idx = jnp.take_along_axis(cand_idx, pos, axis=-1)
    gate = jax.nn.softmax(top_s, axis=-1).astype(x.dtype)
    tp = -(-t // PEER_BLOCK) * PEER_BLOCK
    nb = tp // PEER_BLOCK
    xp = jnp.pad(xt, [(0, tp - t), (0, 0)]).reshape(nb, PEER_BLOCK, d)
    ip = jnp.pad(expert_idx, [(0, tp - t), (0, 0), (0, 0)]).reshape(nb, PEER_BLOCK, PEER_HEADS, PEER_TOPK)
    gp = jnp.pad(gate, [(0, tp - t), (0, 0), (0, 0)]).reshape(nb, PEER_BLOCK, PEER_HEADS, PEER_TOPK)

    def block(args):
        xb, ib, gb = args
        u = w_down[ib]
        act = jax.nn.gelu(jnp.einsum("td,thkd->thk", xb, u), approximate=False) * gb
        v = w_up[ib]
        return jnp.einsum("thk,thkd->td", act, v)

    y = lax.map(block, (xp, ip, gp))
    return y.reshape(tp, d)[:t].reshape(b, l, d)

def first_inputs(seed: int = 0) -> dict:
    key = jax.random.key(seed)
    ks = jax.random.split(key, 24)
    nrm = lambda k, shape, s: jax.random.normal(k, shape, jnp.float32) * s
    L = DEPTH
    dt0 = jnp.exp(jax.random.uniform(ks[5], (L, SSD_HEADS), jnp.float32, np.log(1e-3), np.log(1e-1)))
    return {
        "x": nrm(ks[0], (BATCH, SEQ, D_MODEL), 1.0),
        "meta_tokens": nrm(ks[1], (N_META, D_MODEL), 1.0),
        "norm_mix_w": 1.0 + nrm(ks[2], (L, D_MODEL), 0.02),
        "w_in": nrm(ks[3], (L, D_MODEL, D_IN), D_MODEL ** -0.5),
        "ssd_conv_w": nrm(ks[4], (L, SSD_CONV, D_XBC), SSD_CONV ** -0.5),
        "ssd_conv_b": nrm(ks[6], (L, D_XBC), 0.01),
        "ssd_dt_bias": dt0 + jnp.log(-jnp.expm1(-dt0)),
        "ssd_A_log": jnp.log(jax.random.uniform(ks[7], (L, SSD_HEADS), jnp.float32, 1.0, 16.0)),
        "ssd_D": 1.0 + nrm(ks[8], (L, SSD_HEADS), 0.02),
        "ssd_norm_w": 1.0 + nrm(ks[9], (L, D_SSD), 0.02),
        "conf_conv_w": nrm(ks[10], (L, CONF_KERNEL, D_CONF), CONF_KERNEL ** -0.5),
        "conf_conv_b": nrm(ks[11], (L, D_CONF), 0.01),
        "conf_ln_g": 1.0 + nrm(ks[12], (L, D_CONF), 0.02),
        "conf_ln_b": nrm(ks[13], (L, D_CONF), 0.01),
        "w_out": nrm(ks[14], (L, D_MIX, D_MODEL), D_MIX ** -0.5),
        "norm_ffn_w": 1.0 + nrm(ks[15], (L, D_MODEL), 0.02),
        "peer_w_query": nrm(ks[16], (L, D_MODEL, PEER_HEADS * PEER_DKEY), D_MODEL ** -0.5),
        "peer_sub_keys_1": nrm(ks[17], (L, PEER_HEADS, PEER_NKEYS, PEER_DKEY // 2), (PEER_DKEY // 2) ** -0.5),
        "peer_sub_keys_2": nrm(ks[18], (L, PEER_HEADS, PEER_NKEYS, PEER_DKEY // 2), (PEER_DKEY // 2) ** -0.5),
        "peer_w_down": nrm(ks[19], (L, PEER_EXPERTS, D_MODEL), D_MODEL ** -0.5),
        "peer_w_up": nrm(ks[20], (L, PEER_EXPERTS, D_MODEL), 0.25),
        "norm_final_w": 1.0 + nrm(ks[21], (D_MODEL,), 0.02),
    }

def first_block(x, meta_tokens, norm_mix_w, w_in, ssd_conv_w, ssd_conv_b, ssd_dt_bias, ssd_A_log, ssd_D,
              ssd_norm_w, conf_conv_w, conf_conv_b, conf_ln_g, conf_ln_b, w_out, norm_ffn_w,
              peer_w_query, peer_sub_keys_1, peer_sub_keys_2, peer_w_down, peer_w_up, norm_final_w):
    b = x.shape[0]
    meta = jnp.broadcast_to(meta_tokens.astype(x.dtype)[None], (b, N_META, D_MODEL))
    h = jnp.concatenate([meta, x], axis=1)
    for l in range(DEPTH):
        u = rmsnorm(h, norm_mix_w[l])
        proj = u @ w_in[l]
        z, xbc, dt_raw, conf_in = jnp.split(
            proj, [D_SSD, D_SSD + D_XBC, D_SSD + D_XBC + SSD_HEADS], axis=-1)
        y_ssd = ssd_mixer(z, xbc, dt_raw, ssd_conv_w[l], ssd_conv_b[l], ssd_dt_bias[l],
                          ssd_A_log[l], ssd_D[l], ssd_norm_w[l])
        y_conf = conformer_conv(conf_in, conf_conv_w[l], conf_conv_b[l], conf_ln_g[l], conf_ln_b[l])
        h = h + jnp.concatenate([y_ssd, y_conf], axis=-1) @ w_out[l]
        h = h + peer_ffn(rmsnorm(h, norm_ffn_w[l]), peer_w_query[l], peer_sub_keys_1[l],
                         peer_sub_keys_2[l], peer_w_down[l], peer_w_up[l])
    return rmsnorm(h, norm_final_w)[:, N_META:]


HEAD_DIM = 64
N_Q_HEADS = 8
N_KV_HEADS = 2
Q_REP = N_Q_HEADS // N_KV_HEADS
ATTN_WIDTH = N_Q_HEADS * HEAD_DIM
KV_WIDTH = N_KV_HEADS * HEAD_DIM
WINDOW = 128
ATTN_BLOCK = 128
N_GMLP_GROUPS = 8
GMLP_WIDTH = D_MODEL - ATTN_WIDTH
GMLP_GROUP_DIM = GMLP_WIDTH // N_GMLP_GROUPS
CHUNK = 128
MIX_WIDTH = ATTN_WIDTH + GMLP_WIDTH
IN_WIDTH = ATTN_WIDTH + 2 * KV_WIDTH + 2 * GMLP_WIDTH
N_EXPERTS = 32
TOP_K = 4
D_FF = D_MODEL
SWIGLU_LIMIT = 7.0
SWIGLU_ALPHA = 1.702
MOE_BLOCK = 128
LN_EPS = 1e-5
DEEPNORM_ALPHA = (2.0 * DEPTH) ** 0.25
DEEPNORM_BETA = (8.0 * DEPTH) ** -0.25
NEG_INF = -1e30


def layer_norm(x, g, b):
    xf = x.astype(jnp.float32)
    mu = jnp.mean(xf, axis=-1, keepdims=True)
    xc = xf - mu
    var = jnp.mean(xc * xc, axis=-1, keepdims=True)
    return (xc * lax.rsqrt(var + LN_EPS)).astype(x.dtype) * g + b

def sliding_window_attention(q, k, v, sinks):
    B, S = q.shape[:2]
    nb = S // ATTN_BLOCK
    q = q.reshape(B, nb, ATTN_BLOCK, N_KV_HEADS, Q_REP, HEAD_DIM)
    k = k.reshape(B, nb, ATTN_BLOCK, N_KV_HEADS, HEAD_DIM)
    v = v.reshape(B, nb, ATTN_BLOCK, N_KV_HEADS, HEAD_DIM)

    def band(t):
        prev = jnp.pad(t[:, :-1], ((0, 0), (1, 0), (0, 0), (0, 0), (0, 0)))
        return jnp.concatenate([prev, t], axis=2)

    kb, vb = band(k), band(v)
    scores = jnp.einsum('bnqgrd,bnkgd->bngrqk', q, kb).astype(jnp.float32) * (HEAD_DIM ** -0.5)
    t_idx = jnp.arange(ATTN_BLOCK)[:, None]
    s_idx = jnp.arange(2 * ATTN_BLOCK)[None, :]
    diff = t_idx + ATTN_BLOCK - s_idx
    in_band = (diff >= 0) & (diff < WINDOW)
    blk = jnp.arange(nb)[:, None, None]
    valid = in_band[None] & ((blk * ATTN_BLOCK - ATTN_BLOCK + s_idx[None]) >= 0)
    scores = jnp.where(valid[None, :, None, None], scores, NEG_INF)
    sink = sinks.astype(jnp.float32).reshape(N_KV_HEADS, Q_REP)[None, None, :, :, None, None]
    sink = jnp.broadcast_to(sink, scores.shape[:-1] + (1,))
    probs = jax.nn.softmax(jnp.concatenate([scores, sink], axis=-1), axis=-1)[..., :-1]
    out = jnp.einsum('bngrqk,bnkgd->bnqgrd', probs.astype(v.dtype), vb)
    return out.reshape(B, S, ATTN_WIDTH)

def chunked_spatial_gating(u, g, ln_g, ln_b, w_s, b_s):
    B, S = u.shape[:2]
    nc = S // CHUNK
    u = jax.nn.gelu(u)
    g = jax.nn.gelu(g).reshape(B, S, N_GMLP_GROUPS, GMLP_GROUP_DIM)
    g = layer_norm(g, ln_g.reshape(N_GMLP_GROUPS, GMLP_GROUP_DIM), ln_b.reshape(N_GMLP_GROUPS, GMLP_GROUP_DIM))
    g = g.reshape(B, nc, CHUNK, N_GMLP_GROUPS, GMLP_GROUP_DIM)
    causal = jnp.tril(jnp.ones((CHUNK, CHUNK), dtype=bool))
    w = jnp.where(causal[None], w_s, jnp.zeros_like(w_s))
    mixed = jnp.einsum('gts,bcsgd->bctgd', w, g) + b_s.T[None, None, :, :, None]
    return u * mixed.reshape(B, S, GMLP_WIDTH)

def token_mixer(x, w_in, b_in, sinks, ln_v_g, ln_v_b, w_spatial, b_spatial, w_out, b_out):
    proj = x @ w_in + b_in
    o1 = ATTN_WIDTH
    o2 = o1 + KV_WIDTH
    o3 = o2 + KV_WIDTH
    o4 = o3 + GMLP_WIDTH
    q, k, v = proj[..., :o1], proj[..., o1:o2], proj[..., o2:o3]
    u, g = proj[..., o3:o4], proj[..., o4:]
    attn = sliding_window_attention(q, k, v, sinks)
    sgu = chunked_spatial_gating(u, g, ln_v_g, ln_v_b, w_spatial, b_spatial)
    return jnp.concatenate([attn, sgu], axis=-1) @ w_out + b_out

def routed_experts(x, w_router, b_router, w_gate, b_gate, w_up, b_up, w_down, b_down):
    B, S, D = x.shape
    T = B * S
    TK = T * TOP_K
    xt = x.reshape(T, D)
    logits = (xt @ w_router + b_router).astype(jnp.float32)
    top_vals, top_idx = lax.top_k(logits, TOP_K)
    gates = jax.nn.softmax(top_vals, axis=-1).astype(x.dtype)
    flat_e = top_idx.reshape(-1)
    flat_tok = jnp.arange(TK, dtype=jnp.int32) // TOP_K
    order = jnp.argsort(flat_e)
    sorted_e = flat_e[order]
    counts = jnp.bincount(flat_e, length=N_EXPERTS)
    start = jnp.cumsum(counts) - counts
    padded = (counts + MOE_BLOCK - 1) // MOE_BLOCK * MOE_BLOCK
    padded_end = jnp.cumsum(padded)
    padded_start = padded_end - padded
    dest = padded_start[sorted_e] + jnp.arange(TK, dtype=jnp.int32) - start[sorted_e]
    n_blocks = TK // MOE_BLOCK + N_EXPERTS
    n_rows = n_blocks * MOE_BLOCK
    row_tok = jnp.full((n_rows,), T, dtype=jnp.int32).at[dest].set(flat_tok[order])
    row_gate = jnp.zeros((n_rows,), x.dtype).at[dest].set(gates.reshape(-1)[order])
    block_e = jnp.minimum(
        jnp.searchsorted(padded_end, jnp.arange(n_blocks, dtype=padded_end.dtype) * MOE_BLOCK, side='right'),
        N_EXPERTS - 1)
    x_rows = jnp.concatenate([xt, jnp.zeros((1, D), xt.dtype)], axis=0)[row_tok]
    x_rows = x_rows.reshape(n_blocks, MOE_BLOCK, D)

    def expert_block(args):
        xb, e = args
        gt = jnp.minimum(xb @ w_gate[e] + b_gate[e], SWIGLU_LIMIT)
        up = jnp.clip(xb @ w_up[e] + b_up[e], -SWIGLU_LIMIT, SWIGLU_LIMIT)
        hid = gt * jax.nn.sigmoid(SWIGLU_ALPHA * gt) * (up + 1.0)
        return hid @ w_down[e] + b_down[e]

    y_rows = lax.map(expert_block, (x_rows, block_e)).reshape(n_rows, D)
    out = jnp.zeros((T + 1, D), x.dtype).at[row_tok].add(y_rows * row_gate[:, None])[:T]
    return out.reshape(B, S, D)

def second_inputs(seed: int = 0) -> dict:
    key = jax.random.key(seed)
    ks = jax.random.split(key, 24)
    f32 = jnp.float32

    def nrm(k, shape, scale):
        return jax.random.normal(k, (DEPTH,) + shape, f32) * scale

    x = jax.random.normal(ks[0], (BATCH, SEQ, D_MODEL), f32)
    col_scale = jnp.concatenate([
        jnp.ones((ATTN_WIDTH + KV_WIDTH,), f32),
        jnp.full((KV_WIDTH,), DEEPNORM_BETA, f32),
        jnp.full((GMLP_WIDTH,), DEEPNORM_BETA, f32),
        jnp.ones((GMLP_WIDTH,), f32)])
    w_in = nrm(ks[1], (D_MODEL, IN_WIDTH), D_MODEL ** -0.5) * col_scale
    b_in = nrm(ks[2], (IN_WIDTH,), 0.02)
    sinks = nrm(ks[3], (N_Q_HEADS,), 0.5)
    ln_v_g = 1.0 + nrm(ks[4], (GMLP_WIDTH,), 0.05)
    ln_v_b = nrm(ks[5], (GMLP_WIDTH,), 0.02)
    w_spatial = nrm(ks[6], (N_GMLP_GROUPS, CHUNK, CHUNK), CHUNK ** -0.5)
    b_spatial = 1.0 + nrm(ks[7], (N_GMLP_GROUPS, CHUNK), 0.05)
    w_out = nrm(ks[8], (MIX_WIDTH, D_MODEL), MIX_WIDTH ** -0.5 * DEEPNORM_BETA)
    b_out = nrm(ks[9], (D_MODEL,), 0.02)
    ln1_g = 1.0 + nrm(ks[10], (D_MODEL,), 0.05)
    ln1_b = nrm(ks[11], (D_MODEL,), 0.02)
    w_router = nrm(ks[12], (D_MODEL, N_EXPERTS), D_MODEL ** -0.5)
    b_router = nrm(ks[13], (N_EXPERTS,), 0.01)
    w_gate = nrm(ks[14], (N_EXPERTS, D_MODEL, D_FF), D_MODEL ** -0.5)
    b_gate = nrm(ks[15], (N_EXPERTS, D_FF), 0.02)
    w_up = nrm(ks[16], (N_EXPERTS, D_MODEL, D_FF), D_MODEL ** -0.5 * DEEPNORM_BETA)
    b_up = nrm(ks[17], (N_EXPERTS, D_FF), 0.02)
    w_down = nrm(ks[18], (N_EXPERTS, D_FF, D_MODEL), D_FF ** -0.5 * DEEPNORM_BETA)
    b_down = nrm(ks[19], (N_EXPERTS, D_MODEL), 0.02)
    ln2_g = 1.0 + nrm(ks[20], (D_MODEL,), 0.05)
    ln2_b = nrm(ks[21], (D_MODEL,), 0.02)
    return {"x": x, "w_in": w_in, "b_in": b_in, "sinks": sinks, "ln_v_g": ln_v_g, "ln_v_b": ln_v_b,
            "w_spatial": w_spatial, "b_spatial": b_spatial, "w_out": w_out, "b_out": b_out,
            "ln1_g": ln1_g, "ln1_b": ln1_b, "w_router": w_router, "b_router": b_router,
            "w_gate": w_gate, "b_gate": b_gate, "w_up": w_up, "b_up": b_up,
            "w_down": w_down, "b_down": b_down, "ln2_g": ln2_g, "ln2_b": ln2_b}

def second_block(x, w_in, b_in, sinks, ln_v_g, ln_v_b, w_spatial, b_spatial, w_out, b_out,
              ln1_g, ln1_b, w_router, b_router, w_gate, b_gate, w_up, b_up,
              w_down, b_down, ln2_g, ln2_b):
    for l in range(DEPTH):
        mix = token_mixer(x, w_in[l], b_in[l], sinks[l], ln_v_g[l], ln_v_b[l],
                          w_spatial[l], b_spatial[l], w_out[l], b_out[l])
        h = layer_norm(DEEPNORM_ALPHA * x + mix, ln1_g[l], ln1_b[l])
        ffn = routed_experts(h, w_router[l], b_router[l], w_gate[l], b_gate[l],
                             w_up[l], b_up[l], w_down[l], b_down[l])
        x = layer_norm(DEEPNORM_ALPHA * h + ffn, ln2_g[l], ln2_b[l])
    return x


def setup_inputs(seed=0):
    out = dict(first_inputs(seed))
    for name, value in second_inputs(seed + 1).items():
        if name != "x":
            out[name + "_2"] = value
    return out


def reference(
    x, meta_tokens, norm_mix_w, w_in, ssd_conv_w, ssd_conv_b, ssd_dt_bias, ssd_A_log, ssd_D,
    ssd_norm_w, conf_conv_w, conf_conv_b, conf_ln_g, conf_ln_b, w_out, norm_ffn_w, peer_w_query,
    peer_sub_keys_1, peer_sub_keys_2, peer_w_down, peer_w_up, norm_final_w, w_in_2, b_in_2,
    sinks_2, ln_v_g_2, ln_v_b_2, w_spatial_2, b_spatial_2, w_out_2, b_out_2, ln1_g_2, ln1_b_2,
    w_router_2, b_router_2, w_gate_2, b_gate_2, w_up_2, b_up_2, w_down_2, b_down_2, ln2_g_2,
    ln2_b_2,
):
    x = first_block(
        x, meta_tokens, norm_mix_w, w_in, ssd_conv_w, ssd_conv_b, ssd_dt_bias, ssd_A_log, ssd_D,
        ssd_norm_w, conf_conv_w, conf_conv_b, conf_ln_g, conf_ln_b, w_out, norm_ffn_w,
        peer_w_query, peer_sub_keys_1, peer_sub_keys_2, peer_w_down, peer_w_up, norm_final_w,
    )
    return second_block(
        x, w_in_2, b_in_2, sinks_2, ln_v_g_2, ln_v_b_2, w_spatial_2, b_spatial_2, w_out_2,
        b_out_2, ln1_g_2, ln1_b_2, w_router_2, b_router_2, w_gate_2, b_gate_2, w_up_2, b_up_2,
        w_down_2, b_down_2, ln2_g_2, ln2_b_2,
    )


_drawn_inputs = setup_inputs


def setup_inputs(seed=0):
    import zlib

    import numpy as np

    out = dict(_drawn_inputs(seed))
    spreads = {}
    factors = {'ssd_conv_b': 2.778,
     'ssd_D': 10.657,
     'conf_conv_b': 3.146,
     'conf_ln_g': 2.779,
     'conf_ln_b': 5.152,
     'b_in_2': 3.62,
     'sinks_2': 49.815,
     'ln_v_g_2': 6.527,
     'ln_v_b_2': 24.121,
     'b_spatial_2': 4.153,
     'b_router_2': 4.347,
     'b_gate_2': 8.0,
     'b_up_2': 8.0,
     'b_down_2': 6.364,
     'ln2_b_2': 2.852,
     'ssd_norm_w': 2.751,
     'norm_ffn_w': 2.884,
     'b_out_2': 2.699}
    for name, (base, spread) in spreads.items():
        noise = np.random.default_rng([zlib.crc32(name.encode()), seed]).standard_normal(out[name].shape)
        drawn = base * np.exp(spread * noise) if base else spread * noise
        out[name] = __import__('jax').numpy.asarray(drawn.astype(out[name].dtype))
    for name, factor in factors.items():
        out[name] = (out[name] * factor).astype(out[name].dtype)
    return out
```

```python
from contextlib import ExitStack

import concourse.bass as bass
from concourse import mybir

F32 = mybir.dt.float32
I32 = mybir.dt.int32
U32 = mybir.dt.uint32
ACT = mybir.ActivationFunctionType
ALU = mybir.AluOpType
AX = mybir.AxisListType

P = 128
D = 1024
KD = D // P
T = 512
M = T // P
META = 16
TA = T + META
HALF = TA // 2
EPS = 1e-5
D_XBC = 2048
HEADS = 16
GROUPS = 4
XT = KD
NB, NC_ = 4, 4
CONV = 4
CK = 31
COL_XBC, COL_DT, COL_A, COL_G = 1024, 3072, 3088, 4112
PH = 8
TOPK = 16
NK = 128
ds = bass.ds


def chained(eng, sem, start=0):
    n = [start]

    def step(ins):
        n[0] += 1
        ins.then_inc(sem, 1)
        eng.wait_ge(sem, n[0])
    return step


class Stage:

    def __init__(self, nc, name):
        self.nc, self.name, self.ctx, self.sems = nc, name, ExitStack(), []

    def __enter__(self):
        self.ctx.__enter__()
        return self

    def __exit__(self, *a):
        if a[0] is None:
            self.nc.clear_and_free_semaphores(self.sems)
            self.nc.all_engine_barrier()
        return self.ctx.__exit__(*a)

    def sb(self, name, shape, dt=F32):
        return self.ctx.enter_context(self.nc.sbuf_tensor(f"{self.name}_{name}", shape, dt))

    def ps(self, name, shape, dt=F32):
        return self.ctx.enter_context(self.nc.psum_tensor(f"{self.name}_{name}", shape, dt))

    def sem(self, name):
        self.sems.append(self.nc.alloc_semaphore(f"{self.name}_{name}"))
        return self.sems[-1]

    def block(self):
        return self.nc.Block()


def tokens(ap):
    return ap.rearrange("(m p) d -> p m d", p=P)


def rows(ap):
    return ap.rearrange("(k p) n -> p k n", p=P)


def stage_constants(nc, c):
    with Stage(nc, "const") as s:
        made = s.sem("made")
        with s.block() as block:

            @block.gpsimd
            def _(pool):
                pool.memset(c.ident[:], 0.0).then_inc(made, 1)
                pool.memset(c.ones[:], 1.0).then_inc(made, 1)
                pool.wait_ge(made, 2)
                pool.affine_select(out=c.ident[:], in_=c.ident[:], compare_op=ALU.not_equal, fill=1.0, base=0,
                                   pattern=[[-1, P]], channel_multiplier=1).then_inc(made, 1)
                pool.affine_select(out=c.upper[:], in_=c.ones[:], compare_op=ALU.is_ge, fill=0.0, base=0,
                                   pattern=[[1, P]], channel_multiplier=-1).then_inc(made, 1)
                pool.iota(c.count_i[:], pattern=[[1, P]], base=0, channel_multiplier=0).then_inc(made, 1)
                pool.wait_ge(made, 5)
                pool.tensor_copy(c.count[:], c.count_i[:]).then_inc(made, 1)
                pool.wait_ge(made, 6)


def stage_norm_in(nc, c, a):
    with Stage(nc, "norm") as s:
        x = s.sb("x", [P, M + 1, D])
        junk = s.sb("junk", [P, D])
        wn = s.sb("wn", [P, KD])
        ss = s.sb("ss", [P, M + 1])
        root = s.sb("root", [P, M + 1])
        tp = s.ps("tp", [P, 4, 4, P])
        loaded = [s.sem(f"loaded{m}") for m in range(M + 1)]
        wn_in = s.sem("wn_in")
        cleared, squared, rooted, scaled = (s.sem(n) for n in ("cleared", "squared", "rooted", "scaled"))
        chain, turned, copied = s.sem("chain"), s.sem("turned"), s.sem("copied")
        with s.block() as block:

            @block.sync
            def _(sp):
                for m in range(M):
                    sp.dma_start(x[:, m, :], tokens(a["x"][0])[:, m, :]).then_inc(loaded[m], 16)
                sp.dma_start(x[0:META, M, :], a["meta_tokens"]).then_inc(loaded[M], 16)
                sp.dma_start(wn[:], a["norm_mix_w"]).then_inc(wn_in, 16)

            @block.scalar
            def _(act):
                act.wait_ge(cleared, 1)
                for m in range(M + 1):
                    n = P if m < M else META
                    act.wait_ge(loaded[m], 16)
                    act.activation(junk[0:n, :], x[0:n, m, :], ACT.Square,
                                   accum_out=ss[0:n, m:m + 1]).then_inc(squared, 1)
                    act.wait_ge(squared, m + 1)
                act.wait_ge(scaled, 1)
                act.activation(root[:], root[:], ACT.Sqrt).then_inc(rooted, 1)

            @block.vector
            def _(dve):
                step = chained(dve, chain)
                dve.memset(ss[:], 1.0).then_inc(cleared, 1)
                dve.wait_ge(squared, M + 1)
                dve.tensor_scalar(root[:], ss[:], 1.0 / D, EPS, ALU.mult, ALU.add).then_inc(scaled, 1)
                dve.wait_ge(rooted, 1)
                step(dve.reciprocal(ss[:], root[:]))
                for m in (M, *range(M)):
                    n = P if m < M else META
                    dve.tensor_scalar(x[0:n, m, :], x[0:n, m, :], ss[0:n, m:m + 1], None,
                                      ALU.mult).then_inc(scaled, 1)
                dve.wait_ge(wn_in, 16)
                i = 0
                for m in (M, *range(M)):
                    n, at = (P, META + m * P) if m < M else (META, 0)
                    for h in range(2):
                        dve.wait_ge(turned, i + 1)
                        dve.tensor_tensor(c.uT[:, 4 * h:4 * h + 4, at:at + n], tp[:, i % 4, :, 0:n],
                                          wn[:, 4 * h:4 * h + 4].unsqueeze(2).to_broadcast([P, 4, n]),
                                          ALU.mult).then_inc(copied, 1)
                        i += 1

            @block.tensor
            def _(pe):
                i = 0
                for j, m in enumerate((M, *range(M))):
                    n = P if m < M else META
                    pe.wait_ge(scaled, 2 + j)
                    for h in range(2):
                        if i >= 4:
                            pe.wait_ge(copied, i - 3)
                        for k in range(4):
                            t = pe.transpose(tp[:, i % 4, k, 0:n], x[0:n, m, (4 * h + k) * P:(4 * h + k + 1) * P],
                                             c.ident[0:n, 0:n])
                        t.then_inc(turned, 1)
                        i += 1


def stage_project(nc, c, a):
    w_in = rows(a["w_in"][0])
    with Stage(nc, "proj") as s:
        w = [s.sb(f"w{b}", [P, KD, 512]) for b in range(2)]
        wdt = s.sb("wdt", [P, KD, HEADS])
        taps = s.sb("taps", [P, KD, CK])
        cbias = s.sb("cbias", [P, KD])
        xtaps = s.sb("xtaps", [P, 16, CONV])
        xbias = s.sb("xbias", [P, 16])
        dtb = s.sb("dtb", [P, HEADS])
        sg = s.sb("sg", [P, 2, TA])
        pad = CK - 1 - META
        gated = s.sb("gated", [P, 2, pad + TA])
        raw = s.sb("raw", [P, 2, CONV - 1 + TA])
        acc = s.sb("acc", [P, 2, TA])
        e1 = s.sb("e1", [P, M + 1, HEADS])
        e2 = s.sb("e2", [P, M + 1, HEADS])
        e3 = s.sb("e3", [P, M + 1, HEADS])
        ps = s.ps("ps", [P, 8, 512])
        w_in_sem = [s.sem(f"w_in{b}") for b in range(2)]
        consts_in = s.sem("consts_in")
        w_used = s.sem("w_used")
        pair_done, pair_free = s.sem("pair_done"), s.sem("pair_free")
        sig, g_ready, chain = s.sem("sig"), s.sem("g_ready"), s.sem("chain")
        raw_in, raw_free, conv_out, silu_out = (s.sem(n) for n in ("raw_in", "raw_free", "conv_out", "silu_out"))
        zeroed = s.sem("zeroed")
        dt_done, dt_raw, dt_e, dt_l, dt_ok = (s.sem(n) for n in ("dt_done", "dt_raw", "dt_e", "dt_l", "dt_ok"))

        def columns(block_no):
            return [COL_A, COL_G, COL_A + 512, COL_G + 512,
                    *(COL_XBC + 512 * i for i in range(4)), 0, 512][block_no]

        with s.block() as block:

            @block.sync
            def _(sp):
                sp.dma_start(wdt[:], w_in[:, :, COL_DT:COL_DT + HEADS]).then_inc(consts_in, 16)
                sp.dma_start(dtb[:], a["ssd_dt_bias"].to_broadcast([P, HEADS])).then_inc(consts_in, 16)
                sp.dma_start(taps[:], a["conf_taps"]).then_inc(consts_in, 16)
                sp.dma_start(cbias[:], a["conf_conv_b"]).then_inc(consts_in, 16)
                sp.dma_start(xtaps[:], a["ssd_taps"]).then_inc(consts_in, 16)
                sp.dma_start(xbias[:], a["ssd_conv_b"]).then_inc(consts_in, 16)
                for n in range(10):
                    if n >= 2:
                        sp.wait_ge(w_used, n - 1)
                    at = columns(n)
                    sp.dma_start(w[n % 2][:], w_in[:, :, at:at + 512]).then_inc(w_in_sem[n % 2], 16)

            @block.tensor
            def _(pe):
                pe.wait_ge(consts_in, 96)
                for m in range(M + 1):
                    n, at = (META, 0) if m == 0 else (P, META + (m - 1) * P)
                    for k in range(KD):
                        mm = pe.matmul(ps[0:n, 7, 16 * m:16 * m + 16], c.uT[:, k, at:at + n], wdt[:, k, :],
                                       start=(k == 0), stop=(k == KD - 1))
                mm.then_inc(dt_done, 1)
                job = 0

                def tile(buf, col, first=0):
                    nonlocal job
                    if job == 3:
                        pe.wait_ge(dt_raw, 1)
                    if job >= 4:
                        pe.wait_ge(pair_free, job - 3)
                    for h in range(2):
                        for k in range(KD):
                            mm = pe.matmul(ps[:, 2 * (job % 4) + h, 0:HALF], w[buf][:, k, col * P:col * P + P],
                                           c.uT[:, k, h * HALF:(h + 1) * HALF], start=(k == 0), stop=(k == KD - 1))
                    mm.then_inc(pair_done, 1)
                    job += 1
                    return mm

                for half in range(2):
                    pe.wait_ge(w_in_sem[0], 16 * (half + 1))
                    pe.wait_ge(w_in_sem[1], 16 * (half + 1))
                    for i in range(4):
                        tile(0, i)
                        if i == 3:
                            pe.sem_inc(w_used, 1) if False else None
                        tile(1, i)
                    pe.wait_ge(pair_done, job)
                    pe.sem_inc(w_used, 2)
                for n in range(4, 10):
                    pe.wait_ge(w_in_sem[n % 2], 16 * (n // 2 + 1))
                    for i in range(4):
                        tile(n % 2, i)
                    pe.wait_ge(pair_done, job)
                    pe.sem_inc(w_used, 1)

            @block.scalar
            def _(act):
                act.wait_ge(dt_raw, 2)
                act.activation(e2[:], e1[:], ACT.Exp, scale=-1.0).then_inc(dt_e, 1)
                act.wait_ge(dt_e, 1)
                act.activation(e3[:], e2[:], ACT.Ln, bias=1.0).then_inc(dt_l, 1)
                for i in range(8):
                    act.wait_ge(pair_done, 2 * i + 2)
                    if i >= 2:
                        act.wait_ge(g_ready, i - 1)
                    act.activation(sg[:, i % 2, :].rearrange("p (h n) -> p h n", h=2),
                                   ps[:, 2 * ((2 * i + 1) % 4):2 * ((2 * i + 1) % 4) + 2, 0:HALF],
                                   ACT.Sigmoid).then_inc(sig, 1)
                for i in range(16):
                    job = 16 + i
                    act.wait_ge(pair_done, job + 1)
                    act.wait_ge(zeroed, 4)
                    if i >= 2:
                        act.wait_ge(conv_out, i - 1)
                    act.activation(raw[:, i % 2, CONV - 1:].rearrange("p (h n) -> p h n", h=2),
                                   ps[:, 2 * (job % 4):2 * (job % 4) + 2, 0:HALF], ACT.Copy).then_inc(raw_in, 1)
                    if i >= 1:
                        act.wait_ge(conv_out, i)
                        act.activation(c.xbcT[:, i - 1, :], acc[:, (i - 1) % 2, :], ACT.Silu).then_inc(silu_out, 1)
                act.wait_ge(conv_out, 16)
                act.activation(c.xbcT[:, 15, :], acc[:, 1, :], ACT.Silu).then_inc(silu_out, 1)
                for i in range(8):
                    job = 32 + i
                    act.wait_ge(pair_done, job + 1)
                    b = 2 * (job % 4)
                    act.activation(c.zT[:, i, 0:HALF - META], ps[:, b, META:HALF], ACT.Silu)
                    act.activation(c.zT[:, i, HALF - META:T], ps[:, b + 1, 0:HALF], ACT.Silu).then_inc(silu_out, 1)

            @block.vector
            def _(dve):
                step = chained(dve, chain)
                for b in range(2):
                    dve.memset(gated[:, b, 0:pad], 0.0).then_inc(zeroed, 1)
                    dve.memset(raw[:, b, 0:CONV - 1], 0.0).then_inc(zeroed, 1)
                step(dve.memset(e1[:], 0.0))
                step(dve.memset(c.dt[:], 0.0))
                dve.wait_ge(dt_done, 1)
                dtp = ps[:, 7, 0:16 * (M + 1)].rearrange("p (m h) -> p m h", m=M + 1)
                bias = dtb[:].unsqueeze(1).to_broadcast([P, M, HEADS])
                step(dve.tensor_tensor(c.dt[:, 1:M + 1, :], dtp[:, 1:M + 1, :], bias, ALU.add))
                dve.tensor_tensor(c.dt[0:META, 0, :], dtp[0:META, 0, :], dtb[0:META, :], ALU.add).then_inc(dt_raw, 1)
                dve.wait_ge(dt_raw, 1)
                step(dve.tensor_scalar(e2[:], c.dt[:], -1.0, None, ALU.mult))
                dve.tensor_tensor(e1[:], e2[:], c.dt[:], ALU.max).then_inc(dt_raw, 1)
                dve.wait_ge(dt_l, 1)
                step(dve.tensor_scalar(e1[:], e2[:], 1.0, None, ALU.add))
                step(dve.tensor_scalar(e1[:], e1[:], -1.0, None, ALU.add))
                step(dve.tensor_scalar(c.dta[:], e1[:], 0.0, None, ALU.is_equal))
                step(dve.tensor_tensor(e1[:], e1[:], c.dta[:], ALU.add))
                step(dve.tensor_tensor(e3[:], e3[:], c.dta[:], ALU.add))
                step(dve.reciprocal(e1[:], e1[:]))
                step(dve.tensor_tensor(e3[:], e3[:], e1[:], ALU.mult))
                step(dve.tensor_tensor(e3[:], e3[:], e2[:], ALU.mult))
                for n, m in ((META, slice(0, 1)), (P, slice(1, M + 1))):
                    step(dve.scalar_tensor_tensor(out=c.dt[0:n, m, :], in0=c.dt[0:n, m, :], scalar=0.0,
                                                  in1=e3[0:n, m, :], op0=ALU.max, op1=ALU.add))
                for i in range(8):
                    dve.wait_ge(sig, i + 1)
                    b = 2 * ((2 * i) % 4)
                    dve.tensor_tensor(gated[:, i % 2, pad:].rearrange("p (h n) -> p h n", h=2), ps[:, b:b + 2, 0:HALF],
                                      sg[:, i % 2, :].rearrange("p (h n) -> p h n", h=2), ALU.mult).then_inc(g_ready, 1)
                    dve.wait_ge(g_ready, i + 1)
                    dve.sem_inc(pair_free, 2)
                    y = c.yT[:, KD + i, :]
                    step(dve.tensor_scalar(y, gated[:, i % 2, 0:T], taps[:, i, 0:1], cbias[:, i:i + 1],
                                           ALU.mult, ALU.add))
                    for k in range(1, CK):
                        step(dve.scalar_tensor_tensor(out=y, in0=gated[:, i % 2, k:k + T], scalar=taps[:, i, k:k + 1],
                                                      in1=y, op0=ALU.mult, op1=ALU.add))
                for i in range(16):
                    dve.wait_ge(raw_in, i + 1)
                    dve.sem_inc(pair_free, 1)
                    if i >= 2:
                        dve.wait_ge(silu_out, i - 1)
                    y = acc[:, i % 2, :]
                    step(dve.tensor_scalar(y, raw[:, i % 2, 0:TA], xtaps[:, i, 0:1], xbias[:, i:i + 1],
                                           ALU.mult, ALU.add))
                    for k in range(1, CONV):
                        ins = dve.scalar_tensor_tensor(out=y, in0=raw[:, i % 2, k:k + TA], scalar=xtaps[:, i, k:k + 1],
                                                       in1=y, op0=ALU.mult, op1=ALU.add)
                        if k < CONV - 1:
                            step(ins)
                    ins.then_inc(conv_out, 1)
                    dve.wait_ge(conv_out, i + 1)
                for i in range(8):
                    dve.wait_ge(silu_out, 17 + i)
                    dve.sem_inc(pair_free, 1)


def stage_conf_norm(nc, c, a):
    with Stage(nc, "cnorm") as s:
        sq = s.sb("sq", [P, KD, T])
        rstd = s.sb("rstd", [P, T])
        gam = s.sb("gam", [P, KD])
        bet = s.sb("bet", [P, KD])
        tot = s.ps("tot", [P, 2, T])
        consts_in = s.sem("consts_in")
        summed, centred, squared, var, root, chain, normed, done = (
            s.sem(n) for n in ("summed", "centred", "squared", "var", "root", "chain", "normed", "done"))
        with s.block() as block:

            @block.sync
            def _(sp):
                sp.dma_start(gam[:], a["conf_ln_g"]).then_inc(consts_in, 16)
                sp.dma_start(bet[:], a["conf_ln_b"]).then_inc(consts_in, 16)

            @block.tensor
            def _(pe):
                for i in range(KD):
                    mm = pe.matmul(tot[:, 0, :], c.ones[:], c.yT[:, KD + i, :], start=(i == 0), stop=(i == KD - 1))
                mm.then_inc(summed, 1)
                for i in range(KD):
                    pe.wait_ge(squared, i + 1)
                    mm = pe.matmul(tot[:, 1, :], c.ones[:], sq[:, i, :], start=(i == 0), stop=(i == KD - 1))
                mm.then_inc(summed, 1)

            @block.vector
            def _(dve):
                step = chained(dve, chain)
                dve.wait_ge(summed, 1)
                for i in range(KD):
                    y = c.yT[:, KD + i, :]
                    dve.scalar_tensor_tensor(out=y, in0=tot[:, 0, :], scalar=-1.0 / D, in1=y,
                                             op0=ALU.mult, op1=ALU.add).then_inc(centred, 1)
                dve.wait_ge(summed, 2)
                dve.tensor_scalar(rstd[:], tot[:, 1, :], 1.0 / D, EPS, ALU.mult, ALU.add).then_inc(var, 1)
                dve.wait_ge(root, 1)
                step(dve.reciprocal(rstd[:], rstd[:]))
                for i in range(KD):
                    y = c.yT[:, KD + i, :]
                    dve.tensor_tensor(y, y, rstd[:], ALU.mult).then_inc(normed, 1)

            @block.scalar
            def _(act):
                for i in range(KD):
                    act.wait_ge(centred, i + 1)
                    act.activation(sq[:, i, :], c.yT[:, KD + i, :], ACT.Square).then_inc(squared, 1)
                act.wait_ge(var, 1)
                act.activation(rstd[:], rstd[:], ACT.Sqrt).then_inc(root, 1)
                act.wait_ge(consts_in, 32)
                for i in range(KD):
                    act.wait_ge(normed, i + 1)
                    y = c.yT[:, KD + i, :]
                    act.activation(y, y, ACT.Silu, scale=gam[:, i:i + 1], bias=bet[:, i:i + 1]).then_inc(done, 1)


def stage_ssd(nc, c, a):
    CH = M + 1
    with Stage(nc, "ssd") as s:
        alog = s.sb("alog", [P, HEADS])
        dsk = s.sb("dsk", [P, KD])
        nw = s.sb("nw", [P, KD])
        acs = s.sb("acs", [P, CH, HEADS])
        keep = s.sb("keep", [P, CH, HEADS])
        dec = s.sb("dec", [P, CH, HEADS])
        xdt = s.sb("xdt", [P, HEADS, 64])
        xw = s.sb("xw", [P, HEADS, 64])
        btok = s.sb("btok", [P, GROUPS, P])
        state = s.sb("state", [P, HEADS, 64])
        lmat = s.sb("lmat", [P, 2, 4, P])
        cw = s.sb("cw", [P, 2, 4, P])
        cbm = s.sb("cbm", [P, 2, P])
        sq = s.sb("sq", [P, KD, T])
        rstd = s.sb("rstd", [P, GROUPS, T])
        X = s.ps("X", [P, 2, 512])
        A_ = s.ps("A", [P, 512])
        R = s.ps("R", [P, 2, 4, P])
        CB = s.ps("CB", [P, 4, P])
        Y = s.ps("Y", [P, 2, 512])
        consts_in = s.sem("consts_in")
        aneg, dta_ok, cs_done, cs_ok, w_exp, chain, dve_w = (
            s.sem(n) for n in ("aneg", "dta_ok", "cs_done", "cs_ok", "w_exp", "chain", "dve_w"))
        x_turned, b_turned, b_taken, xdt_ok, xw_ok = (
            s.sem(n) for n in ("x_turned", "b_turned", "b_taken", "xdt_ok", "xw_ok"))
        r_done, e_ok, e_exp, q_exp, w_ok = (s.sem(n) for n in ("r_done", "e_ok", "e_exp", "q_exp", "w_ok"))
        y_done, y_taken, st_done, s_ok = (s.sem(n) for n in ("y_done", "y_taken", "st_done", "s_ok"))
        squared, sums, var, root = (s.sem(n) for n in ("squared", "sums", "var", "root"))

        def cols(ch):
            return (0, META) if ch == 0 else (META + (ch - 1) * P, P)

        with s.block() as block:

            @block.sync
            def _(sp):
                sp.dma_start(alog[:], a["ssd_A_log"].to_broadcast([P, HEADS])).then_inc(consts_in, 16)
                sp.dma_start(dsk[:], a["ssd_D"]).then_inc(consts_in, 16)
                sp.dma_start(nw[:], a["ssd_norm_w"]).then_inc(consts_in, 16)

            @block.tensor
            def _(pe):
                pe.wait_ge(dta_ok, 1)
                dta = c.dta[:].rearrange("p c h -> p (c h)")
                pe.matmul(A_[:, 0:CH * HEADS], c.upper[:], dta, start=True, stop=True)
                pe.matmul(A_[:, 128:128 + CH * HEADS], c.ones[:], dta, start=True, stop=True).then_inc(cs_done, 1)

                def turn(ch):
                    at, n = cols(ch)
                    if ch > 0:
                        pe.wait_ge(s_ok, ch)
                    for h in range(2):
                        for k in range(4):
                            t = pe.transpose(X[0:n, h, k * P:(k + 1) * P], c.xbcT[:, 4 * h + k, at:at + n], c.ident[:])
                        t.then_inc(x_turned, 1)
                    if ch == M:
                        return
                    pe.wait_ge(cs_ok, 1) if ch == 0 else pe.wait_ge(b_taken, ch)
                    for g in range(GROUPS):
                        t = pe.transpose(A_[0:n, g * P:(g + 1) * P], c.xbcT[:, XT + g, at:at + n], c.ident[:])
                    t.then_inc(b_turned, 1)

                def new_state(ch):
                    n = cols(ch)[1]
                    pe.wait_ge(xw_ok, ch + 1)
                    pe.wait_ge(b_taken, ch + 1)
                    for g in range(GROUPS):
                        mm = pe.matmul(X[:, g // 2, (g % 2) * 256:(g % 2) * 256 + 256], btok[0:n, g, :],
                                       xw[0:n, 4 * g:4 * g + 4, :].rearrange("p h d -> p (h d)"), start=True, stop=True)
                    mm.then_inc(st_done, 1)

                def decays(n):
                    ch, g = n // 4 + 1, n % 4
                    at, _ = cols(ch)
                    if n >= 2:
                        pe.wait_ge(e_ok, n - 1)
                        pe.wait_ge(q_exp, n - 1)
                        pe.wait_ge(w_ok, n - 1)
                    for r in range(4):
                        pe.matmul(R[:, n % 2, r, :], c.dta[:, ch, 4 * g + r:4 * g + r + 1].to_broadcast([P, P]),
                                  c.upper[:], start=True, stop=True)
                    if n >= 1:
                        pe.wait_ge(dve_w, n)
                    pe.matmul(CB[:, n % 2, :], c.xbcT[:, XT + g, at:at + P], c.xbcT[:, XT + 4 + g, at:at + P],
                              start=True, stop=True).then_inc(r_done, 1)

                turn(0)
                new_state(0)
                turn(1)
                decays(0)
                for n in range(16):
                    ch, g = n // 4 + 1, n % 4
                    if n + 1 < 16:
                        decays(n + 1)
                    pe.wait_ge(w_ok, n + 1)
                    pe.wait_ge(xdt_ok, ch + 1)
                    pe.wait_ge(s_ok, ch)
                    if n >= 2:
                        pe.wait_ge(y_taken, n - 1)
                    for r in range(4):
                        h = 4 * g + r
                        out = Y[64 * (r % 2):64 * (r % 2) + 64, n % 2, (r // 2) * P:(r // 2) * P + P]
                        pe.matmul(out, xdt[:, h, :], lmat[:, n % 2, r, :], start=True, stop=False)
                        mm = pe.matmul(out, state[:, h, :], cw[:, n % 2, r, :], start=False, stop=True)
                    mm.then_inc(y_done, 1)
                    if g == 3 and ch < M:
                        new_state(ch)
                        turn(ch + 1)
                for g in range(GROUPS):
                    pe.wait_ge(squared, g + 1)
                    pe.wait_ge(y_taken, 16)
                    if g >= 2:
                        pe.wait_ge(var, g - 1)
                    for k in range(2):
                        mm = pe.matmul(Y[:, g % 2, :], c.ones[:], sq[:, 2 * g + k, :], start=(k == 0), stop=(k == 1))
                    mm.then_inc(sums, 1)

            @block.scalar
            def _(act):
                act.wait_ge(consts_in, 48)
                act.activation(alog[:], alog[:], ACT.Exp).then_inc(aneg, 1)
                act.wait_ge(cs_ok, 2)
                act.activation(keep[:], keep[:], ACT.Exp).then_inc(w_exp, 1)
                act.activation(dec[:], dec[:], ACT.Exp).then_inc(w_exp, 1)

                def take_b(ch):
                    n = cols(ch)[1]
                    act.wait_ge(b_turned, ch + 1)
                    act.activation(btok[0:n, :, :], A_[0:n, :].rearrange("p (g n) -> p g n", g=GROUPS),
                                   ACT.Copy).then_inc(b_taken, 1)

                take_b(0)
                take_b(1)
                for n in range(16):
                    act.wait_ge(r_done, n + 1)
                    if n >= 2:
                        act.wait_ge(y_done, n - 1)
                    act.activation(cw[:, n % 2, :, :], R[:, n % 2, :, :], ACT.Exp).then_inc(q_exp, 1)
                    act.wait_ge(e_ok, n + 1)
                    act.activation(lmat[:, n % 2, :, :], lmat[:, n % 2, :, :], ACT.Exp).then_inc(e_exp, 1)
                    if n % 4 == 0 and 1 < n // 4 + 1 < M:
                        take_b(n // 4 + 1)
                for g in range(GROUPS):
                    act.wait_ge(y_taken, 16)
                    act.activation(sq[:, 2 * g:2 * g + 2, :], c.yT[:, 2 * g:2 * g + 2, :], ACT.Square).then_inc(squared, 1)
                act.wait_ge(var, GROUPS)
                act.activation(rstd[:], rstd[:], ACT.Sqrt).then_inc(root, 1)

            @block.vector
            def _(dve):
                step = chained(dve, chain)
                dve.wait_ge(aneg, 1)
                dve.scalar_tensor_tensor(out=c.dta[:], in0=c.dt[:], scalar=-1.0,
                                         in1=alog[:].unsqueeze(1).to_broadcast([P, CH, HEADS]),
                                         op0=ALU.mult, op1=ALU.mult).then_inc(dta_ok, 1)
                dve.wait_ge(cs_done, 1)
                n_ = CH * HEADS
                step(dve.tensor_copy(acs[:].rearrange("p c h -> p (c h)"), A_[:, 0:n_]))
                step(dve.tensor_copy(dec[:].rearrange("p c h -> p (c h)"), A_[:, 128:128 + n_]))
                dve.tensor_tensor(keep[:], dec[:], acs[:], ALU.subtract).then_inc(cs_ok, 2)
                dve.wait_ge(w_exp, 2)

                def take_x(ch):
                    n = cols(ch)[1]
                    for h in range(2):
                        dve.wait_ge(x_turned, 2 * ch + h + 1)
                        ins = dve.tensor_tensor(xdt[0:n, 8 * h:8 * h + 8, :],
                                                X[0:n, h, :].rearrange("p (h d) -> p h d", h=8),
                                                c.dt[0:n, ch, 8 * h:8 * h + 8].unsqueeze(2).to_broadcast([n, 8, 64]), ALU.mult)
                        if h == 0:
                            step(ins)
                    ins.then_inc(xdt_ok, 1)
                    dve.wait_ge(xdt_ok, ch + 1)
                    dve.tensor_tensor(xw[0:n, :, :], xdt[0:n, :, :],
                                      keep[0:n, ch, :].unsqueeze(2).to_broadcast([n, HEADS, 64]), ALU.mult).then_inc(xw_ok, 1)

                def take_state(ch):
                    dve.wait_ge(st_done, ch + 1)
                    new = X[:].rearrange("p b (h d) -> p (b h) d", d=64)
                    if ch == 0:
                        dve.tensor_copy(state[:], new).then_inc(s_ok, 1)
                        return
                    step(dve.tensor_tensor(state[:], state[:], dec[:, ch, :].unsqueeze(2).to_broadcast([P, HEADS, 64]),
                                           ALU.mult))
                    dve.tensor_tensor(state[:], state[:], new, ALU.add).then_inc(s_ok, 1)

                def prepare(n):
                    ch, g = n // 4 + 1, n % 4
                    at, _ = cols(ch)
                    dve.wait_ge(r_done, n + 1)
                    if n >= 2:
                        dve.wait_ge(y_done, n - 1)
                    dve.tensor_tensor(cbm[:, n % 2, :], CB[:, n % 2, :], c.upper[:], ALU.mult).then_inc(dve_w, 1)
                    dve.wait_ge(q_exp, n + 1)
                    for r in range(4):
                        h = 4 * g + r
                        ins = dve.tensor_scalar(lmat[:, n % 2, r, :], R[:, n % 2, r, :], acs[:, ch, h:h + 1], 0.0,
                                                ALU.subtract, ALU.min)
                    ins.then_inc(e_ok, 1)
                    dve.tensor_tensor(cw[:, n % 2, :, :], cw[:, n % 2, :, :],
                                      c.xbcT[:, XT + 4 + g, at:at + P].unsqueeze(1).to_broadcast([P, 4, P]), ALU.mult)
                    dve.wait_ge(e_exp, n + 1)
                    dve.wait_ge(dve_w, n + 1)
                    dve.tensor_tensor(lmat[:, n % 2, :, :], lmat[:, n % 2, :, :],
                                      cbm[:, n % 2, :].unsqueeze(1).to_broadcast([P, 4, P]), ALU.mult).then_inc(w_ok, 1)

                take_x(0)
                take_state(0)
                take_x(1)
                prepare(0)
                for n in range(16):
                    ch, g = n // 4 + 1, n % 4
                    at, _ = cols(ch)
                    if n + 1 < 16:
                        prepare(n + 1)
                    dve.wait_ge(y_done, n + 1)
                    for k in range(2):
                        j = 2 * g + k
                        ins = dve.scalar_tensor_tensor(out=c.yT[:, j, at - META:at - META + P],
                                                       in0=c.xbcT[:, j, at:at + P], scalar=dsk[:, j:j + 1],
                                                       in1=Y[:, n % 2, k * P:k * P + P], op0=ALU.mult, op1=ALU.add)
                    step(ins)
                    y = c.yT[:, 2 * g:2 * g + 2, at - META:at - META + P]
                    dve.tensor_tensor(y, y, c.zT[:, 2 * g:2 * g + 2, at - META:at - META + P],
                                      ALU.mult).then_inc(y_taken, 1)
                    if g == 3 and ch < M:
                        take_state(ch)
                        take_x(ch + 1)
                for g in range(GROUPS):
                    dve.wait_ge(sums, g + 1)
                    dve.tensor_scalar(rstd[:, g, :], Y[:, g % 2, :], 1.0 / 256, EPS, ALU.mult, ALU.add).then_inc(var, 1)
                dve.wait_ge(root, 1)
                step(dve.reciprocal(rstd[:], rstd[:]))
                for j in range(KD):
                    dve.scalar_tensor_tensor(out=c.yT[:, j, :], in0=c.yT[:, j, :], scalar=nw[:, j:j + 1],
                                             in1=rstd[:, j // 2, :], op0=ALU.mult, op1=ALU.mult).then_inc(chain, 1)


def stage_out_proj(nc, c, a, name, yT, w_dram, kt, resid, resid_scale, bias=None):
    RING = 4
    with Stage(nc, name) as s:
        w = s.sb("w", [P, RING, 2, D])
        res = s.sb("res", [P, M, D])
        acc = s.ps("acc", [P, M, 2, 512])
        bb = s.sb("bb", [P, D]) if bias is not None else None
        loaded = [s.sem(f"loaded{b}") for b in range(RING)]
        res_in, bias_in, used, done, chain = (s.sem(n) for n in ("res_in", "bias_in", "used", "done", "chain"))
        pairs = kt // 2
        with s.block() as block:

            @block.sync
            def _(sp):
                if resid is not None:
                    sp.dma_start(res[:], tokens(resid)).then_inc(res_in, 16)
                if bias is not None:
                    sp.dma_start(bb[:], bias.to_broadcast([P, D])).then_inc(bias_in, 16)
                for q in range(pairs):
                    if q >= RING:
                        sp.wait_ge(used, q - RING + 1)
                    sp.dma_start(w[:, q % RING, :, :], rows(w_dram)[:, 2 * q:2 * q + 2, :]).then_inc(loaded[q % RING], 16)

            @block.tensor
            def _(pe):
                for q in range(pairs):
                    pe.wait_ge(loaded[q % RING], 16 * (q // RING + 1))
                    for m in range(M):
                        for n in range(2):
                            for j in range(2):
                                k = 2 * q + j
                                mm = pe.matmul(acc[:, m, n, :], yT[:, k, m * P:m * P + P],
                                               w[:, q % RING, j, n * 512:n * 512 + 512],
                                               start=(k == 0), stop=(k == kt - 1))
                            if q == pairs - 1:
                                mm.then_inc(done, 1)
                    if q < pairs - 1:
                        mm.then_inc(used, 1)

            @block.vector
            def _(dve):
                step = chained(dve, chain)
                if resid is not None:
                    dve.wait_ge(res_in, 16)
                if bias is not None:
                    dve.wait_ge(bias_in, 16)
                for m in range(M):
                    for n in range(2):
                        dve.wait_ge(done, 2 * m + n + 1)
                        out = c.h[:, m, n * 512:n * 512 + 512]
                        old = (res if resid is not None else c.h)[:, m, n * 512:n * 512 + 512]
                        ins = dve.scalar_tensor_tensor(out=out, in0=old, scalar=resid_scale, in1=acc[:, m, n, :],
                                                       op0=ALU.mult, op1=ALU.add)
                        step(ins)
                        if bias is not None:
                            step(dve.tensor_tensor(out, out, bb[:, n * 512:n * 512 + 512], ALU.add))


def stage_token_norm(nc, c, a, name, dst, dstT=None, centre=False, norm=True, row_w=None, row_b=None, col_w=None,
                     save=None):
    src = c.h
    with Stage(nc, name) as s:
        junk = s.sb("junk", [P, 2, D])
        rw = s.sb("rw", [P, D]) if row_w is not None else None
        rb = s.sb("rb", [P, D]) if row_b is not None else None
        cwt = s.sb("cwt", [P, KD]) if col_w is not None else None
        stat = s.sb("stat", [P, 2, M])
        tp = s.ps("tp", [P, 4, 4, P])
        (w_in, summed, meaned, centred, squared, var, root, inv, scaled, turned, copied, saved, chain) = (
            s.sem(n) for n in ("w_in", "summed", "meaned", "centred", "squared", "var", "root", "inv", "scaled",
                               "turned", "copied", "saved", "chain"))
        n_w = 16 * sum(v is not None for v in (row_w, row_b, col_w))
        with s.block() as block:

            @block.sync
            def _(sp):
                if row_w is not None:
                    sp.dma_start(rw[:], row_w.to_broadcast([P, D])).then_inc(w_in, 16)
                if row_b is not None:
                    sp.dma_start(rb[:], row_b.to_broadcast([P, D])).then_inc(w_in, 16)
                if col_w is not None:
                    sp.dma_start(cwt[:], col_w).then_inc(w_in, 16)
                if save is not None:
                    for m in range(M):
                        sp.wait_ge(scaled, m + 1)
                        sp.dma_start(tokens(save)[:, m, :], dst[:, m, :]).then_inc(saved, 16)
                    sp.wait_ge(saved, 16 * M)

            @block.scalar
            def _(act):
                if not norm:
                    return
                if centre:
                    for m in range(M):
                        act.activation(junk[:, m % 2, :], src[:, m, :], ACT.Copy, accum_out=stat[:, 0, m:m + 1]).then_inc(summed, 1)
                        act.wait_ge(summed, m + 1)
                for m in range(M):
                    if centre:
                        act.wait_ge(centred, m + 1)
                    act.activation(junk[:, m % 2, :], dst[:, m, :] if centre else src[:, m, :], ACT.Square,
                                   accum_out=stat[:, 1, m:m + 1]).then_inc(squared, 1)
                    act.wait_ge(squared, m + 1)
                act.wait_ge(var, 1)
                act.activation(stat[:, 1, :], stat[:, 1, :], ACT.Sqrt).then_inc(root, 1)

            @block.vector
            def _(dve):
                step = chained(dve, chain)
                if norm:
                    if centre:
                        dve.wait_ge(summed, M)
                        step(dve.tensor_scalar(stat[:, 0, :], stat[:, 0, :], 1.0 / D, None, ALU.mult))
                        for m in range(M):
                            dve.tensor_scalar(dst[:, m, :], src[:, m, :], stat[:, 0, m:m + 1], None,
                                              ALU.subtract).then_inc(centred, 1)
                    dve.wait_ge(squared, M)
                    dve.tensor_scalar(stat[:, 1, :], stat[:, 1, :], 1.0 / D, EPS, ALU.mult, ALU.add).then_inc(var, 1)
                    dve.wait_ge(root, 1)
                    step(dve.reciprocal(stat[:, 1, :], stat[:, 1, :]))
                if n_w:
                    dve.wait_ge(w_in, n_w)
                for m in range(M if norm else 0):
                    x = (dst if centre else src)[:, m, :]
                    if rw is None:
                        dve.tensor_scalar(dst[:, m, :], x, stat[:, 1, m:m + 1], None, ALU.mult).then_inc(scaled, 1)
                    else:
                        ins = dve.scalar_tensor_tensor(out=dst[:, m, :], in0=x, scalar=stat[:, 1, m:m + 1], in1=rw[:],
                                                       op0=ALU.mult, op1=ALU.mult)
                        if rb is not None:
                            step(ins)
                            ins = dve.tensor_tensor(dst[:, m, :], dst[:, m, :], rb[:], ALU.add)
                        ins.then_inc(scaled, 1)
                if dstT is None:
                    return
                for i in range(2 * M):
                    m, h = i // 2, i % 2
                    dve.wait_ge(turned, i + 1)
                    out = dstT[:, 4 * h:4 * h + 4, m * P:m * P + P]
                    if cwt is not None:
                        ins = dve.tensor_tensor(out, tp[:, i % 4, :, :],
                                                cwt[:, 4 * h:4 * h + 4].unsqueeze(2).to_broadcast([P, 4, P]), ALU.mult)
                    else:
                        ins = dve.tensor_copy(out, tp[:, i % 4, :, :])
                    ins.then_inc(copied, 1)

            @block.tensor
            def _(pe):
                if dstT is None:
                    return
                for i in range(2 * M):
                    m, h = i // 2, i % 2
                    if h == 0 and norm:
                        pe.wait_ge(scaled, m + 1)
                    if i >= 4:
                        pe.wait_ge(copied, i - 3)
                    for k in range(4):
                        t = pe.transpose(tp[:, i % 4, k, :], dst[:, m, (4 * h + k) * P:(4 * h + k + 1) * P], c.ident[:])
                    t.then_inc(turned, 1)


def stage_peer_scores(nc, c, a):
    NQ = 2 * PH
    with Stage(nc, "score") as s:
        w = s.sb("w", [P, 2, KD, 512])
        qT = s.sb("qT", [P, NQ, T])
        keysT = s.sb("keysT", [P, NQ, NK])
        S = s.sb("S", [P, 2, NQ, NK])
        v = s.sb("v", [P, NQ, TOPK])
        iu = s.sb("iu", [P, NQ, TOPK], U32)
        fi = s.sb("fi", [P, NQ, TOPK])
        cand = s.sb("cand", [P, PH, TOPK * TOPK])
        best = s.sb("best", [P, PH, TOPK])
        pos = s.sb("pos", [P, PH, TOPK], U32)
        hi = s.sb("hi", [P, PH, TOPK], U32)
        posf = s.sb("posf", [P, 2, PH, TOPK])
        gate = s.sb("gate", [P, PH, TOPK])
        total = s.sb("total", [P, PH])
        eq = s.sb("eq", [P, PH, TOPK, TOPK])
        pick = s.sb("pick", [P, 3, PH * TOPK])
        q_ps = s.ps("q_ps", [P, 2, 512])
        s_ps = s.ps("s_ps", [P, 4, 4, NK])
        t_ps = s.ps("t_ps", [P, 4, P])
        w_in = [s.sem(f"w_in{b}") for b in range(2)]
        (keys_in, q_done, q_taken, s_done, s_taken, s_used, chain, centred, exped, picks, turned, copied) = (
            s.sem(n) for n in ("keys_in", "q_done", "q_taken", "s_done", "s_taken", "s_used", "chain", "centred",
                               "exped", "picks", "turned", "copied"))
        wq = rows(a["peer_w_query"][0])
        LOW = -3.0e38
        with s.block() as block:

            @block.sync
            def _(sp):
                sp.dma_start(keysT[:], a["peer_keysT"]).then_inc(keys_in, 16)
                for n in range(4):
                    if n >= 2:
                        sp.wait_ge(q_done, 4 * (n - 1))
                    sp.dma_start(w[:, n % 2, :, :], wq[:, :, n * 512:n * 512 + 512]).then_inc(w_in[n % 2], 16)

            @block.tensor
            def _(pe):
                for n in range(NQ):
                    if n % 4 == 0:
                        pe.wait_ge(w_in[n // 4 % 2], 16 * (n // 8 + 1))
                    if n >= 2:
                        pe.wait_ge(q_taken, n - 1)
                    for k in range(KD):
                        mm = pe.matmul(q_ps[:, n % 2, :], w[:, n // 4 % 2, k, (n % 4) * P:(n % 4) * P + P], c.hT[:, k, :],
                                       start=(k == 0), stop=(k == KD - 1))
                    mm.then_inc(q_done, 1)
                pe.wait_ge(q_taken, NQ)
                pe.wait_ge(keys_in, 16)

                def scores(m):
                    for b in range(4):
                        if m >= 1:
                            pe.wait_ge(s_taken, 4 * (m - 1) + b + 1)
                        for j in range(4):
                            n = 4 * b + j
                            mm = pe.matmul(s_ps[:, b, j, :], qT[:, n, m * P:m * P + P], keysT[:, n, :],
                                           start=True, stop=True)
                        mm.then_inc(s_done, 1)

                scores(0)
                scores(1)
                for m in range(M):
                    pe.wait_ge(picks, m + 1)
                    if m >= 1:
                        pe.wait_ge(copied, m)
                    for j in range(3):
                        t = pe.transpose(t_ps[:, j, :], pick[:, j, :], c.ident[:])
                    t.then_inc(turned, 1)
                    if m + 2 < M:
                        scores(m + 2)

            @block.scalar
            def _(act):
                for n in range(NQ):
                    act.wait_ge(q_done, n + 1)
                    act.activation(qT[:, n, :], q_ps[:, n % 2, :], ACT.Copy).then_inc(q_taken, 1)

                def take(m):
                    if m >= 2:
                        act.wait_ge(s_used, m - 1)
                    for b in range(4):
                        act.wait_ge(s_done, 4 * m + b + 1)
                        act.activation(S[:, m % 2, 4 * b:4 * b + 4, :], s_ps[:, b, :, :], ACT.Copy).then_inc(s_taken, 1)

                take(0)
                for m in range(M):
                    if m + 1 < M:
                        take(m + 1)
                    act.wait_ge(centred, m + 1)
                    act.activation(gate[:], gate[:], ACT.Exp).then_inc(exped, 1)
                    act.wait_ge(turned, m + 1)
                    act.activation(c.idxT[:, :, m * P:m * P + P], t_ps[:, 0:3, :], ACT.Copy).then_inc(copied, 1)

            @block.vector
            def _(dve):
                step = chained(dve, chain)

                def top16(values, vals, idx, n):
                    for half in range(2):
                        o = slice(8 * half, 8 * half + 8)
                        for r in range(n):
                            ins = dve.max(vals[:, r, o], values[:, r, :])
                        step(ins)
                        for r in range(n):
                            ins = dve.max_index(idx[:, r, o], vals[:, r, o], values[:, r, :])
                        step(ins)
                        if half == 0:
                            for r in range(n):
                                ins = dve.match_replace(out=values[:, r, :], in_to_replace=vals[:, r, o],
                                                        in_values=values[:, r, :], imm_value=LOW)
                            step(ins)

                for m in range(M):
                    dve.wait_ge(s_taken, 4 * m + 4)
                    top16(S[:, m % 2, :, :], v, iu, NQ)
                    dve.tensor_copy(fi[:], iu[:]).then_inc(s_used, 1)
                    dve.wait_ge(s_used, m + 1)
                    halves = v[:].rearrange("p (h two) k -> p h two k", two=2)
                    step(dve.tensor_tensor(cand[:].rearrange("p h (i j) -> p h i j", i=TOPK),
                                           halves[:, :, 0, :].unsqueeze(3).to_broadcast([P, PH, TOPK, TOPK]),
                                           halves[:, :, 1, :].unsqueeze(2).to_broadcast([P, PH, TOPK, TOPK]), ALU.add))
                    top16(cand, best, pos, PH)
                    dve.tensor_tensor(gate[:], best[:], best[:, :, 0:1].to_broadcast([P, PH, TOPK]),
                                      ALU.subtract).then_inc(centred, 1)
                    step(dve.tensor_scalar(hi[:], pos[:], 4, None, ALU.logical_shift_right))
                    step(dve.tensor_copy(posf[:, 0, :, :], hi[:]))
                    step(dve.tensor_scalar(hi[:], pos[:], 15, None, ALU.bitwise_and))
                    step(dve.tensor_copy(posf[:, 1, :, :], hi[:]))
                    fih = fi[:].rearrange("p (h two) k -> p h two k", two=2)
                    if m >= 1:
                        dve.wait_ge(turned, m)
                    for half in range(2):
                        step(dve.tensor_tensor(eq[:].rearrange("p h k i -> p (h k) i"),
                                               posf[:, half, :, :].rearrange("p h k -> p (h k)").unsqueeze(2).to_broadcast([P, PH * TOPK, TOPK]),
                                               c.count[:, 0:TOPK].unsqueeze(1).to_broadcast([P, PH * TOPK, TOPK]),
                                               ALU.is_equal))
                        step(dve.tensor_tensor(eq[:], eq[:],
                                               fih[:, :, half, :].unsqueeze(2).to_broadcast([P, PH, TOPK, TOPK]), ALU.mult))
                        step(dve.tensor_reduce(pick[:, half, :], eq[:].rearrange("p h k i -> p (h k) i"), AX.X, ALU.add))
                    dve.wait_ge(exped, m + 1)
                    step(dve.tensor_reduce(total[:], gate[:], AX.X, ALU.add))
                    step(dve.reciprocal(total[:], total[:]))
                    dve.tensor_tensor(pick[:, 2, :].rearrange("p (h k) -> p h k", h=PH), gate[:],
                                      total[:].unsqueeze(2).to_broadcast([P, PH, TOPK]), ALU.mult).then_inc(picks, 1)
                    dve.wait_ge(picks, m + 1)


TB = 64
BATCHES = T // TB


def stage_gate_matrix(nc, c, a):
    U = 4
    with Stage(nc, "gates") as s:
        one = s.sb("one", [P, 2, U, NK])
        two = s.sb("two", [P, 2, U, NK])
        out = s.sb("out", [P, 2, NK, TB])
        ps = s.ps("ps", [P, 2, U, NK])
        (hot, used, g_done, taken) = (s.sem(n) for n in ("hot", "used", "g_done", "taken"))
        saved = [s.sem(f"saved{b}") for b in range(2)]
        per = TB // (2 * U)
        with s.block() as block:

            @block.vector
            def _(dve):
                with dve.Fori(0, T // (2 * U)) as it:
                    for u in range(2):
                        dve.wait_ge(g_done, it * 2 + (u + 1))
                        for j in range(U):
                            t = it * (2 * U) + (u * U + j)
                            dve.tensor_scalar(one[:, u, j, :], c.count[:], c.idxT[:, 0, ds(t, 1)], c.idxT[:, 2, ds(t, 1)],
                                              ALU.is_equal, ALU.mult)
                            ins = dve.tensor_scalar(two[:, u, j, :], c.count[:], c.idxT[:, 1, ds(t, 1)], None, ALU.is_equal)
                        ins.then_inc(hot, 1)

            @block.tensor
            def _(pe):
                pe.sem_inc(g_done, 2)
                with pe.Fori(0, T // (2 * U)) as it:
                    for u in range(2):
                        pe.wait_ge(hot, it * 2 + (u + 1))
                        pe.wait_ge(taken, it * 2 + (u + 1))
                        for j in range(U):
                            mm = pe.matmul(ps[:, u, j, :], two[:, u, j, :], one[:, u, j, :], start=True, stop=True)
                        mm.then_inc(g_done, 1)

            @block.scalar
            def _(act):
                act.sem_inc(taken, 2)
                for b in range(BATCHES):
                    if b >= 2:
                        act.wait_ge(saved[b % 2], 16 * (b // 2))
                    with act.Fori(0, per) as q:
                        for u in range(2):
                            act.wait_ge(g_done, q * 2 + (2 * per * b + u + 3))
                            act.activation(out[:, b % 2, :, ds(q * (2 * U) + u * U, U)],
                                           ps[:, u, :, :].rearrange("p t i -> p i t"), ACT.Copy).then_inc(taken, 1)

            @block.sync
            def _(sp):
                for b in range(BATCHES):
                    sp.wait_ge(taken, 2 * per * (b + 1) + 2)
                    sp.dma_start(c.gates[b], out[:, b % 2, :, :].rearrange("p i t -> p (i t)")).then_inc(saved[b % 2], 16)
                for b in range(2):
                    sp.wait_ge(saved[b], 16 * (BATCHES // 2))


def stage_peer_experts(nc, c, a):
    G = 4
    GROUPS_ = NK // G
    wd_d = rows(a["peer_w_downT"])
    wu_d = a["peer_w_up"][0].rearrange("(k p) n -> p k n", p=P)
    g_d = c.gates.rearrange("b p (i t) -> p b i t", t=TB)
    with Stage(nc, "experts") as s:
        wd = s.sb("wd", [P, 2, KD, G * P])
        wu = s.sb("wu", [P, 2, G, D])
        gt = s.sb("gt", [P, 2, BATCHES, G * TB])
        hid = s.sb("hid", [P, G, T])
        H = s.ps("H", [P, G, T])
        Y = s.ps("Y", [P, 4, 512])
        wd_in = [s.sem(f"wd_in{b}") for b in range(2)]
        wu_in = [s.sem(f"wu_in{b}") for b in range(2)]
        gt_in = [s.sem(f"gt_in{b}") for b in range(2)]
        (h_done, gelued, gated, y_done, added) = (s.sem(n) for n in ("h_done", "gelued", "gated", "y_done", "added"))
        with s.block() as block:

            @block.sync
            def _(sp):
                def load(u, e0, g0):
                    sp.dma_start(wd[:, u, :, :], wd_d[:, :, ds(e0, G * P)]).then_inc(wd_in[u], 16)

                def load_rest(u, k0, t0):
                    sp.dma_start(wu[:, u, :, :], wu_d[:, ds(k0, G), :]).then_inc(wu_in[u], 16)
                    sp.dma_start(gt[:, u, :, :].rearrange("p b (i t) -> p b i t", t=TB),
                                 g_d[:, :, ds(k0, G), :]).then_inc(gt_in[u], 16)

                for u in range(2):
                    load(u, u * G * P, 0)
                    load_rest(u, u * G, 0)
                with sp.Fori(0, GROUPS_ // 2 - 1) as it:
                    for u in range(2):
                        e0 = sp.snap(it * (2 * G * P) + (2 + u) * G * P)
                        k0 = sp.snap(it * (2 * G) + (2 + u) * G)
                        sp.wait_ge(h_done, it * (2 * G) + G * (u + 1))
                        load(u, e0, 0)
                        sp.wait_ge(y_done, it * 16 + 8 * (u + 1))
                        load_rest(u, k0, 0)

            @block.tensor
            def _(pe):
                with pe.Fori(0, GROUPS_ // 2) as it:
                    for u in range(2):
                        pe.wait_ge(wd_in[u], it * 16 + 16)
                        pe.wait_ge(gelued, it * (2 * G) + (G * u + 1))
                        for j in range(G):
                            for k in range(KD):
                                mm = pe.matmul(H[:, j, :], wd[:, u, k, j * P:j * P + P], c.hT[:, k, :],
                                               start=(k == 0), stop=(k == KD - 1))
                            mm.then_inc(h_done, 1)
                        pe.wait_ge(wu_in[u], it * 16 + 16)
                        pe.wait_ge(added, it * 16 + (8 * u + 1))
                        for y in range(8):
                            m, n = y // 2, y % 2
                            if y >= 4:
                                pe.wait_ge(added, it * 16 + (8 * u + y - 2))
                            for j in range(G):
                                if y == 0:
                                    pe.wait_ge(gated, it * (2 * G) + (G * u + j + 1))
                                mm = pe.matmul(Y[:, y % 4, :], hid[:, j, m * P:m * P + P], wu[:, u, j, n * 512:n * 512 + 512],
                                               start=(j == 0), stop=(j == G - 1))
                            mm.then_inc(y_done, 1)

            @block.scalar
            def _(act):
                act.sem_inc(gelued, 1)
                with act.Fori(0, GROUPS_ // 2) as it:
                    for u in range(2):
                        for j in range(G):
                            act.wait_ge(h_done, it * (2 * G) + (G * u + j + 1))
                            act.activation(hid[:, j, :], H[:, j, :], ACT.Gelu).then_inc(gelued, 1)

            @block.vector
            def _(dve):
                dve.sem_inc(added, 1)
                with dve.Fori(0, GROUPS_ // 2) as it:
                    for u in range(2):
                        dve.wait_ge(gt_in[u], it * 16 + 16)
                        for j in range(G):
                            dve.wait_ge(gelued, it * (2 * G) + (G * u + j + 2))
                            dve.tensor_tensor(hid[:, j, :].rearrange("p (b t) -> p b t", b=BATCHES),
                                              hid[:, j, :].rearrange("p (b t) -> p b t", b=BATCHES),
                                              gt[:, u, :, j * TB:(j + 1) * TB], ALU.mult).then_inc(gated, 1)
                        for y in range(8):
                            m, n = y // 2, y % 2
                            dve.wait_ge(y_done, it * 16 + (8 * u + y + 1))
                            out = c.h[:, m, n * 512:n * 512 + 512]
                            if y == 0:
                                dve.wait_ge(added, it * 16 + (8 * u + 1))
                            dve.tensor_tensor(out, out, Y[:, y % 4, :], ALU.add).then_inc(added, 1)


AH = 8
AJ = 4
GG = 8
ALPHA = 2.0 ** 0.25
NEG = -1e30
COL_K, COL_V, COL_U, COL_S = 512, 640, 768, 1280
EXPERTS = 32
EK = 4
BLOCKS = (T * EK) // P + EXPERTS - 1
NBLK = BLOCKS + 1
LIMIT, SWIGLU = 7.0, 1.702
ROWS = T * EK


def stage_project2(nc, c, a):
    w_d = rows(a["w_in_2"])
    with Stage(nc, "proj2") as s:
        w = s.sb("w", [P, KD, 1792])
        cb = s.sb("cb", [P, 14])
        rb = s.sb("rb", [P, P + 512])
        lg = s.sb("lg", [P, 512])
        lb = s.sb("lb", [P, 512])
        sq = s.sb("sq", [P, M, GG, 64])
        stat = s.sb("stat", [P, 2, M, GG])
        ps = s.ps("ps", [P, 8, 512])
        parts = ((COL_V, COL_U), (COL_S, 1792), (0, COL_V), (COL_U, COL_S))
        w_in = [s.sem(f"w_in{i}") for i in range(len(parts))]
        (cb_in, rb_in, done, taken, added, gelued, chain, root, var) = (
            s.sem(n) for n in ("cb_in", "rb_in", "done", "taken", "added", "gelued", "chain", "root", "var"))
        chans = [(c.qT[:, j, :], j) for j in range(AJ)] + [(c.kT[:], 4)] + [(c.uT2[:, j, :], 6 + j) for j in range(4)]
        with s.block() as block:

            @block.sync
            def _(sp):
                sp.dma_start(rb[:], a["b_in_2_row"].to_broadcast([P, P + 512])).then_inc(rb_in, 16)
                for i, (lo, hi) in enumerate(parts):
                    sp.dma_start(w[:, :, lo:hi], w_d[:, :, lo:hi]).then_inc(w_in[i], 16)
                sp.dma_start(lg[:], a["ln_v_g_2"].to_broadcast([P, 512])).then_inc(rb_in, 16)
                sp.dma_start(lb[:], a["ln_v_b_2"].to_broadcast([P, 512])).then_inc(rb_in, 16)
                sp.dma_start(cb[:], a["b_in_2_col"]).then_inc(cb_in, 16)

            @block.tensor
            def _(pe):
                pe.wait_ge(w_in[0], 16)
                for m in range(M):
                    for k in range(KD):
                        mm = pe.matmul(ps[:, 4, m * P:m * P + P], c.hT[:, k, m * P:m * P + P], w[:, k, COL_V:COL_U],
                                       start=(k == 0), stop=(k == KD - 1))
                mm.then_inc(done, 1)
                pe.wait_ge(w_in[1], 16)
                for m in range(M):
                    for k in range(KD):
                        mm = pe.matmul(ps[:, m, :], c.hT[:, k, m * P:m * P + P], w[:, k, COL_S:1792],
                                       start=(k == 0), stop=(k == KD - 1))
                    mm.then_inc(done, 1)
                pe.wait_ge(w_in[2], 16)
                for i, (_, t) in enumerate(chans):
                    if i == 5:
                        pe.wait_ge(w_in[3], 16)
                    if i >= 3:
                        pe.wait_ge(taken, i - 2)
                    for k in range(KD):
                        mm = pe.matmul(ps[:, 5 + i % 3, :], w[:, k, t * P:t * P + P], c.hT[:, k, :],
                                       start=(k == 0), stop=(k == KD - 1))
                    mm.then_inc(done, 1)

            @block.scalar
            def _(act):
                for m in range(M):
                    act.wait_ge(added, m + 2)
                    act.activation(c.gtok[:, m, :], c.gtok[:, m, :], ACT.Gelu_apprx_tanh).then_inc(gelued, 1)
                act.wait_ge(cb_in, 16)
                for i, (out, t) in enumerate(chans):
                    act.wait_ge(done, 5 + i + 1)
                    act.activation(out, ps[:, 5 + i % 3, :], ACT.Identity if i < 5 else ACT.Gelu_apprx_tanh,
                                   bias=cb[:, t:t + 1]).then_inc(taken, 1)
                act.wait_ge(var, 1)
                act.activation(stat[:, 1, :, :], stat[:, 1, :, :], ACT.Sqrt).then_inc(root, 1)

            @block.vector
            def _(dve):
                step = chained(dve, chain)
                dve.wait_ge(rb_in, 48)
                dve.wait_ge(done, 1)
                dve.tensor_tensor(c.vtok[:], ps[:, 4, :].rearrange("p (m d) -> p m d", m=M),
                                  rb[:, 0:P].unsqueeze(1).to_broadcast([P, M, P]), ALU.add).then_inc(added, 1)
                for m in range(M):
                    dve.wait_ge(done, m + 2)
                    dve.tensor_tensor(c.gtok[:, m, :], ps[:, m, :], rb[:, P:P + 512], ALU.add).then_inc(added, 1)
                dve.wait_ge(gelued, M)
                g = c.gtok[:].rearrange("p m (g d) -> p m g d", g=GG)
                g3 = c.gtok[:].rearrange("p m (g d) -> p (m g) d", g=GG)
                sq3 = sq[:].rearrange("p m g d -> p (m g) d")
                mean, var_ = (stat[:, i, :, :].rearrange("p m g -> p (m g)") for i in range(2))
                step(dve.tensor_reduce(mean, g3, AX.X, ALU.add))
                step(dve.tensor_scalar(mean, mean, 1.0 / 64, None, ALU.mult))
                step(dve.tensor_tensor(g3, g3, mean.unsqueeze(2).to_broadcast([P, M * GG, 64]), ALU.subtract))
                step(dve.tensor_tensor(sq3, g3, g3, ALU.mult))
                step(dve.tensor_reduce(var_, sq3, AX.X, ALU.add))
                dve.tensor_scalar(var_, var_, 1.0 / 64, EPS, ALU.mult, ALU.add).then_inc(var, 1)
                dve.wait_ge(root, 1)
                step(dve.reciprocal(var_, var_))
                step(dve.tensor_tensor(g3, g3, var_.unsqueeze(2).to_broadcast([P, M * GG, 64]), ALU.mult))
                step(dve.tensor_tensor(c.gtok[:], c.gtok[:], lg[:].unsqueeze(1).to_broadcast([P, M, 512]), ALU.mult))
                step(dve.tensor_tensor(c.gtok[:], c.gtok[:], lb[:].unsqueeze(1).to_broadcast([P, M, 512]), ALU.add))


def stage_attention(nc, c, a):
    W2 = 2 * P
    with Stage(nc, "attn") as s:
        mask = s.sb("mask", [P, W2])
        sink = s.sb("sink", [P, 2, AJ])
        sc = s.sb("sc", [P, 2, 2, W2])
        top = s.sb("top", [P, 2, 2, 4])
        pT = s.sb("pT", [P, 2, 4, P])
        wsT = s.sb("wsT", [P, GG, P])
        bsb = s.sb("bsb", [P, 4, P])
        S = s.ps("S", [P, 2, 2, 512])
        X = s.ps("X", [P, 2, 4, P])
        O = s.ps("O", [P, 2, 512])
        (masked, sink_in, ws_in, bs_in, s_done, maxed, exped, probs, chain, turned, pt_ok, o_done, o_taken, s_read,
         g_done, g_taken, ws_ok) = (s.sem(n) for n in (
             "masked", "sink_in", "ws_in", "bs_in", "s_done", "maxed", "exped", "probs", "chain", "turned", "pt_ok",
             "o_done", "o_taken", "s_read", "g_done", "g_taken", "ws_ok"))
        PAIRS = M * AJ

        def span(n):
            return (P, P) if n == 0 else (0, W2)

        with s.block() as block:

            @block.sync
            def _(sp):
                sp.dma_start(sink[:], a["sinks_2"].to_broadcast([P, AH]).rearrange("p (t j) -> p t j", t=2)).then_inc(sink_in, 16)
                sp.dma_start(wsT[:], a["w_spatial_2T"]).then_inc(ws_in, 16)
                bs = a["b_spatial_2"][0].rearrange("(k two) t -> two k t", two=2)
                for two in range(2):
                    sp.dma_start(bsb[64 * two:64 * two + 64, :, :],
                                 bs[two:two + 1].to_broadcast([64, 4, P])).then_inc(bs_in, 16)

            @block.gpsimd
            def _(pool):
                pool.memset(mask[:], 0.0).then_inc(masked, 1)
                pool.wait_ge(masked, 1)
                pool.affine_select(out=mask[:, 0:P], in_=mask[:, 0:P], compare_op=ALU.is_gt, fill=NEG, base=0,
                                   pattern=[[1, P]], channel_multiplier=-1).then_inc(masked, 1)
                pool.affine_select(out=mask[:, P:W2], in_=mask[:, P:W2], compare_op=ALU.is_ge, fill=NEG, base=0,
                                   pattern=[[-1, P]], channel_multiplier=1).then_inc(masked, 1)
                pool.wait_ge(ws_in, 16)
                pool.affine_select(out=wsT[:], in_=wsT[:], compare_op=ALU.is_ge, fill=0.0, base=0,
                                   pattern=[[0, GG], [1, P]], channel_multiplier=-1).then_inc(ws_ok, 1)

            @block.tensor
            def _(pe):
                def scores(i):
                    n, j = i // AJ, i % AJ
                    lo, width = span(n)
                    if i >= 2:
                        pe.wait_ge(s_read, i - 1)
                    for t in range(2):
                        h = slice(64 * t, 64 * t + 64)
                        mm = pe.matmul(S[:, i % 2, t, lo:lo + width], c.qT[h, j, n * P:n * P + P],
                                       c.kT[h, (n - 1) * P + lo:(n - 1) * P + lo + width], start=True, stop=True)
                    mm.then_inc(s_done, 1)

                def turn(i):
                    n = i // AJ
                    pe.wait_ge(probs, i + 1)
                    if i >= 2:
                        pe.wait_ge(pt_ok, i - 1)
                    for t in range(2):
                        for b in range(2):
                            if n > 0 or b == 1:
                                x = pe.transpose(X[:, i % 2, 2 * t + b, :], sc[:, i % 2, t, b * P:b * P + P], c.ident[:])
                    x.then_inc(turned, 1)

                def values(i):
                    n, j = i // AJ, i % AJ
                    pe.wait_ge(pt_ok, i + 1)
                    if i >= 2:
                        pe.wait_ge(o_taken, i - 1)
                    for t in range(2):
                        for b in range(2):
                            if n > 0 or b == 1:
                                mm = pe.matmul(O[64 * t:64 * t + 64, i % 2, 0:P], c.vtok[:, n - 1 + b, 64 * t:64 * t + 64],
                                               pT[:, i % 2, 2 * t + b, :], start=(b == 0 or n == 0), stop=(b == 1))
                    mm.then_inc(o_done, 1)

                scores(0)
                for i in range(PAIRS):
                    if i + 1 < PAIRS:
                        scores(i + 1)
                    turn(i)
                    if i >= 1:
                        values(i - 1)
                values(PAIRS - 1)
                pe.wait_ge(ws_ok, 1)
                for n in range(M):
                    if n >= 2:
                        pe.wait_ge(g_taken, n - 1)
                    else:
                        pe.wait_ge(pt_ok, PAIRS)
                    for g in range(GG):
                        mm = pe.matmul(X[64 * (g % 2):64 * (g % 2) + 64, n % 2, g // 2, :],
                                       c.gtok[:, n, 64 * g:64 * g + 64], wsT[:, g, :], start=True, stop=True)
                    mm.then_inc(g_done, 1)

            @block.scalar
            def _(act):
                def exps(i):
                    lo, width = span(i // AJ)
                    b = i % 2
                    act.wait_ge(maxed, i + 1)
                    for t in range(2):
                        act.activation(sc[:, b, t, lo:lo + width], sc[:, b, t, lo:lo + width], ACT.Exp,
                                       bias=top[:, b, t, 0:1], accum_out=top[:, b, t, 2:3])
                        ins = act.activation(top[:, b, t, 1:2], sink[:, t, i % AJ:i % AJ + 1], ACT.Exp, bias=top[:, b, t, 0:1])
                    ins.then_inc(exped, 1)

                def copies(i):
                    act.wait_ge(turned, i + 1)
                    if i >= 2:
                        act.wait_ge(o_done, i - 1)
                    if i < AJ:
                        act.activation(pT[:, i % 2, 1:4:2, :], X[:, i % 2, 1:4:2, :], ACT.Copy).then_inc(pt_ok, 1)
                    else:
                        act.activation(pT[:, i % 2, :, :], X[:, i % 2, :, :], ACT.Copy).then_inc(pt_ok, 1)

                def outs(i):
                    n, j = i // AJ, i % AJ
                    act.wait_ge(o_done, i + 1)
                    act.activation(c.mixT[:, j, n * P:n * P + P], O[:, i % 2, 0:P], ACT.Copy).then_inc(o_taken, 1)

                act.wait_ge(sink_in, 16)
                exps(0)
                for i in range(PAIRS):
                    copies(i)
                    if i + 1 < PAIRS:
                        exps(i + 1)
                    if i >= 1:
                        outs(i - 1)
                outs(PAIRS - 1)

            @block.vector
            def _(dve):
                step = chained(dve, chain)

                def maxes(i):
                    n, j, b = i // AJ, i % AJ, i % 2
                    lo, width = span(n)
                    dve.wait_ge(s_done, i + 1)
                    if i >= 2:
                        dve.wait_ge(turned, i - 1)
                    x = sc[:, b, :, lo:lo + width]
                    dve.scalar_tensor_tensor(out=x, in0=S[:, b, :, lo:lo + width], scalar=64 ** -0.5,
                                             in1=mask[:, lo:lo + width].unsqueeze(1).to_broadcast([P, 2, width]),
                                             op0=ALU.mult, op1=ALU.add).then_inc(s_read, 1)
                    dve.wait_ge(s_read, i + 1)
                    step(dve.tensor_reduce(top[:, b, :, 3], x, AX.X, ALU.max))
                    step(dve.tensor_tensor(top[:, b, :, 3], top[:, b, :, 3], sink[:, :, j], ALU.max))
                    dve.tensor_scalar(top[:, b, :, 0], top[:, b, :, 3], -1.0, None, ALU.mult).then_inc(maxed, 1)

                def norms(i):
                    b = i % 2
                    lo, width = span(i // AJ)
                    dve.wait_ge(exped, i + 1)
                    step(dve.tensor_tensor(top[:, b, :, 3], top[:, b, :, 1], top[:, b, :, 2], ALU.add))
                    step(dve.reciprocal(top[:, b, :, 3], top[:, b, :, 3]))
                    for t in range(2):
                        ins = dve.tensor_scalar(sc[:, b, t, lo:lo + width], sc[:, b, t, lo:lo + width],
                                                top[:, b, t, 3:4], None, ALU.mult)
                    ins.then_inc(probs, 1)

                dve.wait_ge(sink_in, 16)
                dve.wait_ge(masked, 3)
                maxes(0)
                for i in range(PAIRS):
                    if i + 1 < PAIRS:
                        maxes(i + 1)
                    norms(i)
                dve.wait_ge(bs_in, 32)
                for n in range(M):
                    dve.wait_ge(g_done, n + 1)
                    out = c.mixT[:, AJ:, n * P:n * P + P]
                    dve.tensor_tensor(out, X[:, n % 2, :, :], bsb[:], ALU.add).then_inc(g_taken, 1)
                    dve.wait_ge(g_taken, n + 1)
                    step(dve.tensor_tensor(out, out, c.uT2[:, :, n * P:n * P + P], ALU.mult))


def stage_route(nc, c, a):
    ME = [P, M, EXPERTS]
    with Stage(nc, "route") as s:
        wr = s.sb("wr", [P, KD, EXPERTS])
        br = s.sb("br", [P, EXPERTS])
        bd = s.sb("bd", [EXPERTS, D])
        logit = s.sb("logit", ME)
        v8 = s.sb("v8", [P, M, 8])
        i8 = s.sb("i8", [P, M, 8], U32)
        i4 = s.sb("i4", [P, M, EK])
        gate = s.sb("gate", [P, M, EK])
        tot = s.sb("tot", [P, M])
        hot = s.sb("hot", [P, M * EK, EXPERTS])
        hg = s.sb("hg", [P, M * EK, EXPERTS])
        mem = s.sb("mem", ME)
        ge = s.sb("ge", ME)
        rank = s.sb("rank", ME)
        over = s.sb("over", ME)
        tmp = s.sb("tmp", ME)
        cnt = s.sb("cnt", [P, EXPERTS])
        nb = s.sb("nb", [P, EXPERTS])
        t2 = s.sb("t2", [P, EXPERTS])
        onesE = s.sb("onesE", [P, EXPERTS])
        end = s.sb("end", [P, EXPERTS])
        start = s.sb("start", [P, EXPERTS])
        dest = s.sb("dest", [P, M * EK])
        desti = s.sb("desti", [P, M * EK], U32)
        entry = s.sb("entry", [P, M * EK, 4], I32)
        blank = s.sb("blank", [P, NBLK, 4], I32)
        ecmp = s.sb("ecmp", [1, NBLK, EXPERTS])
        ownf = s.sb("ownf", [1, NBLK])
        geT = s.sb("geT", [EXPERTS, M, P])
        ps = s.ps("ps", [P, 8, 512])
        wr_in, bd_in, br_in = s.sem("wr_in"), s.sem("bd_in"), s.sem("br_in")
        (l_done, shifted, exped, chain, mem_ok, cnt_done, ge_ok, turned, gt_ok, b_done, b_taken, blanked, blank_out,
         ids, dest_ok, scattered, back) = (s.sem(n) for n in (
             "l_done", "shifted", "exped", "chain", "mem_ok", "cnt_done", "ge_ok", "turned", "gt_ok", "b_done",
             "b_taken", "blanked", "blank_out", "ids", "dest_ok", "scattered", "back"))
        table = c.table
        with s.block() as block:

            @block.sync
            def _(sp):
                sp.dma_start(wr[:], rows(a["w_router_2"][0])).then_inc(wr_in, 16)
                sp.dma_start(br[:], a["b_router_2"].to_broadcast([P, EXPERTS])).then_inc(br_in, 16)
                sp.dma_start(bd[:], a["b_down_2"][0]).then_inc(bd_in, 16)
                sp.wait_ge(blanked, 2)
                sp.dma_start(table.rearrange("(p r) w -> p r w", p=P), blank[:]).then_inc(blank_out, 16)

            @block.gpsimd
            def _(pool):
                pool.memset(blank[:], 0).then_inc(ids, 1)
                pool.wait_ge(ids, 1)
                pool.memset(blank[:, :, 1:2], 4 * ROWS).then_inc(blanked, 1)
                pool.memset(entry[:], 0).then_inc(blanked, 1)
                pool.wait_ge(blanked, 2)
                e4 = entry[:].rearrange("p (m k) w -> p m k w", m=M)
                pool.iota(e4[:, :, :, 0], pattern=[[P, M], [0, EK]], base=0, channel_multiplier=1).then_inc(ids, 1)
                pool.iota(e4[:, :, :, 1], pattern=[[P * EK, M], [1, EK]], base=0, channel_multiplier=EK).then_inc(ids, 1)
                pool.wait_ge(blank_out, 16)
                pool.wait_ge(dest_ok, 1)
                for i in range(M * EK):
                    pool.indirect_dma_start(out=table[:, :], out_offset=bass.IndirectOffsetOnAxis(ap=desti[:, i:i + 1], axis=0),
                                            in_=entry[:, i, :], in_offset=None, bounds_check=P * NBLK - 1,
                                            oob_is_err=False).then_inc(scattered, 16)
                pool.wait_ge(scattered, 16 * M * EK)
                pool.dma_start(c.slots[:, 0:NBLK, :], table.rearrange("(p r) w -> p r w", p=P)).then_inc(back, 16)
                pool.wait_ge(back, 16)

            @block.tensor
            def _(pe):
                pe.wait_ge(wr_in, 16)
                for m in range(M):
                    for k in range(KD):
                        mm = pe.matmul(ps[:, 0, m * EXPERTS:(m + 1) * EXPERTS], c.hT[:, k, m * P:m * P + P], wr[:, k, :],
                                       start=(k == 0), stop=(k == KD - 1))
                mm.then_inc(l_done, 1)
                pe.wait_ge(mem_ok, 1)
                for m in range(M):
                    for q in range(m + 1):
                        pe.matmul(ps[:, 1, m * EXPERTS:(m + 1) * EXPERTS], c.upper[:] if q == m else c.ones[:],
                                  mem[:, q, :], start=(q == 0), stop=(q == m))
                for q in range(M):
                    mm = pe.matmul(ps[:, 2, 0:EXPERTS], c.ones[:], mem[:, q, :], start=(q == 0), stop=(q == M - 1))
                mm.then_inc(cnt_done, 1)
                pe.wait_ge(ge_ok, 1)
                for m in range(M):
                    t = pe.transpose(ps[0:EXPERTS, 3, m * P:m * P + P], ge[:, m, :], c.ident[:])
                t.then_inc(turned, 1)
                pe.wait_ge(gt_ok, 1)
                pe.wait_ge(bd_in, 16)
                for i in range(2 * M):
                    m, n = i // 2, i % 2
                    if i >= 4:
                        pe.wait_ge(b_taken, i - 3)
                    pe.matmul(ps[:, 4 + i % 4, :], geT[:, m, :], bd[:, n * 512:n * 512 + 512],
                              start=True, stop=True).then_inc(b_done, 1)

            @block.scalar
            def _(act):
                act.wait_ge(shifted, 1)
                act.activation(gate[:], gate[:], ACT.Exp).then_inc(exped, 1)
                act.wait_ge(turned, 1)
                act.activation(geT[:], ps[0:EXPERTS, 3, :].rearrange("e (m t) -> e m t", m=M), ACT.Copy).then_inc(gt_ok, 1)

            @block.vector
            def _(dve):
                step = chained(dve, chain)
                step(dve.memset(onesE[:], 1.0))
                dve.wait_ge(br_in, 16)
                dve.wait_ge(l_done, 1)
                step(dve.tensor_tensor(logit[:], ps[:, 0, 0:M * EXPERTS].rearrange("p (m e) -> p m e", m=M),
                                       br[:].unsqueeze(1).to_broadcast(ME), ALU.add))
                for m in range(M):
                    ins = dve.max(v8[:, m, :], logit[:, m, :])
                step(ins)
                for m in range(M):
                    ins = dve.max_index(i8[:, m, :], v8[:, m, :], logit[:, m, :])
                step(ins)
                dve.tensor_tensor(gate[:], v8[:, :, 0:EK], v8[:, :, 0:1].to_broadcast([P, M, EK]),
                                  ALU.subtract).then_inc(shifted, 1)
                step(dve.tensor_copy(i4[:], i8[:, :, 0:EK]))
                step(dve.tensor_tensor(hot[:], i4[:].rearrange("p m k -> p (m k)").unsqueeze(2).to_broadcast([P, M * EK, EXPERTS]),
                                       c.count[:, 0:EXPERTS].unsqueeze(1).to_broadcast([P, M * EK, EXPERTS]), ALU.is_equal))
                hot4 = hot[:].rearrange("p (m k) e -> p m k e", m=M)
                by_e = "p (m k) e -> p m e k"
                for m in range(M):
                    ins = dve.tensor_reduce(mem[:, m, :], hot[:, m * EK:(m + 1) * EK, :].rearrange("p k e -> p e k"),
                                            AX.X, ALU.add)
                ins.then_inc(mem_ok, 1)
                dve.wait_ge(mem_ok, 1)
                dve.wait_ge(exped, 1)
                step(dve.tensor_reduce(tot[:], gate[:], AX.X, ALU.add))
                step(dve.reciprocal(tot[:], tot[:]))
                step(dve.tensor_tensor(gate[:], gate[:], tot[:].unsqueeze(2).to_broadcast([P, M, EK]), ALU.mult))
                step(dve.tensor_tensor(hg[:], hot[:], gate[:].rearrange("p m k -> p (m k)").unsqueeze(2)
                                       .to_broadcast([P, M * EK, EXPERTS]), ALU.mult))
                for m in range(M):
                    ins = dve.tensor_reduce(ge[:, m, :], hg[:, m * EK:(m + 1) * EK, :].rearrange("p k e -> p e k"),
                                            AX.X, ALU.add)
                ins.then_inc(ge_ok, 1)
                dve.wait_ge(cnt_done, 1)
                step(dve.tensor_copy(cnt[:], ps[:, 2, 0:EXPERTS]))
                step(dve.tensor_scalar(nb[:], cnt[:], 0.0, None, ALU.is_gt))
                for r in range(1, T // P):
                    step(dve.tensor_scalar(t2[:], cnt[:], float(P * r), None, ALU.is_gt))
                    step(dve.tensor_tensor(nb[:], nb[:], t2[:], ALU.add))
                step(dve.tensor_tensor_scan(end[:], onesE[:], nb[:], 0.0, ALU.mult, ALU.add))
                step(dve.tensor_tensor(start[:], end[:], nb[:], ALU.subtract))
                step(dve.tensor_scalar(rank[:], ps[:, 1, 0:M * EXPERTS].rearrange("p (m e) -> p m e", m=M), -1.0, None, ALU.add))
                step(dve.tensor_scalar(over[:], rank[:], float(P), None, ALU.is_ge))
                for r in range(2, T // P):
                    step(dve.tensor_scalar(tmp[:], rank[:], float(P * r), None, ALU.is_ge))
                    step(dve.tensor_tensor(over[:], over[:], tmp[:], ALU.add))
                step(dve.tensor_scalar(over[:], over[:], -float(P * NBLK - 1), None, ALU.mult))
                step(dve.scalar_tensor_tensor(out=rank[:], in0=rank[:], scalar=float(NBLK), in1=over[:],
                                              op0=ALU.mult, op1=ALU.add))
                step(dve.tensor_tensor(rank[:], rank[:], start[:].unsqueeze(1).to_broadcast(ME), ALU.add))
                step(dve.tensor_tensor(hg[:].rearrange("p (m k) e -> p m k e", m=M), hot4,
                                       rank[:].unsqueeze(2).to_broadcast([P, M, EK, EXPERTS]), ALU.mult))
                step(dve.tensor_reduce(dest[:], hg[:], AX.X, ALU.add))
                step(dve.tensor_copy(desti[:], dest[:]))
                dve.wait_ge(ids, 3)
                dve.tensor_copy(entry[:, :, 2], gate[:].rearrange("p m k -> p (m k)").bitcast(I32)).then_inc(dest_ok, 1)
                step(dve.tensor_tensor(ecmp[:], end[0:1, :].unsqueeze(1).to_broadcast([1, NBLK, EXPERTS]),
                                       c.count[0:1, 0:NBLK].unsqueeze(2).to_broadcast([1, NBLK, EXPERTS]), ALU.is_le))
                step(dve.tensor_reduce(ownf[:], ecmp[:], AX.X, ALU.add))
                step(dve.tensor_scalar(ownf[:], ownf[:], float(EXPERTS - 1), None, ALU.min))
                step(dve.tensor_copy(c.owner[0:1, 0:NBLK], ownf[:]))
                step(dve.tensor_copy(c.owner[0:1, NBLK:NBLK + 1], end[0:1, EXPERTS - 1:EXPERTS]))
                for i in range(2 * M):
                    m, n = i // 2, i % 2
                    dve.wait_ge(b_done, i + 1)
                    out = c.h[:, m, n * 512:n * 512 + 512]
                    dve.scalar_tensor_tensor(out=out, in0=out, scalar=ALPHA, in1=ps[:, 4 + i % 4, :],
                                             op0=ALU.mult, op1=ALU.add).then_inc(b_taken, 1)


def stage_experts(nc, c, a):
    CHUNK = 512
    HT = 4
    with Stage(nc, "moe") as s:
        wb = [s.sb(f"w{i}", [P, 4096]) for i in range(6)]
        bias_all = s.sb("bias_all", [P, EXPERTS, 2 * KD])
        bias = s.sb("bias", [P, 2, 2 * KD])
        slot = s.sb("slot", [P, 2, 4], I32)
        xg = s.sb("xg", [P, 2, D])
        xT = s.sb("xT", [P, 2, KD, P])
        ga = s.sb("ga", [P, HT, P])
        up = s.sb("up", [P, HT, P])
        sg = s.sb("sg", [P, HT, P])
        hid = s.sb("hid", [P, KD, P])
        y = s.sb("y", [P, 2, D])
        GU = s.ps("GU", [P, 4, HT, P])
        Y = s.ps("Y", [P, 2, CHUNK])
        X = s.ps("X", [P, 2, 4, P])
        w_in = [s.sem(f"w_in{i}") for i in range(6)]
        w_used = [s.sem(f"w_used{i}") for i in range(6)]
        bias_in = s.sem("bias_in")
        gathered = [s.sem(f"gathered{i}") for i in range(2)]
        (slotted, cleared, biased, x_done, x_ok, gu_done, g_ok, u_ok, sig, h_chain, h_ok, gu_free, y_done, y_ok,
         stored, paced) = (s.sem(n) for n in ("slotted", "cleared", "biased", "x_done", "x_ok", "gu_done", "g_ok", "u_ok",
                                           "sig", "h_chain", "h_ok", "gu_free", "y_done", "y_ok", "stored", "paced"))
        wg_d, wu_d, wd_d = (a[n][0] for n in ("w_gate_2", "w_up_2", "w_down_2"))

        def n_blocks(eng):
            return eng.value_load(c.owner[0:1, NBLK:NBLK + 1], min_val=1, max_val=BLOCKS)

        def owner_of(eng, j):
            return eng.value_load(c.owner[0:1, ds(j, 1)], min_val=0, max_val=EXPERTS - 1)

        with s.block() as block:

            @block.sync
            def _(sp):
                sp.dma_start(bias_all[:], a["bias_gate_up"]).then_inc(bias_in, 16)
                n = n_blocks(sp)
                with sp.Fori(0, BLOCKS) as j:
                    with sp.If(j < n):
                        e = owner_of(sp, j)
                        for half in range(2):
                            for i, w_d in ((0, wg_d), (1, wu_d)):
                                q = 2 * half + i
                                src = w_d[ds(e, 1), :, half * CHUNK:(half + 1) * CHUNK].rearrange("o (k p) n -> p (o k) n", p=P)
                                sp.wait_ge(w_used[q], j + 1)
                                sp.dma_start(wb[q][:].rearrange("p (k n) -> p k n", k=KD), src).then_inc(w_in[q], 16)
                        for half in range(2):
                            q = 4 + half
                            src = wd_d[ds(e, 1), half * CHUNK:(half + 1) * CHUNK, :].rearrange("o (k p) n -> p (o k) n", p=P)
                            sp.wait_ge(w_used[q], j + 1)
                            sp.dma_start(wb[q][:].rearrange("p (k n) -> p k n", k=HT), src).then_inc(w_in[q], 16)

            @block.gpsimd
            def _(pool):
                n = n_blocks(pool)

                def gather(j, b):
                    pool.tensor_copy(slot[:, b, :], c.slots[:, ds(j, 1), :].rearrange("p o w -> p (o w)")).then_inc(slotted, 1)
                    pool.wait_ge(slotted, j + 1)
                    pool.sem_inc(paced, 1)
                    pool.indirect_dma_start(out=xg[:, b, :], out_offset=None, in_=c.h_rows[:, :],
                                            in_offset=bass.IndirectOffsetOnAxis(ap=slot[:, b, 0:1].bitcast(U32), axis=0),
                                            bounds_check=T - 1, oob_is_err=False).then_inc(gathered[b], 16)

                gather(0, 0)
                with pool.Fori(0, NBLK // 2) as it:
                    for u in range(2):
                        j = it * 2 + u
                        with pool.If(j + 1 < n):
                            gather(j + 1, 1 - u)
                        with pool.If(j < n):
                            pool.wait_ge(y_ok, j + 2)
                            pool.sem_inc(paced, 1)
                            pool.indirect_dma_start(out=c.pair_rows[:, :],
                                                    out_offset=bass.IndirectOffsetOnAxis(ap=slot[:, u, 1:2].bitcast(U32), axis=0),
                                                    in_=y[:, u, :], in_offset=None, bounds_check=ROWS - 1,
                                                    oob_is_err=False).then_inc(stored, 16)
                            pool.wait_ge(stored, j * 16 + 16)

            @block.tensor
            def _(pe):
                n = n_blocks(pe)

                def turn(j, b, nth):
                    pe.wait_ge(gathered[b], nth * 16 + 16)
                    pe.wait_ge(x_ok, j + 1)
                    for h in range(2):
                        for k in range(4):
                            t = pe.transpose(X[:, h, k, :], xg[:, b, (4 * h + k) * P:(4 * h + k + 1) * P], c.ident[:])
                    t.then_inc(x_done, 1)

                for q in range(6):
                    pe.sem_inc(w_used[q], 1)
                turn(0, 0, 0)
                with pe.Fori(0, NBLK // 2) as it:
                    for u in range(2):
                        j = it * 2 + u
                        with pe.If(j < n):
                            pe.wait_ge(x_ok, j + 2)
                            pe.wait_ge(gu_free, j * 4 + 1)
                            for q in range(4):
                                pe.wait_ge(w_in[q], j * 16 + 16)
                                w = wb[q][:].rearrange("p (k n) -> p k n", k=KD)
                                for f in range(HT):
                                    for k in range(KD):
                                        mm = pe.matmul(GU[:, q, f, :], w[:, k, f * P:f * P + P], xT[:, u, k, :],
                                                       start=(k == 0), stop=(k == KD - 1))
                                mm.then_inc(w_used[q], 1)
                            with pe.If(j + 1 < n):
                                turn(j + 1, 1 - u, it + u)
                            pe.wait_ge(y_ok, j + 1)
                            for half in range(2):
                                q = 4 + half
                                pe.wait_ge(w_in[q], j * 16 + 16)
                                pe.wait_ge(h_ok, j * 2 + half + 1)
                                w = wb[q][:].rearrange("p (k n) -> p k n", k=HT)
                                for b in range(2):
                                    for f in range(HT):
                                        mm = pe.matmul(Y[:, b, :], hid[:, HT * half + f, :], w[:, f, b * CHUNK:(b + 1) * CHUNK],
                                                       start=(half == 0 and f == 0), stop=(half == 1 and f == HT - 1))
                                mm.then_inc(w_used[q], 1)

            @block.scalar
            def _(act):
                n = n_blocks(act)

                def take_x(j, b):
                    act.wait_ge(x_done, j + 1)
                    act.activation(xT[:, b, 0:4, :], X[:, 0, :, :], ACT.Copy)
                    act.activation(xT[:, b, 4:8, :], X[:, 1, :, :], ACT.Copy).then_inc(x_ok, 1)

                act.sem_inc(x_ok, 1)
                take_x(0, 0)
                with act.Fori(0, NBLK // 2) as it:
                    for u in range(2):
                        j = it * 2 + u
                        with act.If(j < n):
                            act.wait_ge(g_ok, j * 2 + 1)
                            act.activation(sg[:], ga[:], ACT.Sigmoid, scale=SWIGLU).then_inc(sig, 1)
                            act.wait_ge(g_ok, j * 2 + 2)
                            act.activation(sg[:], ga[:], ACT.Sigmoid, scale=SWIGLU).then_inc(sig, 1)
                            with act.If(j + 1 < n):
                                take_x(j + 1, 1 - u)

            @block.vector
            def _(dve):
                n = n_blocks(dve)
                dve.sem_inc(gu_free, 1)
                dve.sem_inc(y_ok, 1)
                dve.wait_ge(bias_in, 16)
                with dve.Fori(0, NBLK // 2) as it:
                    for u in range(2):
                        j = it * 2 + u
                        with dve.If(j < n):
                            e = owner_of(dve, j)
                            dve.tensor_copy(bias[:, u, :], bias_all[:, ds(e, 1), :].rearrange("p o w -> p (o w)")).then_inc(biased, 1)
                            dve.wait_ge(biased, j + 1)
                            for half in range(2):
                                h = slice(HT * half, HT * half + HT)
                                dve.wait_ge(w_used[2 * half], j + 2)
                                for f in range(HT):
                                    ins = dve.tensor_scalar(ga[:, f, :], GU[:, 2 * half, f, :], bias[:, u, HT * half + f:HT * half + f + 1],
                                                            LIMIT, ALU.add, ALU.min)
                                ins.then_inc(g_ok, 1)
                                dve.wait_ge(w_used[2 * half + 1], j + 2)
                                for f in range(HT):
                                    o = KD + HT * half + f
                                    ins = dve.tensor_scalar(up[:, f, :], GU[:, 2 * half + 1, f, :], bias[:, u, o:o + 1],
                                                            LIMIT, ALU.add, ALU.min)
                                ins.then_inc(gu_free, 2)
                                dve.wait_ge(gu_free, j * 4 + (2 * half + 3))
                                dve.tensor_scalar(up[:], up[:], -LIMIT, 1.0, ALU.max, ALU.add).then_inc(h_chain, 1)
                                dve.wait_ge(sig, j * 2 + half + 1)
                                dve.tensor_tensor(ga[:], ga[:], sg[:], ALU.mult).then_inc(h_chain, 1)
                                dve.wait_ge(h_chain, j * 4 + (2 * half + 2))
                                dve.tensor_tensor(hid[:, h, :], ga[:], up[:], ALU.mult).then_inc(h_ok, 1)
                                dve.wait_ge(h_ok, j * 2 + half + 1)
                            dve.wait_ge(w_used[5], j + 2)
                            for b in range(2):
                                ins = dve.tensor_scalar(y[:, u, b * CHUNK:(b + 1) * CHUNK], Y[:, b, :],
                                                        c.slots[:, ds(j, 1), 2:3].bitcast(F32).rearrange("p o w -> p (o w)"),
                                                        None, ALU.mult)
                            ins.then_inc(y_ok, 1)


def stage_combine(nc, c, a):
    with Stage(nc, "comb") as s:
        r = s.sb("r", [P, M, EK, D])
        loaded = [s.sem(f"loaded{m}") for m in range(M)]
        chain = s.sem("chain")
        src = c.pair_rows.rearrange("(m p k) d -> p m k d", p=P, k=EK)
        with s.block() as block:

            @block.sync
            def _(sp):
                for m in range(M):
                    sp.dma_start(r[:, m, :, :], src[:, m, :, :]).then_inc(loaded[m], 16)

            @block.vector
            def _(dve):
                step = chained(dve, chain)
                for m in range(M):
                    dve.wait_ge(loaded[m], 16)
                    for k in range(EK):
                        step(dve.tensor_tensor(c.h[:, m, :], c.h[:, m, :], r[:, m, k, :], ALU.add))


def program(nc, a, out):
    with ExitStack() as ctx:
        c = Common(nc, ctx)
        c.stream(ctx)
        stage_constants(nc, c)
        with ExitStack() as front:
            c.front(front)
            stage_norm_in(nc, c, a)
            stage_project(nc, c, a)
            stage_conf_norm(nc, c, a)
            stage_ssd(nc, c, a)
            stage_out_proj(nc, c, a, "out1", c.yT, a["w_out"][0], 2 * KD, a["x"][0], 1.0)
        with ExitStack() as peer:
            c.peer(peer)
            with ExitStack() as tmp:
                xn = c.sb(tmp, "xn", [P, M, D])
                stage_token_norm(nc, c, a, "nffn", xn, c.hT, col_w=a["norm_ffn_w"])
            stage_peer_scores(nc, c, a)
            stage_gate_matrix(nc, c, a)
            stage_peer_experts(nc, c, a)
        stage_token_norm(nc, c, a, "nfin", c.h, c.hT, row_w=a["norm_final_w"])
        second_block(nc, c, a, out)


def second_block(nc, c, a, out):
    with ExitStack() as mix:
        c.second(mix)
        stage_project2(nc, c, a)
        stage_attention(nc, c, a)
        stage_out_proj(nc, c, a, "out2", c.mixT, a["w_out_2"], KD, None, ALPHA, bias=a["b_out_2"])
    with ExitStack() as moe:
        c.routed(moe)
        stage_token_norm(nc, c, a, "ln1", c.h, c.hT, centre=True, row_w=a["ln1_g_2"], row_b=a["ln1_b_2"], save=c.h_rows)
        stage_route(nc, c, a)
        stage_experts(nc, c, a)
        stage_combine(nc, c, a)
        stage_token_norm(nc, c, a, "ln2", c.h, centre=True, row_w=a["ln2_g_2"], row_b=a["ln2_b_2"], save=out[0])


class Common:

    def __init__(self, nc, ctx):
        self.nc = nc
        self.ident = self.sb(ctx, "ident", [P, P])
        self.ones = self.sb(ctx, "ones", [P, P])
        self.upper = self.sb(ctx, "upper", [P, P])
        self.count = self.sb(ctx, "count", [P, P])
        self.count_i = self.sb(ctx, "count_i", [P, P], I32)

    def sb(self, ctx, name, shape, dt=F32):
        return ctx.enter_context(self.nc.sbuf_tensor(f"all_{name}", shape, dt))

    def stream(self, ctx):
        self.h = self.sb(ctx, "h", [P, M, D])
        self.hT = self.sb(ctx, "hT", [P, KD, T])

    def peer(self, ctx):
        self.idxT = self.sb(ctx, "idxT", [P, 3, T])
        self.gates = self.nc.dram_tensor("peer_gates", [BATCHES, NK, NK * TB], F32, kind="Internal").ap()

    def second(self, ctx):
        self.qT = self.sb(ctx, "qT", [P, AJ, T])
        self.kT = self.sb(ctx, "kT", [P, T])
        self.uT2 = self.sb(ctx, "uT2", [P, 4, T])
        self.vtok = self.sb(ctx, "vtok", [P, M, P])
        self.gtok = self.sb(ctx, "gtok", [P, M, 512])
        self.mixT = self.sb(ctx, "mixT", [P, KD, T])

    def routed(self, ctx):
        self.slots = self.sb(ctx, "slots", [P, NBLK + 1, 4], I32)
        self.owner = self.sb(ctx, "owner", [1, NBLK + 1], I32)
        self.table = self.nc.dram_tensor("slot_table", [P * NBLK, 4], I32, kind="Internal").ap()
        self.h_rows = self.nc.dram_tensor("h_rows", [T, D], F32, kind="Internal").ap()
        self.pair_rows = self.nc.dram_tensor("pair_rows", [ROWS, D], F32, kind="Internal").ap()

    def front(self, ctx):
        self.yT = self.sb(ctx, "yT", [P, 2 * KD, T])
        self.uT = self.sb(ctx, "uT", [P, KD, TA])
        self.xbcT = self.sb(ctx, "xbcT", [P, 16, TA])
        self.zT = self.sb(ctx, "zT", [P, KD, T])
        self.dt = self.sb(ctx, "dt", [P, M + 1, HEADS])
        self.dta = self.sb(ctx, "dta", [P, M + 1, HEADS])


FRONT = ("x", "meta_tokens", "norm_mix_w", "w_in", "ssd_dt_bias", "conf_taps", "conf_conv_b", "ssd_taps",
         "ssd_conv_b", "ssd_A_log", "ssd_D", "ssd_norm_w", "conf_ln_g", "conf_ln_b")


def layout(inputs):
    import numpy as np
    v = {k: np.asarray(x) for k, x in inputs.items()}

    def channels(x):
        return np.ascontiguousarray(x.reshape(-1, P).T)

    def channel_rows(x):
        return np.ascontiguousarray(x.reshape(x.shape[0], -1, P).transpose(2, 1, 0))

    out = {k: v[k] for k in ("x", "meta_tokens", "w_in", "ssd_dt_bias", "ssd_A_log")}
    for k in ("norm_mix_w", "conf_conv_b", "ssd_conv_b", "ssd_norm_w", "conf_ln_g", "conf_ln_b"):
        out[k] = channels(v[k][0])
    out["conf_taps"] = channel_rows(v["conf_conv_w"][0])
    out["ssd_taps"] = channel_rows(v["ssd_conv_w"][0])
    out["ssd_D"] = channels(np.repeat(v["ssd_D"][0], 64))
    keys = np.stack([v["peer_sub_keys_1"][0], v["peer_sub_keys_2"][0]], 1)
    out["peer_keysT"] = np.ascontiguousarray(keys.reshape(2 * PH, NK, P).transpose(2, 0, 1))
    for k in ("w_out", "peer_w_query", "peer_w_up"):
        out[k] = v[k]
    out["peer_w_downT"] = np.ascontiguousarray(v["peer_w_down"][0].T)
    out["norm_ffn_w"] = channels(v["norm_ffn_w"][0])
    out["norm_final_w"] = v["norm_final_w"][None]
    heads = np.arange(AH * 64).reshape(2, AJ, 64).transpose(1, 0, 2).reshape(-1)
    cols = np.concatenate([heads, np.arange(AH * 64, 1792)])
    out["w_in_2"] = np.ascontiguousarray(v["w_in_2"][0][:, cols])
    out["b_in_2_col"] = channels(v["b_in_2"][0][cols])
    out["b_in_2_row"] = np.concatenate([v["b_in_2"][:, COL_V:COL_U], v["b_in_2"][:, COL_S:]], 1)
    out["w_out_2"] = np.ascontiguousarray(v["w_out_2"][0][np.concatenate([heads, np.arange(AH * 64, D)])])
    out["w_spatial_2T"] = np.ascontiguousarray(v["w_spatial_2"][0].transpose(2, 0, 1))
    bias = np.stack([v["b_gate_2"][0], v["b_up_2"][0]], 1)
    out["bias_gate_up"] = np.ascontiguousarray(bias.reshape(EXPERTS, 2 * KD, P).transpose(2, 0, 1))
    for k in ("ln_v_g_2", "ln_v_b_2", "sinks_2", "b_spatial_2", "b_out_2", "ln1_g_2", "ln1_b_2", "w_router_2",
              "b_router_2", "w_gate_2", "w_up_2", "w_down_2", "b_down_2", "ln2_g_2", "ln2_b_2"):
        out[k] = v[k]
    return out


def kernel(**inputs):
    from concourse import bacc
    from concourse.bass_utils import run_bass_kernel_spmd

    nc = bacc.Bacc("TRN2", target_bir_lowering=False, num_devices=1)
    arrays = {f"in_{k}": x for k, x in layout(inputs).items()}
    a = {k[3:]: nc.dram_tensor(k, x.shape, F32, kind="ExternalInput").ap() for k, x in arrays.items()}
    out = nc.dram_tensor("out", (1, T, D), F32, kind="ExternalOutput").ap()
    program(nc, a, out)
    r = run_bass_kernel_spmd(nc, [arrays], core_ids=[0])
    return r.results[0]["out"]
```

```python
from contextlib import ExitStack

import concourse.bass as bass
from concourse import mybir

F32 = mybir.dt.float32
F32R = mybir.dt.float32r
I32 = mybir.dt.int32
U32 = mybir.dt.uint32
ACT = mybir.ActivationFunctionType
ALU = mybir.AluOpType
AX = mybir.AxisListType

P = 128
D = 1024
KD = D // P
T = 512
M = T // P
META = 16
TA = T + META
HALF = TA // 2
EPS = 1e-5
D_XBC = 2048
HEADS = 16
GROUPS = 4
XT = KD
NB, NC_ = 4, 4
CONV = 4
CK = 31
COL_XBC, COL_DT, COL_A, COL_G = 1024, 3072, 3088, 4112
PH = 8
TOPK = 16
NK = 128
ds = bass.ds


def chained(eng, sem, start=0):
    n = [start]

    def step(ins):
        n[0] += 1
        ins.then_inc(sem, 1)
        eng.wait_ge(sem, n[0])
    return step


class Stage:

    def __init__(self, nc, name):
        self.nc, self.name, self.ctx, self.sems = nc, name, ExitStack(), []

    def __enter__(self):
        self.ctx.__enter__()
        return self

    def __exit__(self, *a):
        if a[0] is None:
            self.nc.clear_and_free_semaphores(self.sems)
            self.nc.all_engine_barrier()
        return self.ctx.__exit__(*a)

    def sb(self, name, shape, dt=F32):
        return self.ctx.enter_context(self.nc.sbuf_tensor(f"{self.name}_{name}", shape, dt))

    def ps(self, name, shape, dt=F32):
        return self.ctx.enter_context(self.nc.psum_tensor(f"{self.name}_{name}", shape, dt))

    def sem(self, name):
        self.sems.append(self.nc.alloc_semaphore(f"{self.name}_{name}"))
        return self.sems[-1]

    def block(self):
        return self.nc.Block()


def tokens(ap):
    return ap.rearrange("(m p) d -> p m d", p=P)


def rows(ap):
    return ap.rearrange("(k p) n -> p k n", p=P)


def stage_constants(nc, c):
    with Stage(nc, "const") as s:
        made = s.sem("made")
        with s.block() as block:

            @block.gpsimd
            def _(pool):
                pool.memset(c.ident[:], 0.0).then_inc(made, 1)
                pool.memset(c.ones[:], 1.0).then_inc(made, 1)
                pool.wait_ge(made, 2)
                pool.affine_select(out=c.ident[:], in_=c.ident[:], compare_op=ALU.not_equal, fill=1.0, base=0,
                                   pattern=[[-1, P]], channel_multiplier=1).then_inc(made, 1)
                pool.affine_select(out=c.upper[:], in_=c.ones[:], compare_op=ALU.is_ge, fill=0.0, base=0,
                                   pattern=[[1, P]], channel_multiplier=-1).then_inc(made, 1)
                pool.iota(c.count_i[:], pattern=[[1, P]], base=0, channel_multiplier=0).then_inc(made, 1)
                pool.wait_ge(made, 5)
                pool.tensor_copy(c.count[:], c.count_i[:]).then_inc(made, 1)
                pool.wait_ge(made, 6)


def stage_norm_in(nc, c, a):
    with Stage(nc, "norm") as s:
        x = s.sb("x", [P, M + 1, D])
        junk = s.sb("junk", [P, D])
        wn = s.sb("wn", [P, KD])
        ss = s.sb("ss", [P, M + 1])
        root = s.sb("root", [P, M + 1])
        tp = s.ps("tp", [P, 4, 4, P])
        loaded = [s.sem(f"loaded{m}") for m in range(M + 1)]
        wn_in = s.sem("wn_in")
        cleared, squared, rooted, scaled = (s.sem(n) for n in ("cleared", "squared", "rooted", "scaled"))
        chain, turned, copied = s.sem("chain"), s.sem("turned"), s.sem("copied")
        with s.block() as block:

            @block.sync
            def _(sp):
                for m in range(M):
                    sp.dma_start(x[:, m, :], tokens(a["x"][0])[:, m, :]).then_inc(loaded[m], 16)
                sp.dma_start(x[0:META, M, :], a["meta_tokens"]).then_inc(loaded[M], 16)
                sp.dma_start(wn[:], a["norm_mix_w"]).then_inc(wn_in, 16)

            @block.scalar
            def _(act):
                act.wait_ge(cleared, 1)
                for m in range(M + 1):
                    n = P if m < M else META
                    act.wait_ge(loaded[m], 16)
                    act.activation(junk[0:n, :], x[0:n, m, :], ACT.Square,
                                   accum_out=ss[0:n, m:m + 1]).then_inc(squared, 1)
                    act.wait_ge(squared, m + 1)
                act.wait_ge(scaled, 1)
                act.activation(root[:], root[:], ACT.Sqrt).then_inc(rooted, 1)

            @block.vector
            def _(dve):
                step = chained(dve, chain)
                dve.memset(ss[:], 1.0).then_inc(cleared, 1)
                dve.wait_ge(squared, M + 1)
                dve.tensor_scalar(root[:], ss[:], 1.0 / D, EPS, ALU.mult, ALU.add).then_inc(scaled, 1)
                dve.wait_ge(rooted, 1)
                step(dve.reciprocal(ss[:], root[:]))
                for m in (M, *range(M)):
                    n = P if m < M else META
                    dve.tensor_scalar(x[0:n, m, :], x[0:n, m, :], ss[0:n, m:m + 1], None,
                                      ALU.mult).then_inc(scaled, 1)
                dve.wait_ge(wn_in, 16)
                i = 0
                for m in (M, *range(M)):
                    n, at = (P, META + m * P) if m < M else (META, 0)
                    for h in range(2):
                        dve.wait_ge(turned, i + 1)
                        dve.tensor_tensor(c.uT[:, 4 * h:4 * h + 4, at:at + n], tp[:, i % 4, :, 0:n],
                                          wn[:, 4 * h:4 * h + 4].unsqueeze(2).to_broadcast([P, 4, n]),
                                          ALU.mult).then_inc(copied, 1)
                        i += 1

            @block.tensor
            def _(pe):
                i = 0
                for j, m in enumerate((M, *range(M))):
                    n = P if m < M else META
                    pe.wait_ge(scaled, 2 + j)
                    for h in range(2):
                        if i >= 4:
                            pe.wait_ge(copied, i - 3)
                        for k in range(4):
                            t = pe.transpose(tp[:, i % 4, k, 0:n], x[0:n, m, (4 * h + k) * P:(4 * h + k + 1) * P],
                                             c.ident[0:n, 0:n])
                        t.then_inc(turned, 1)
                        i += 1


def stage_project(nc, c, a):
    w_in = rows(a["w_in"][0])
    with Stage(nc, "proj") as s:
        w = [s.sb(f"w{b}", [P, KD, 512]) for b in range(2)]
        wdt = s.sb("wdt", [P, KD, HEADS])
        taps = s.sb("taps", [P, KD, CK])
        cbias = s.sb("cbias", [P, KD])
        xtaps = s.sb("xtaps", [P, 16, CONV])
        xbias = s.sb("xbias", [P, 16])
        dtb = s.sb("dtb", [P, HEADS])
        sg = s.sb("sg", [P, 2, TA])
        pad = CK - 1 - META
        gated = s.sb("gated", [P, 2, pad + TA])
        raw = s.sb("raw", [P, 2, CONV - 1 + TA])
        acc = s.sb("acc", [P, 2, TA])
        e1 = s.sb("e1", [P, M + 1, HEADS])
        e2 = s.sb("e2", [P, M + 1, HEADS])
        e3 = s.sb("e3", [P, M + 1, HEADS])
        ps = s.ps("ps", [P, 8, 512])
        w_in_sem = [s.sem(f"w_in{b}") for b in range(2)]
        consts_in = s.sem("consts_in")
        w_used = s.sem("w_used")
        pair_done, pair_free = s.sem("pair_done"), s.sem("pair_free")
        sig, g_ready, chain = s.sem("sig"), s.sem("g_ready"), s.sem("chain")
        raw_in, raw_free, conv_out, silu_out = (s.sem(n) for n in ("raw_in", "raw_free", "conv_out", "silu_out"))
        zeroed = s.sem("zeroed")
        dt_done, dt_raw, dt_e, dt_l, dt_ok = (s.sem(n) for n in ("dt_done", "dt_raw", "dt_e", "dt_l", "dt_ok"))

        def columns(block_no):
            return [COL_A, COL_G, COL_A + 512, COL_G + 512,
                    *(COL_XBC + 512 * i for i in range(4)), 0, 512][block_no]

        with s.block() as block:

            @block.sync
            def _(sp):
                sp.dma_start(wdt[:], w_in[:, :, COL_DT:COL_DT + HEADS]).then_inc(consts_in, 16)
                sp.dma_start(dtb[:], a["ssd_dt_bias"].to_broadcast([P, HEADS])).then_inc(consts_in, 16)
                sp.dma_start(taps[:], a["conf_taps"]).then_inc(consts_in, 16)
                sp.dma_start(cbias[:], a["conf_conv_b"]).then_inc(consts_in, 16)
                sp.dma_start(xtaps[:], a["ssd_taps"]).then_inc(consts_in, 16)
                sp.dma_start(xbias[:], a["ssd_conv_b"]).then_inc(consts_in, 16)
                for n in range(10):
                    if n >= 2:
                        sp.wait_ge(w_used, n - 1)
                    at = columns(n)
                    sp.dma_start(w[n % 2][:], w_in[:, :, at:at + 512]).then_inc(w_in_sem[n % 2], 16)

            @block.tensor
            def _(pe):
                pe.wait_ge(consts_in, 96)
                for m in range(M + 1):
                    n, at = (META, 0) if m == 0 else (P, META + (m - 1) * P)
                    for k in range(KD):
                        mm = pe.matmul(ps[0:n, 7, 16 * m:16 * m + 16], c.uT[:, k, at:at + n], wdt[:, k, :],
                                       start=(k == 0), stop=(k == KD - 1))
                mm.then_inc(dt_done, 1)
                job = 0

                def tile(buf, col, first=0):
                    nonlocal job
                    if job == 3:
                        pe.wait_ge(dt_raw, 1)
                    if job >= 4:
                        pe.wait_ge(pair_free, job - 3)
                    for h in range(2):
                        for k in range(KD):
                            mm = pe.matmul(ps[:, 2 * (job % 4) + h, 0:HALF], w[buf][:, k, col * P:col * P + P],
                                           c.uT[:, k, h * HALF:(h + 1) * HALF], start=(k == 0), stop=(k == KD - 1))
                    mm.then_inc(pair_done, 1)
                    job += 1
                    return mm

                for half in range(2):
                    pe.wait_ge(w_in_sem[0], 16 * (half + 1))
                    pe.wait_ge(w_in_sem[1], 16 * (half + 1))
                    for i in range(4):
                        tile(0, i)
                        if i == 3:
                            pe.sem_inc(w_used, 1) if False else None
                        tile(1, i)
                    pe.wait_ge(pair_done, job)
                    pe.sem_inc(w_used, 2)
                for n in range(4, 10):
                    pe.wait_ge(w_in_sem[n % 2], 16 * (n // 2 + 1))
                    for i in range(4):
                        tile(n % 2, i)
                    pe.wait_ge(pair_done, job)
                    pe.sem_inc(w_used, 1)

            @block.scalar
            def _(act):
                act.wait_ge(dt_raw, 2)
                act.activation(e2[:], e1[:], ACT.Exp, scale=-1.0).then_inc(dt_e, 1)
                act.wait_ge(dt_e, 1)
                act.activation(e3[:], e2[:], ACT.Ln, bias=1.0).then_inc(dt_l, 1)
                for i in range(8):
                    act.wait_ge(pair_done, 2 * i + 2)
                    if i >= 2:
                        act.wait_ge(g_ready, i - 1)
                    act.activation(sg[:, i % 2, :].rearrange("p (h n) -> p h n", h=2),
                                   ps[:, 2 * ((2 * i + 1) % 4):2 * ((2 * i + 1) % 4) + 2, 0:HALF],
                                   ACT.Sigmoid).then_inc(sig, 1)
                for i in range(16):
                    job = 16 + i
                    act.wait_ge(pair_done, job + 1)
                    act.wait_ge(zeroed, 4)
                    if i >= 2:
                        act.wait_ge(conv_out, i - 1)
                    act.activation(raw[:, i % 2, CONV - 1:].rearrange("p (h n) -> p h n", h=2),
                                   ps[:, 2 * (job % 4):2 * (job % 4) + 2, 0:HALF], ACT.Copy).then_inc(raw_in, 1)
                    if i >= 1:
                        act.wait_ge(conv_out, i)
                        act.activation(c.xbcT[:, i - 1, :], acc[:, (i - 1) % 2, :], ACT.Silu).then_inc(silu_out, 1)
                act.wait_ge(conv_out, 16)
                act.activation(c.xbcT[:, 15, :], acc[:, 1, :], ACT.Silu).then_inc(silu_out, 1)
                for i in range(8):
                    job = 32 + i
                    act.wait_ge(pair_done, job + 1)
                    b = 2 * (job % 4)
                    act.activation(c.zT[:, i, 0:HALF - META], ps[:, b, META:HALF], ACT.Silu)
                    act.activation(c.zT[:, i, HALF - META:T], ps[:, b + 1, 0:HALF], ACT.Silu).then_inc(silu_out, 1)

            @block.vector
            def _(dve):
                step = chained(dve, chain)
                for b in range(2):
                    dve.memset(gated[:, b, 0:pad], 0.0).then_inc(zeroed, 1)
                    dve.memset(raw[:, b, 0:CONV - 1], 0.0).then_inc(zeroed, 1)
                step(dve.memset(e1[:], 0.0))
                step(dve.memset(c.dt[:], 0.0))
                dve.wait_ge(dt_done, 1)
                dtp = ps[:, 7, 0:16 * (M + 1)].rearrange("p (m h) -> p m h", m=M + 1)
                bias = dtb[:].unsqueeze(1).to_broadcast([P, M, HEADS])
                step(dve.tensor_tensor(c.dt[:, 1:M + 1, :], dtp[:, 1:M + 1, :], bias, ALU.add))
                dve.tensor_tensor(c.dt[0:META, 0, :], dtp[0:META, 0, :], dtb[0:META, :], ALU.add).then_inc(dt_raw, 1)
                dve.wait_ge(dt_raw, 1)
                step(dve.tensor_scalar(e2[:], c.dt[:], -1.0, None, ALU.mult))
                dve.tensor_tensor(e1[:], e2[:], c.dt[:], ALU.max).then_inc(dt_raw, 1)
                dve.wait_ge(dt_l, 1)
                step(dve.tensor_scalar(e1[:], e2[:], 1.0, None, ALU.add))
                step(dve.tensor_scalar(e1[:], e1[:], -1.0, None, ALU.add))
                step(dve.tensor_scalar(c.dta[:], e1[:], 0.0, None, ALU.is_equal))
                step(dve.tensor_tensor(e1[:], e1[:], c.dta[:], ALU.add))
                step(dve.tensor_tensor(e3[:], e3[:], c.dta[:], ALU.add))
                step(dve.reciprocal(e1[:], e1[:]))
                step(dve.tensor_tensor(e3[:], e3[:], e1[:], ALU.mult))
                step(dve.tensor_tensor(e3[:], e3[:], e2[:], ALU.mult))
                for n, m in ((META, slice(0, 1)), (P, slice(1, M + 1))):
                    step(dve.scalar_tensor_tensor(out=c.dt[0:n, m, :], in0=c.dt[0:n, m, :], scalar=0.0,
                                                  in1=e3[0:n, m, :], op0=ALU.max, op1=ALU.add))
                for i in range(8):
                    dve.wait_ge(sig, i + 1)
                    b = 2 * ((2 * i) % 4)
                    dve.tensor_tensor(gated[:, i % 2, pad:].rearrange("p (h n) -> p h n", h=2), ps[:, b:b + 2, 0:HALF],
                                      sg[:, i % 2, :].rearrange("p (h n) -> p h n", h=2), ALU.mult).then_inc(g_ready, 1)
                    dve.wait_ge(g_ready, i + 1)
                    dve.sem_inc(pair_free, 2)
                    y = c.yT[:, KD + i, :]
                    step(dve.tensor_scalar(y, gated[:, i % 2, 0:T], taps[:, i, 0:1], cbias[:, i:i + 1],
                                           ALU.mult, ALU.add))
                    for k in range(1, CK):
                        step(dve.scalar_tensor_tensor(out=y, in0=gated[:, i % 2, k:k + T], scalar=taps[:, i, k:k + 1],
                                                      in1=y, op0=ALU.mult, op1=ALU.add))
                for i in range(16):
                    dve.wait_ge(raw_in, i + 1)
                    dve.sem_inc(pair_free, 1)
                    if i >= 2:
                        dve.wait_ge(silu_out, i - 1)
                    y = acc[:, i % 2, :]
                    step(dve.tensor_scalar(y, raw[:, i % 2, 0:TA], xtaps[:, i, 0:1], xbias[:, i:i + 1],
                                           ALU.mult, ALU.add))
                    for k in range(1, CONV):
                        ins = dve.scalar_tensor_tensor(out=y, in0=raw[:, i % 2, k:k + TA], scalar=xtaps[:, i, k:k + 1],
                                                       in1=y, op0=ALU.mult, op1=ALU.add)
                        if k < CONV - 1:
                            step(ins)
                    ins.then_inc(conv_out, 1)
                    dve.wait_ge(conv_out, i + 1)
                for i in range(8):
                    dve.wait_ge(silu_out, 17 + i)
                    dve.sem_inc(pair_free, 1)


def stage_conf_norm(nc, c, a):
    with Stage(nc, "cnorm") as s:
        sq = s.sb("sq", [P, KD, T])
        rstd = s.sb("rstd", [P, T])
        gam = s.sb("gam", [P, KD])
        bet = s.sb("bet", [P, KD])
        tot = s.ps("tot", [P, 2, T])
        consts_in = s.sem("consts_in")
        summed, centred, squared, var, root, chain, normed, done = (
            s.sem(n) for n in ("summed", "centred", "squared", "var", "root", "chain", "normed", "done"))
        with s.block() as block:

            @block.sync
            def _(sp):
                sp.dma_start(gam[:], a["conf_ln_g"]).then_inc(consts_in, 16)
                sp.dma_start(bet[:], a["conf_ln_b"]).then_inc(consts_in, 16)

            @block.tensor
            def _(pe):
                for i in range(KD):
                    mm = pe.matmul(tot[:, 0, :], c.ones[:], c.yT[:, KD + i, :], start=(i == 0), stop=(i == KD - 1))
                mm.then_inc(summed, 1)
                for i in range(KD):
                    pe.wait_ge(squared, i + 1)
                    mm = pe.matmul(tot[:, 1, :], c.ones[:], sq[:, i, :], start=(i == 0), stop=(i == KD - 1))
                mm.then_inc(summed, 1)

            @block.vector
            def _(dve):
                step = chained(dve, chain)
                dve.wait_ge(summed, 1)
                for i in range(KD):
                    y = c.yT[:, KD + i, :]
                    dve.scalar_tensor_tensor(out=y, in0=tot[:, 0, :], scalar=-1.0 / D, in1=y,
                                             op0=ALU.mult, op1=ALU.add).then_inc(centred, 1)
                dve.wait_ge(summed, 2)
                dve.tensor_scalar(rstd[:], tot[:, 1, :], 1.0 / D, EPS, ALU.mult, ALU.add).then_inc(var, 1)
                dve.wait_ge(root, 1)
                step(dve.reciprocal(rstd[:], rstd[:]))
                for i in range(KD):
                    y = c.yT[:, KD + i, :]
                    dve.tensor_tensor(y, y, rstd[:], ALU.mult).then_inc(normed, 1)

            @block.scalar
            def _(act):
                for i in range(KD):
                    act.wait_ge(centred, i + 1)
                    act.activation(sq[:, i, :], c.yT[:, KD + i, :], ACT.Square).then_inc(squared, 1)
                act.wait_ge(var, 1)
                act.activation(rstd[:], rstd[:], ACT.Sqrt).then_inc(root, 1)
                act.wait_ge(consts_in, 32)
                for i in range(KD):
                    act.wait_ge(normed, i + 1)
                    y = c.yT[:, KD + i, :]
                    act.activation(y, y, ACT.Silu, scale=gam[:, i:i + 1], bias=bet[:, i:i + 1]).then_inc(done, 1)


def stage_ssd(nc, c, a):
    CH = M + 1
    with Stage(nc, "ssd") as s:
        alog = s.sb("alog", [P, HEADS])
        dsk = s.sb("dsk", [P, KD])
        nw = s.sb("nw", [P, KD])
        acs = s.sb("acs", [P, CH, HEADS])
        keep = s.sb("keep", [P, CH, HEADS])
        dec = s.sb("dec", [P, CH, HEADS])
        xdt = s.sb("xdt", [P, HEADS, 64])
        xw = s.sb("xw", [P, HEADS, 64])
        btok = s.sb("btok", [P, GROUPS, P])
        state = s.sb("state", [P, HEADS, 64])
        lmat = s.sb("lmat", [P, 2, 4, P])
        cw = s.sb("cw", [P, 2, 4, P])
        cbm = s.sb("cbm", [P, 2, P])
        sq = s.sb("sq", [P, KD, T])
        rstd = s.sb("rstd", [P, GROUPS, T])
        X = s.ps("X", [P, 2, 512])
        A_ = s.ps("A", [P, 512])
        R = s.ps("R", [P, 2, 4, P])
        CB = s.ps("CB", [P, 4, P])
        Y = s.ps("Y", [P, 2, 512])
        consts_in = s.sem("consts_in")
        aneg, dta_ok, cs_done, cs_ok, w_exp, chain, dve_w = (
            s.sem(n) for n in ("aneg", "dta_ok", "cs_done", "cs_ok", "w_exp", "chain", "dve_w"))
        x_turned, b_turned, b_taken, xdt_ok, xw_ok = (
            s.sem(n) for n in ("x_turned", "b_turned", "b_taken", "xdt_ok", "xw_ok"))
        r_done, e_ok, e_exp, q_exp, w_ok = (s.sem(n) for n in ("r_done", "e_ok", "e_exp", "q_exp", "w_ok"))
        y_done, y_taken, st_done, s_ok = (s.sem(n) for n in ("y_done", "y_taken", "st_done", "s_ok"))
        squared, sums, var, root = (s.sem(n) for n in ("squared", "sums", "var", "root"))

        def cols(ch):
            return (0, META) if ch == 0 else (META + (ch - 1) * P, P)

        with s.block() as block:

            @block.sync
            def _(sp):
                sp.dma_start(alog[:], a["ssd_A_log"].to_broadcast([P, HEADS])).then_inc(consts_in, 16)
                sp.dma_start(dsk[:], a["ssd_D"]).then_inc(consts_in, 16)
                sp.dma_start(nw[:], a["ssd_norm_w"]).then_inc(consts_in, 16)

            @block.tensor
            def _(pe):
                pe.wait_ge(dta_ok, 1)
                dta = c.dta[:].rearrange("p c h -> p (c h)")
                pe.matmul(A_[:, 0:CH * HEADS], c.upper[:], dta, start=True, stop=True)
                pe.matmul(A_[:, 128:128 + CH * HEADS], c.ones[:], dta, start=True, stop=True).then_inc(cs_done, 1)

                def turn(ch):
                    at, n = cols(ch)
                    if ch > 0:
                        pe.wait_ge(s_ok, ch)
                    for h in range(2):
                        for k in range(4):
                            t = pe.transpose(X[0:n, h, k * P:(k + 1) * P], c.xbcT[:, 4 * h + k, at:at + n], c.ident[:])
                        t.then_inc(x_turned, 1)
                    if ch == M:
                        return
                    pe.wait_ge(cs_ok, 1) if ch == 0 else pe.wait_ge(b_taken, ch)
                    for g in range(GROUPS):
                        t = pe.transpose(A_[0:n, g * P:(g + 1) * P], c.xbcT[:, XT + g, at:at + n], c.ident[:])
                    t.then_inc(b_turned, 1)

                def new_state(ch):
                    n = cols(ch)[1]
                    pe.wait_ge(xw_ok, ch + 1)
                    pe.wait_ge(b_taken, ch + 1)
                    for g in range(GROUPS):
                        mm = pe.matmul(X[:, g // 2, (g % 2) * 256:(g % 2) * 256 + 256], btok[0:n, g, :],
                                       xw[0:n, 4 * g:4 * g + 4, :].rearrange("p h d -> p (h d)"), start=True, stop=True)
                    mm.then_inc(st_done, 1)

                def decays(n):
                    ch, g = n // 4 + 1, n % 4
                    at, _ = cols(ch)
                    if n >= 2:
                        pe.wait_ge(e_ok, n - 1)
                        pe.wait_ge(q_exp, n - 1)
                        pe.wait_ge(w_ok, n - 1)
                    for r in range(4):
                        pe.matmul(R[:, n % 2, r, :], c.dta[:, ch, 4 * g + r:4 * g + r + 1].to_broadcast([P, P]),
                                  c.upper[:], start=True, stop=True)
                    if n >= 1:
                        pe.wait_ge(dve_w, n)
                    pe.matmul(CB[:, n % 2, :], c.xbcT[:, XT + g, at:at + P], c.xbcT[:, XT + 4 + g, at:at + P],
                              start=True, stop=True).then_inc(r_done, 1)

                turn(0)
                new_state(0)
                turn(1)
                decays(0)
                for n in range(16):
                    ch, g = n // 4 + 1, n % 4
                    if n + 1 < 16:
                        decays(n + 1)
                    pe.wait_ge(w_ok, n + 1)
                    pe.wait_ge(xdt_ok, ch + 1)
                    pe.wait_ge(s_ok, ch)
                    if n >= 2:
                        pe.wait_ge(y_taken, n - 1)
                    for r in range(4):
                        h = 4 * g + r
                        out = Y[64 * (r % 2):64 * (r % 2) + 64, n % 2, (r // 2) * P:(r // 2) * P + P]
                        pe.matmul(out, xdt[:, h, :], lmat[:, n % 2, r, :], start=True, stop=False)
                        mm = pe.matmul(out, state[:, h, :], cw[:, n % 2, r, :], start=False, stop=True)
                    mm.then_inc(y_done, 1)
                    if g == 3 and ch < M:
                        new_state(ch)
                        turn(ch + 1)
                for g in range(GROUPS):
                    pe.wait_ge(squared, g + 1)
                    pe.wait_ge(y_taken, 16)
                    if g >= 2:
                        pe.wait_ge(var, g - 1)
                    for k in range(2):
                        mm = pe.matmul(Y[:, g % 2, :], c.ones[:], sq[:, 2 * g + k, :], start=(k == 0), stop=(k == 1))
                    mm.then_inc(sums, 1)

            @block.scalar
            def _(act):
                act.wait_ge(consts_in, 48)
                act.activation(alog[:], alog[:], ACT.Exp).then_inc(aneg, 1)
                act.wait_ge(cs_ok, 2)
                act.activation(keep[:], keep[:], ACT.Exp).then_inc(w_exp, 1)
                act.activation(dec[:], dec[:], ACT.Exp).then_inc(w_exp, 1)

                def take_b(ch):
                    n = cols(ch)[1]
                    act.wait_ge(b_turned, ch + 1)
                    act.activation(btok[0:n, :, :], A_[0:n, :].rearrange("p (g n) -> p g n", g=GROUPS),
                                   ACT.Copy).then_inc(b_taken, 1)

                take_b(0)
                take_b(1)
                for n in range(16):
                    act.wait_ge(r_done, n + 1)
                    if n >= 2:
                        act.wait_ge(y_done, n - 1)
                    act.activation(cw[:, n % 2, :, :], R[:, n % 2, :, :], ACT.Exp).then_inc(q_exp, 1)
                    act.wait_ge(e_ok, n + 1)
                    act.activation(lmat[:, n % 2, :, :], lmat[:, n % 2, :, :], ACT.Exp).then_inc(e_exp, 1)
                    if n % 4 == 0 and 1 < n // 4 + 1 < M:
                        take_b(n // 4 + 1)
                for g in range(GROUPS):
                    act.wait_ge(y_taken, 16)
                    act.activation(sq[:, 2 * g:2 * g + 2, :], c.yT[:, 2 * g:2 * g + 2, :], ACT.Square).then_inc(squared, 1)
                act.wait_ge(var, GROUPS)
                act.activation(rstd[:], rstd[:], ACT.Sqrt).then_inc(root, 1)

            @block.vector
            def _(dve):
                step = chained(dve, chain)
                dve.wait_ge(aneg, 1)
                dve.scalar_tensor_tensor(out=c.dta[:], in0=c.dt[:], scalar=-1.0,
                                         in1=alog[:].unsqueeze(1).to_broadcast([P, CH, HEADS]),
                                         op0=ALU.mult, op1=ALU.mult).then_inc(dta_ok, 1)
                dve.wait_ge(cs_done, 1)
                n_ = CH * HEADS
                step(dve.tensor_copy(acs[:].rearrange("p c h -> p (c h)"), A_[:, 0:n_]))
                step(dve.tensor_copy(dec[:].rearrange("p c h -> p (c h)"), A_[:, 128:128 + n_]))
                dve.tensor_tensor(keep[:], dec[:], acs[:], ALU.subtract).then_inc(cs_ok, 2)
                dve.wait_ge(w_exp, 2)

                def take_x(ch):
                    n = cols(ch)[1]
                    for h in range(2):
                        dve.wait_ge(x_turned, 2 * ch + h + 1)
                        ins = dve.tensor_tensor(xdt[0:n, 8 * h:8 * h + 8, :],
                                                X[0:n, h, :].rearrange("p (h d) -> p h d", h=8),
                                                c.dt[0:n, ch, 8 * h:8 * h + 8].unsqueeze(2).to_broadcast([n, 8, 64]), ALU.mult)
                        if h == 0:
                            step(ins)
                    ins.then_inc(xdt_ok, 1)
                    dve.wait_ge(xdt_ok, ch + 1)
                    dve.tensor_tensor(xw[0:n, :, :], xdt[0:n, :, :],
                                      keep[0:n, ch, :].unsqueeze(2).to_broadcast([n, HEADS, 64]), ALU.mult).then_inc(xw_ok, 1)

                def take_state(ch):
                    dve.wait_ge(st_done, ch + 1)
                    new = X[:].rearrange("p b (h d) -> p (b h) d", d=64)
                    if ch == 0:
                        dve.tensor_copy(state[:], new).then_inc(s_ok, 1)
                        return
                    step(dve.tensor_tensor(state[:], state[:], dec[:, ch, :].unsqueeze(2).to_broadcast([P, HEADS, 64]),
                                           ALU.mult))
                    dve.tensor_tensor(state[:], state[:], new, ALU.add).then_inc(s_ok, 1)

                def prepare(n):
                    ch, g = n // 4 + 1, n % 4
                    at, _ = cols(ch)
                    dve.wait_ge(r_done, n + 1)
                    if n >= 2:
                        dve.wait_ge(y_done, n - 1)
                    dve.tensor_tensor(cbm[:, n % 2, :], CB[:, n % 2, :], c.upper[:], ALU.mult).then_inc(dve_w, 1)
                    dve.wait_ge(q_exp, n + 1)
                    for r in range(4):
                        h = 4 * g + r
                        ins = dve.tensor_scalar(lmat[:, n % 2, r, :], R[:, n % 2, r, :], acs[:, ch, h:h + 1], 0.0,
                                                ALU.subtract, ALU.min)
                    ins.then_inc(e_ok, 1)
                    dve.tensor_tensor(cw[:, n % 2, :, :], cw[:, n % 2, :, :],
                                      c.xbcT[:, XT + 4 + g, at:at + P].unsqueeze(1).to_broadcast([P, 4, P]), ALU.mult)
                    dve.wait_ge(e_exp, n + 1)
                    dve.wait_ge(dve_w, n + 1)
                    dve.tensor_tensor(lmat[:, n % 2, :, :], lmat[:, n % 2, :, :],
                                      cbm[:, n % 2, :].unsqueeze(1).to_broadcast([P, 4, P]), ALU.mult).then_inc(w_ok, 1)

                take_x(0)
                take_state(0)
                take_x(1)
                prepare(0)
                for n in range(16):
                    ch, g = n // 4 + 1, n % 4
                    at, _ = cols(ch)
                    if n + 1 < 16:
                        prepare(n + 1)
                    dve.wait_ge(y_done, n + 1)
                    for k in range(2):
                        j = 2 * g + k
                        ins = dve.scalar_tensor_tensor(out=c.yT[:, j, at - META:at - META + P],
                                                       in0=c.xbcT[:, j, at:at + P], scalar=dsk[:, j:j + 1],
                                                       in1=Y[:, n % 2, k * P:k * P + P], op0=ALU.mult, op1=ALU.add)
                    step(ins)
                    y = c.yT[:, 2 * g:2 * g + 2, at - META:at - META + P]
                    dve.tensor_tensor(y, y, c.zT[:, 2 * g:2 * g + 2, at - META:at - META + P],
                                      ALU.mult).then_inc(y_taken, 1)
                    if g == 3 and ch < M:
                        take_state(ch)
                        take_x(ch + 1)
                for g in range(GROUPS):
                    dve.wait_ge(sums, g + 1)
                    dve.tensor_scalar(rstd[:, g, :], Y[:, g % 2, :], 1.0 / 256, EPS, ALU.mult, ALU.add).then_inc(var, 1)
                dve.wait_ge(root, 1)
                step(dve.reciprocal(rstd[:], rstd[:]))
                for j in range(KD):
                    dve.scalar_tensor_tensor(out=c.yT[:, j, :], in0=c.yT[:, j, :], scalar=nw[:, j:j + 1],
                                             in1=rstd[:, j // 2, :], op0=ALU.mult, op1=ALU.mult).then_inc(chain, 1)


def stage_out_proj(nc, c, a, name, yT, w_dram, kt, resid, resid_scale, bias=None):
    RING = 4
    with Stage(nc, name) as s:
        w = s.sb("w", [P, RING, 2, D])
        res = s.sb("res", [P, M, D])
        acc = s.ps("acc", [P, M, 2, 512])
        bb = s.sb("bb", [P, D]) if bias is not None else None
        loaded = [s.sem(f"loaded{b}") for b in range(RING)]
        res_in, bias_in, used, done, chain = (s.sem(n) for n in ("res_in", "bias_in", "used", "done", "chain"))
        pairs = kt // 2
        with s.block() as block:

            @block.sync
            def _(sp):
                if resid is not None:
                    sp.dma_start(res[:], tokens(resid)).then_inc(res_in, 16)
                if bias is not None:
                    sp.dma_start(bb[:], bias.to_broadcast([P, D])).then_inc(bias_in, 16)
                for q in range(pairs):
                    if q >= RING:
                        sp.wait_ge(used, q - RING + 1)
                    sp.dma_start(w[:, q % RING, :, :], rows(w_dram)[:, 2 * q:2 * q + 2, :]).then_inc(loaded[q % RING], 16)

            @block.tensor
            def _(pe):
                for q in range(pairs):
                    pe.wait_ge(loaded[q % RING], 16 * (q // RING + 1))
                    for m in range(M):
                        for n in range(2):
                            for j in range(2):
                                k = 2 * q + j
                                mm = pe.matmul(acc[:, m, n, :], yT[:, k, m * P:m * P + P],
                                               w[:, q % RING, j, n * 512:n * 512 + 512],
                                               start=(k == 0), stop=(k == kt - 1))
                            if q == pairs - 1:
                                mm.then_inc(done, 1)
                    if q < pairs - 1:
                        mm.then_inc(used, 1)

            @block.vector
            def _(dve):
                step = chained(dve, chain)
                if resid is not None:
                    dve.wait_ge(res_in, 16)
                if bias is not None:
                    dve.wait_ge(bias_in, 16)
                for m in range(M):
                    for n in range(2):
                        dve.wait_ge(done, 2 * m + n + 1)
                        out = c.h[:, m, n * 512:n * 512 + 512]
                        old = (res if resid is not None else c.h)[:, m, n * 512:n * 512 + 512]
                        ins = dve.scalar_tensor_tensor(out=out, in0=old, scalar=resid_scale, in1=acc[:, m, n, :],
                                                       op0=ALU.mult, op1=ALU.add)
                        step(ins)
                        if bias is not None:
                            step(dve.tensor_tensor(out, out, bb[:, n * 512:n * 512 + 512], ALU.add))


def stage_token_norm(nc, c, a, name, dst, dstT=None, centre=False, norm=True, row_w=None, row_b=None, col_w=None,
                     save=None):
    src = c.h
    with Stage(nc, name) as s:
        junk = s.sb("junk", [P, 2, D])
        rw = s.sb("rw", [P, D]) if row_w is not None else None
        rb = s.sb("rb", [P, D]) if row_b is not None else None
        cwt = s.sb("cwt", [P, KD]) if col_w is not None else None
        stat = s.sb("stat", [P, 2, M])
        tp = s.ps("tp", [P, 4, 4, P])
        (w_in, summed, meaned, centred, squared, var, root, inv, scaled, turned, copied, saved, chain) = (
            s.sem(n) for n in ("w_in", "summed", "meaned", "centred", "squared", "var", "root", "inv", "scaled",
                               "turned", "copied", "saved", "chain"))
        n_w = 16 * sum(v is not None for v in (row_w, row_b, col_w))
        with s.block() as block:

            @block.sync
            def _(sp):
                if row_w is not None:
                    sp.dma_start(rw[:], row_w.to_broadcast([P, D])).then_inc(w_in, 16)
                if row_b is not None:
                    sp.dma_start(rb[:], row_b.to_broadcast([P, D])).then_inc(w_in, 16)
                if col_w is not None:
                    sp.dma_start(cwt[:], col_w).then_inc(w_in, 16)
                if save is not None:
                    for m in range(M):
                        sp.wait_ge(scaled, m + 1)
                        sp.dma_start(tokens(save)[:, m, :], dst[:, m, :]).then_inc(saved, 16)
                    sp.wait_ge(saved, 16 * M)

            @block.scalar
            def _(act):
                if not norm:
                    return
                if centre:
                    for m in range(M):
                        act.activation(junk[:, m % 2, :], src[:, m, :], ACT.Copy, accum_out=stat[:, 0, m:m + 1]).then_inc(summed, 1)
                        act.wait_ge(summed, m + 1)
                for m in range(M):
                    if centre:
                        act.wait_ge(centred, m + 1)
                    act.activation(junk[:, m % 2, :], dst[:, m, :] if centre else src[:, m, :], ACT.Square,
                                   accum_out=stat[:, 1, m:m + 1]).then_inc(squared, 1)
                    act.wait_ge(squared, m + 1)
                act.wait_ge(var, 1)
                act.activation(stat[:, 1, :], stat[:, 1, :], ACT.Sqrt).then_inc(root, 1)

            @block.vector
            def _(dve):
                step = chained(dve, chain)
                if norm:
                    if centre:
                        dve.wait_ge(summed, M)
                        step(dve.tensor_scalar(stat[:, 0, :], stat[:, 0, :], 1.0 / D, None, ALU.mult))
                        for m in range(M):
                            dve.tensor_scalar(dst[:, m, :], src[:, m, :], stat[:, 0, m:m + 1], None,
                                              ALU.subtract).then_inc(centred, 1)
                    dve.wait_ge(squared, M)
                    dve.tensor_scalar(stat[:, 1, :], stat[:, 1, :], 1.0 / D, EPS, ALU.mult, ALU.add).then_inc(var, 1)
                    dve.wait_ge(root, 1)
                    step(dve.reciprocal(stat[:, 1, :], stat[:, 1, :]))
                if n_w:
                    dve.wait_ge(w_in, n_w)
                for m in range(M if norm else 0):
                    x = (dst if centre else src)[:, m, :]
                    if rw is None:
                        dve.tensor_scalar(dst[:, m, :], x, stat[:, 1, m:m + 1], None, ALU.mult).then_inc(scaled, 1)
                    else:
                        ins = dve.scalar_tensor_tensor(out=dst[:, m, :], in0=x, scalar=stat[:, 1, m:m + 1], in1=rw[:],
                                                       op0=ALU.mult, op1=ALU.mult)
                        if rb is not None:
                            step(ins)
                            ins = dve.tensor_tensor(dst[:, m, :], dst[:, m, :], rb[:], ALU.add)
                        ins.then_inc(scaled, 1)
                if dstT is None:
                    return
                for i in range(2 * M):
                    m, h = i // 2, i % 2
                    dve.wait_ge(turned, i + 1)
                    out = dstT[:, 4 * h:4 * h + 4, m * P:m * P + P]
                    if cwt is not None:
                        ins = dve.tensor_tensor(out, tp[:, i % 4, :, :],
                                                cwt[:, 4 * h:4 * h + 4].unsqueeze(2).to_broadcast([P, 4, P]), ALU.mult)
                    else:
                        ins = dve.tensor_copy(out, tp[:, i % 4, :, :])
                    ins.then_inc(copied, 1)

            @block.tensor
            def _(pe):
                if dstT is None:
                    return
                for i in range(2 * M):
                    m, h = i // 2, i % 2
                    if h == 0 and norm:
                        pe.wait_ge(scaled, m + 1)
                    if i >= 4:
                        pe.wait_ge(copied, i - 3)
                    for k in range(4):
                        t = pe.transpose(tp[:, i % 4, k, :], dst[:, m, (4 * h + k) * P:(4 * h + k + 1) * P], c.ident[:])
                    t.then_inc(turned, 1)


def stage_peer_scores(nc, c, a):
    NQ = 2 * PH
    with Stage(nc, "score") as s:
        w = s.sb("w", [P, 2, KD, 512])
        qT = s.sb("qT", [P, NQ, T])
        keysT = s.sb("keysT", [P, NQ, NK])
        S = s.sb("S", [P, 2, NQ, NK])
        v = s.sb("v", [P, NQ, TOPK])
        iu = s.sb("iu", [P, NQ, TOPK], U32)
        fi = s.sb("fi", [P, NQ, TOPK])
        cand = s.sb("cand", [P, PH, TOPK * TOPK])
        best = s.sb("best", [P, PH, TOPK])
        pos = s.sb("pos", [P, PH, TOPK], U32)
        hi = s.sb("hi", [P, PH, TOPK], U32)
        posf = s.sb("posf", [P, 2, PH, TOPK])
        gate = s.sb("gate", [P, PH, TOPK])
        total = s.sb("total", [P, PH])
        eq = s.sb("eq", [P, PH, TOPK, TOPK])
        pick = s.sb("pick", [P, 3, PH * TOPK])
        q_ps = s.ps("q_ps", [P, 2, 512])
        s_ps = s.ps("s_ps", [P, 4, 4, NK])
        t_ps = s.ps("t_ps", [P, 4, P])
        w_in = [s.sem(f"w_in{b}") for b in range(2)]
        (keys_in, q_done, q_taken, s_done, s_taken, s_used, chain, centred, exped, picks, turned, copied) = (
            s.sem(n) for n in ("keys_in", "q_done", "q_taken", "s_done", "s_taken", "s_used", "chain", "centred",
                               "exped", "picks", "turned", "copied"))
        wq = rows(a["peer_w_query"][0])
        LOW = -3.0e38
        with s.block() as block:

            @block.sync
            def _(sp):
                sp.dma_start(keysT[:], a["peer_keysT"]).then_inc(keys_in, 16)
                for n in range(4):
                    if n >= 2:
                        sp.wait_ge(q_done, 4 * (n - 1))
                    sp.dma_start(w[:, n % 2, :, :], wq[:, :, n * 512:n * 512 + 512]).then_inc(w_in[n % 2], 16)

            @block.tensor
            def _(pe):
                for n in range(NQ):
                    if n % 4 == 0:
                        pe.wait_ge(w_in[n // 4 % 2], 16 * (n // 8 + 1))
                    if n >= 2:
                        pe.wait_ge(q_taken, n - 1)
                    for k in range(KD):
                        mm = pe.matmul(q_ps[:, n % 2, :], w[:, n // 4 % 2, k, (n % 4) * P:(n % 4) * P + P], c.hT[:, k, :],
                                       start=(k == 0), stop=(k == KD - 1))
                    mm.then_inc(q_done, 1)
                pe.wait_ge(q_taken, NQ)
                pe.wait_ge(keys_in, 16)

                def scores(m):
                    for b in range(4):
                        if m >= 1:
                            pe.wait_ge(s_taken, 4 * (m - 1) + b + 1)
                        for j in range(4):
                            n = 4 * b + j
                            mm = pe.matmul(s_ps[:, b, j, :], qT[:, n, m * P:m * P + P], keysT[:, n, :],
                                           start=True, stop=True)
                        mm.then_inc(s_done, 1)

                scores(0)
                scores(1)
                for m in range(M):
                    pe.wait_ge(picks, m + 1)
                    if m >= 1:
                        pe.wait_ge(copied, m)
                    for j in range(3):
                        t = pe.transpose(t_ps[:, j, :], pick[:, j, :], c.ident[:])
                    t.then_inc(turned, 1)
                    if m + 2 < M:
                        scores(m + 2)

            @block.scalar
            def _(act):
                for n in range(NQ):
                    act.wait_ge(q_done, n + 1)
                    act.activation(qT[:, n, :], q_ps[:, n % 2, :], ACT.Copy).then_inc(q_taken, 1)

                def take(m):
                    if m >= 2:
                        act.wait_ge(s_used, m - 1)
                    for b in range(4):
                        act.wait_ge(s_done, 4 * m + b + 1)
                        act.activation(S[:, m % 2, 4 * b:4 * b + 4, :], s_ps[:, b, :, :], ACT.Copy).then_inc(s_taken, 1)

                take(0)
                for m in range(M):
                    if m + 1 < M:
                        take(m + 1)
                    act.wait_ge(centred, m + 1)
                    act.activation(gate[:], gate[:], ACT.Exp).then_inc(exped, 1)
                    act.wait_ge(turned, m + 1)
                    act.activation(c.idxT[:, :, m * P:m * P + P], t_ps[:, 0:3, :], ACT.Copy).then_inc(copied, 1)

            @block.vector
            def _(dve):
                step = chained(dve, chain)

                def top16(values, vals, idx, n):
                    for half in range(2):
                        o = slice(8 * half, 8 * half + 8)
                        for r in range(n):
                            ins = dve.max(vals[:, r, o], values[:, r, :])
                        step(ins)
                        for r in range(n):
                            ins = dve.max_index(idx[:, r, o], vals[:, r, o], values[:, r, :])
                        step(ins)
                        if half == 0:
                            for r in range(n):
                                ins = dve.match_replace(out=values[:, r, :], in_to_replace=vals[:, r, o],
                                                        in_values=values[:, r, :], imm_value=LOW)
                            step(ins)

                for m in range(M):
                    dve.wait_ge(s_taken, 4 * m + 4)
                    top16(S[:, m % 2, :, :], v, iu, NQ)
                    dve.tensor_copy(fi[:], iu[:]).then_inc(s_used, 1)
                    dve.wait_ge(s_used, m + 1)
                    halves = v[:].rearrange("p (h two) k -> p h two k", two=2)
                    step(dve.tensor_tensor(cand[:].rearrange("p h (i j) -> p h i j", i=TOPK),
                                           halves[:, :, 0, :].unsqueeze(3).to_broadcast([P, PH, TOPK, TOPK]),
                                           halves[:, :, 1, :].unsqueeze(2).to_broadcast([P, PH, TOPK, TOPK]), ALU.add))
                    top16(cand, best, pos, PH)
                    dve.tensor_tensor(gate[:], best[:], best[:, :, 0:1].to_broadcast([P, PH, TOPK]),
                                      ALU.subtract).then_inc(centred, 1)
                    step(dve.tensor_scalar(hi[:], pos[:], 4, None, ALU.logical_shift_right))
                    step(dve.tensor_copy(posf[:, 0, :, :], hi[:]))
                    step(dve.tensor_scalar(hi[:], pos[:], 15, None, ALU.bitwise_and))
                    step(dve.tensor_copy(posf[:, 1, :, :], hi[:]))
                    fih = fi[:].rearrange("p (h two) k -> p h two k", two=2)
                    if m >= 1:
                        dve.wait_ge(turned, m)
                    for half in range(2):
                        step(dve.tensor_tensor(eq[:].rearrange("p h k i -> p (h k) i"),
                                               posf[:, half, :, :].rearrange("p h k -> p (h k)").unsqueeze(2).to_broadcast([P, PH * TOPK, TOPK]),
                                               c.count[:, 0:TOPK].unsqueeze(1).to_broadcast([P, PH * TOPK, TOPK]),
                                               ALU.is_equal))
                        step(dve.tensor_tensor(eq[:], eq[:],
                                               fih[:, :, half, :].unsqueeze(2).to_broadcast([P, PH, TOPK, TOPK]), ALU.mult))
                        step(dve.tensor_reduce(pick[:, half, :], eq[:].rearrange("p h k i -> p (h k) i"), AX.X, ALU.add))
                    dve.wait_ge(exped, m + 1)
                    step(dve.tensor_reduce(total[:], gate[:], AX.X, ALU.add))
                    step(dve.reciprocal(total[:], total[:]))
                    dve.tensor_tensor(pick[:, 2, :].rearrange("p (h k) -> p h k", h=PH), gate[:],
                                      total[:].unsqueeze(2).to_broadcast([P, PH, TOPK]), ALU.mult).then_inc(picks, 1)
                    dve.wait_ge(picks, m + 1)


TB = 64
BATCHES = T // TB


def stage_gate_matrix(nc, c, a):
    U = 4
    with Stage(nc, "gates") as s:
        one = s.sb("one", [P, 2, U, NK])
        two = s.sb("two", [P, 2, U, NK])
        out = s.sb("out", [P, 2, NK, TB])
        ps = s.ps("ps", [P, 2, U, NK])
        (hot, used, g_done, taken) = (s.sem(n) for n in ("hot", "used", "g_done", "taken"))
        saved = [s.sem(f"saved{b}") for b in range(2)]
        per = TB // (2 * U)
        with s.block() as block:

            @block.vector
            def _(dve):
                with dve.Fori(0, T // (2 * U)) as it:
                    for u in range(2):
                        dve.wait_ge(g_done, it * 2 + (u + 1))
                        for j in range(U):
                            t = it * (2 * U) + (u * U + j)
                            dve.tensor_scalar(one[:, u, j, :], c.count[:], c.idxT[:, 0, ds(t, 1)], c.idxT[:, 2, ds(t, 1)],
                                              ALU.is_equal, ALU.mult)
                            ins = dve.tensor_scalar(two[:, u, j, :], c.count[:], c.idxT[:, 1, ds(t, 1)], None, ALU.is_equal)
                        ins.then_inc(hot, 1)

            @block.tensor
            def _(pe):
                pe.sem_inc(g_done, 2)
                with pe.Fori(0, T // (2 * U)) as it:
                    for u in range(2):
                        pe.wait_ge(hot, it * 2 + (u + 1))
                        pe.wait_ge(taken, it * 2 + (u + 1))
                        for j in range(U):
                            mm = pe.matmul(ps[:, u, j, :], two[:, u, j, :], one[:, u, j, :], start=True, stop=True)
                        mm.then_inc(g_done, 1)

            @block.scalar
            def _(act):
                act.sem_inc(taken, 2)
                for b in range(BATCHES):
                    if b >= 2:
                        act.wait_ge(saved[b % 2], 16 * (b // 2))
                    with act.Fori(0, per) as q:
                        for u in range(2):
                            act.wait_ge(g_done, q * 2 + (2 * per * b + u + 3))
                            act.activation(out[:, b % 2, :, ds(q * (2 * U) + u * U, U)],
                                           ps[:, u, :, :].rearrange("p t i -> p i t"), ACT.Copy).then_inc(taken, 1)

            @block.sync
            def _(sp):
                for b in range(BATCHES):
                    sp.wait_ge(taken, 2 * per * (b + 1) + 2)
                    sp.dma_start(c.gates[b], out[:, b % 2, :, :].rearrange("p i t -> p (i t)")).then_inc(saved[b % 2], 16)
                for b in range(2):
                    sp.wait_ge(saved[b], 16 * (BATCHES // 2))


def stage_peer_experts(nc, c, a):
    G = 4
    N = NK // G
    wd_d = rows(a["peer_w_downT"])
    wu_d = a["peer_w_up"][0].rearrange("(k p) n -> p k n", p=P)
    g_d = c.gates.rearrange("b p (i t) -> p b i t", t=TB)
    with Stage(nc, "experts") as s:
        wd = s.sb("wd", [P, KD, G * P])
        wd_hi = s.sb("wd_hi", [P, KD, G * P], F32R)
        wd_lo = s.sb("wd_lo", [P, KD, G * P], F32R)
        wu = s.sb("wu", [P, G, D])
        wu_hi = s.sb("wu_hi", [P, G, D], F32R)
        wu_lo = s.sb("wu_lo", [P, G, D], F32R)
        gt = s.sb("gt", [P, BATCHES, G * TB])
        hid = s.sb("hid", [P, G, T])
        hid_hi = s.sb("hid_hi", [P, G, T], F32R)
        hid_lo = s.sb("hid_lo", [P, G, T], F32R)
        H = s.ps("H", [P, G, T])
        Y = s.ps("Y", [P, 4, 512])
        (wd_in, wu_in, gt_in, wd_h, wd_l, wu_h, wu_l, h_done, gelued, gated, hid_h, hid_l, y_done, added) = (
            s.sem(n) for n in ("wd_in", "wu_in", "gt_in", "wd_h", "wd_l", "wu_h", "wu_l", "h_done", "gelued",
                               "gated", "hid_h", "hid_l", "y_done", "added"))

        def tile(w, j):
            return w[:, :, j * P:(j + 1) * P]

        with s.block() as block:

            @block.sync
            def _(sp):
                def load_wd(e0):
                    sp.dma_start(wd[:], wd_d[:, :, ds(e0, G * P)]).then_inc(wd_in, 16)

                def load_gt(k0):
                    sp.dma_start(gt[:].rearrange("p b (i t) -> p b i t", t=TB), g_d[:, :, ds(k0, G), :]).then_inc(gt_in, 16)

                def load_wu(k0):
                    sp.dma_start(wu[:], wu_d[:, ds(k0, G), :]).then_inc(wu_in, 16)

                load_wd(0)
                load_gt(0)
                load_wu(0)
                with sp.Fori(0, N - 1) as it:
                    e0 = sp.snap(it * (G * P) + G * P)
                    k0 = sp.snap(it * G + G)
                    sp.wait_ge(wd_l, it * G + G)
                    load_wd(e0)
                    sp.wait_ge(gated, it * G + G)
                    load_gt(k0)
                    sp.wait_ge(wu_l, it * G + G)
                    load_wu(k0)

            @block.tensor
            def _(pe):
                with pe.Fori(0, N) as it:
                    for j in range(G):
                        pe.wait_ge(wd_h, it * G + (j + 1))
                        pe.wait_ge(wd_l, it * G + (j + 1))
                        for k in range(KD):
                            hi, lo = tile(wd_hi, j)[:, k, :], tile(wd_lo, j)[:, k, :]
                            pe.matmul(H[:, j, :], hi, c.x_hi[:, k, :], start=(k == 0), stop=False)
                            pe.matmul(H[:, j, :], hi, c.x_lo[:, k, :], start=False, stop=False)
                            mm = pe.matmul(H[:, j, :], lo, c.x_hi[:, k, :], start=False, stop=(k == KD - 1))
                        mm.then_inc(h_done, 1)
                    pe.wait_ge(added, it * 8 + 1)
                    for y in range(8):
                        m, n = y // 2, y % 2
                        if y >= 4:
                            pe.wait_ge(added, it * 8 + (y - 2))
                        for j in range(G):
                            if y == 0:
                                pe.wait_ge(wu_l, it * G + (j + 1))
                                pe.wait_ge(hid_l, it * G + (j + 1))
                            hi, lo = hid_hi[:, j, m * P:m * P + P], hid_lo[:, j, m * P:m * P + P]
                            w = slice(n * 512, n * 512 + 512)
                            pe.matmul(Y[:, y % 4, :], hi, wu_hi[:, j, w], start=(j == 0), stop=False)
                            pe.matmul(Y[:, y % 4, :], hi, wu_lo[:, j, w], start=False, stop=False)
                            mm = pe.matmul(Y[:, y % 4, :], lo, wu_hi[:, j, w], start=False, stop=(j == G - 1))
                        mm.then_inc(y_done, 1)

            @block.scalar
            def _(act):
                def split_wd(nth, j):
                    act.wait_ge(wd_in, nth * 16 + 16)
                    act.activation(tile(wd_hi, j), tile(wd, j), ACT.Copy).then_inc(wd_h, 1)

                def group(it, last):
                    for j in range(G):
                        act.wait_ge(h_done, it * G + (j + 1))
                        act.activation(hid[:, j, :], H[:, j, :], ACT.Gelu).then_inc(gelued, 1)
                        act.wait_ge(wu_in, it * 16 + 16)
                        act.activation(wu_hi[:, j, :], wu[:, j, :], ACT.Copy).then_inc(wu_h, 1)
                        act.wait_ge(gated, it * G + (j + 1))
                        act.activation(hid_hi[:, j, :], hid[:, j, :], ACT.Copy).then_inc(hid_h, 1)
                    if not last:
                        for j in range(G):
                            split_wd(it + 1, j)

                for j in range(G):
                    split_wd(0, j)
                with act.Fori(0, N - 1) as it:
                    group(it, False)
                group(N - 1, True)

            @block.vector
            def _(dve):
                def split_wd(nth, j):
                    dve.wait_ge(wd_h, nth * G + (j + 1))
                    dve.tensor_tensor(tile(wd_lo, j), tile(wd, j), tile(wd_hi, j).bitcast(F32),
                                      ALU.subtract).then_inc(wd_l, 1)

                def group(it, last):
                    dve.wait_ge(gt_in, it * 16 + 16)
                    for j in range(G):
                        dve.wait_ge(gelued, it * G + (j + 1))
                        h = hid[:, j, :].rearrange("p (b t) -> p b t", b=BATCHES)
                        dve.tensor_tensor(h, h, gt[:, :, j * TB:(j + 1) * TB], ALU.mult).then_inc(gated, 1)
                        dve.wait_ge(wu_h, it * G + (j + 1))
                        dve.tensor_tensor(wu_lo[:, j, :], wu[:, j, :], wu_hi[:, j, :].bitcast(F32),
                                          ALU.subtract).then_inc(wu_l, 1)
                        dve.wait_ge(hid_h, it * G + (j + 1))
                        dve.tensor_tensor(hid_lo[:, j, :], hid[:, j, :], hid_hi[:, j, :].bitcast(F32),
                                          ALU.subtract).then_inc(hid_l, 1)
                    for y in range(8):
                        m, n = y // 2, y % 2
                        if y % 2 == 0 and not last:
                            split_wd(it + 1, y // 2)
                        dve.wait_ge(y_done, it * 8 + (y + 1))
                        out = c.h[:, m, n * 512:n * 512 + 512]
                        if y == 0:
                            dve.wait_ge(added, it * 8 + 1)
                        dve.tensor_tensor(out, out, Y[:, y % 4, :], ALU.add).then_inc(added, 1)

                dve.sem_inc(added, 1)
                for j in range(G):
                    split_wd(0, j)
                with dve.Fori(0, N - 1) as it:
                    group(it, False)
                group(N - 1, True)


def stage_split_x(nc, c):
    with Stage(nc, "splitx") as s:
        high, low = s.sem("high"), s.sem("low")
        with s.block() as block:

            @block.scalar
            def _(act):
                for k in range(KD):
                    act.activation(c.x_hi[:, k, :], c.hT[:, k, :], ACT.Copy).then_inc(high, 1)

            @block.vector
            def _(dve):
                for k in range(KD):
                    dve.wait_ge(high, k + 1)
                    dve.tensor_tensor(c.x_lo[:, k, :], c.hT[:, k, :], c.x_hi[:, k, :].bitcast(F32),
                                      ALU.subtract).then_inc(low, 1)


AH = 8
AJ = 4
GG = 8
ALPHA = 2.0 ** 0.25
NEG = -1e30
COL_K, COL_V, COL_U, COL_S = 512, 640, 768, 1280
EXPERTS = 32
EK = 4
BLOCKS = (T * EK) // P + EXPERTS - 1
NBLK = BLOCKS + 1
LIMIT, SWIGLU = 7.0, 1.702
ROWS = T * EK


def stage_project2(nc, c, a):
    w_d = rows(a["w_in_2"])
    with Stage(nc, "proj2") as s:
        w = s.sb("w", [P, KD, 1792])
        cb = s.sb("cb", [P, 14])
        rb = s.sb("rb", [P, P + 512])
        lg = s.sb("lg", [P, 512])
        lb = s.sb("lb", [P, 512])
        sq = s.sb("sq", [P, M, GG, 64])
        stat = s.sb("stat", [P, 2, M, GG])
        ps = s.ps("ps", [P, 8, 512])
        parts = ((COL_V, COL_U), (COL_S, 1792), (0, COL_V), (COL_U, COL_S))
        w_in = [s.sem(f"w_in{i}") for i in range(len(parts))]
        (cb_in, rb_in, done, taken, added, gelued, chain, root, var) = (
            s.sem(n) for n in ("cb_in", "rb_in", "done", "taken", "added", "gelued", "chain", "root", "var"))
        chans = [(c.qT[:, j, :], j) for j in range(AJ)] + [(c.kT[:], 4)] + [(c.uT2[:, j, :], 6 + j) for j in range(4)]
        with s.block() as block:

            @block.sync
            def _(sp):
                sp.dma_start(rb[:], a["b_in_2_row"].to_broadcast([P, P + 512])).then_inc(rb_in, 16)
                for i, (lo, hi) in enumerate(parts):
                    sp.dma_start(w[:, :, lo:hi], w_d[:, :, lo:hi]).then_inc(w_in[i], 16)
                sp.dma_start(lg[:], a["ln_v_g_2"].to_broadcast([P, 512])).then_inc(rb_in, 16)
                sp.dma_start(lb[:], a["ln_v_b_2"].to_broadcast([P, 512])).then_inc(rb_in, 16)
                sp.dma_start(cb[:], a["b_in_2_col"]).then_inc(cb_in, 16)

            @block.tensor
            def _(pe):
                pe.wait_ge(w_in[0], 16)
                for m in range(M):
                    for k in range(KD):
                        mm = pe.matmul(ps[:, 4, m * P:m * P + P], c.hT[:, k, m * P:m * P + P], w[:, k, COL_V:COL_U],
                                       start=(k == 0), stop=(k == KD - 1))
                mm.then_inc(done, 1)
                pe.wait_ge(w_in[1], 16)
                for m in range(M):
                    for k in range(KD):
                        mm = pe.matmul(ps[:, m, :], c.hT[:, k, m * P:m * P + P], w[:, k, COL_S:1792],
                                       start=(k == 0), stop=(k == KD - 1))
                    mm.then_inc(done, 1)
                pe.wait_ge(w_in[2], 16)
                for i, (_, t) in enumerate(chans):
                    if i == 5:
                        pe.wait_ge(w_in[3], 16)
                    if i >= 3:
                        pe.wait_ge(taken, i - 2)
                    for k in range(KD):
                        mm = pe.matmul(ps[:, 5 + i % 3, :], w[:, k, t * P:t * P + P], c.hT[:, k, :],
                                       start=(k == 0), stop=(k == KD - 1))
                    mm.then_inc(done, 1)

            @block.scalar
            def _(act):
                for m in range(M):
                    act.wait_ge(added, m + 2)
                    act.activation(c.gtok[:, m, :], c.gtok[:, m, :], ACT.Gelu_apprx_tanh).then_inc(gelued, 1)
                act.wait_ge(cb_in, 16)
                for i, (out, t) in enumerate(chans):
                    act.wait_ge(done, 5 + i + 1)
                    act.activation(out, ps[:, 5 + i % 3, :], ACT.Identity if i < 5 else ACT.Gelu_apprx_tanh,
                                   bias=cb[:, t:t + 1]).then_inc(taken, 1)
                act.wait_ge(var, 1)
                act.activation(stat[:, 1, :, :], stat[:, 1, :, :], ACT.Sqrt).then_inc(root, 1)

            @block.vector
            def _(dve):
                step = chained(dve, chain)
                dve.wait_ge(rb_in, 48)
                dve.wait_ge(done, 1)
                dve.tensor_tensor(c.vtok[:], ps[:, 4, :].rearrange("p (m d) -> p m d", m=M),
                                  rb[:, 0:P].unsqueeze(1).to_broadcast([P, M, P]), ALU.add).then_inc(added, 1)
                for m in range(M):
                    dve.wait_ge(done, m + 2)
                    dve.tensor_tensor(c.gtok[:, m, :], ps[:, m, :], rb[:, P:P + 512], ALU.add).then_inc(added, 1)
                dve.wait_ge(gelued, M)
                g = c.gtok[:].rearrange("p m (g d) -> p m g d", g=GG)
                g3 = c.gtok[:].rearrange("p m (g d) -> p (m g) d", g=GG)
                sq3 = sq[:].rearrange("p m g d -> p (m g) d")
                mean, var_ = (stat[:, i, :, :].rearrange("p m g -> p (m g)") for i in range(2))
                step(dve.tensor_reduce(mean, g3, AX.X, ALU.add))
                step(dve.tensor_scalar(mean, mean, 1.0 / 64, None, ALU.mult))
                step(dve.tensor_tensor(g3, g3, mean.unsqueeze(2).to_broadcast([P, M * GG, 64]), ALU.subtract))
                step(dve.tensor_tensor(sq3, g3, g3, ALU.mult))
                step(dve.tensor_reduce(var_, sq3, AX.X, ALU.add))
                dve.tensor_scalar(var_, var_, 1.0 / 64, EPS, ALU.mult, ALU.add).then_inc(var, 1)
                dve.wait_ge(root, 1)
                step(dve.reciprocal(var_, var_))
                step(dve.tensor_tensor(g3, g3, var_.unsqueeze(2).to_broadcast([P, M * GG, 64]), ALU.mult))
                step(dve.tensor_tensor(c.gtok[:], c.gtok[:], lg[:].unsqueeze(1).to_broadcast([P, M, 512]), ALU.mult))
                step(dve.tensor_tensor(c.gtok[:], c.gtok[:], lb[:].unsqueeze(1).to_broadcast([P, M, 512]), ALU.add))


def stage_attention(nc, c, a):
    W2 = 2 * P
    with Stage(nc, "attn") as s:
        mask = s.sb("mask", [P, W2])
        sink = s.sb("sink", [P, 2, AJ])
        sc = s.sb("sc", [P, 2, 2, W2])
        top = s.sb("top", [P, 2, 2, 4])
        pT = s.sb("pT", [P, 2, 4, P])
        wsT = s.sb("wsT", [P, GG, P])
        bsb = s.sb("bsb", [P, 4, P])
        S = s.ps("S", [P, 2, 2, 512])
        X = s.ps("X", [P, 2, 4, P])
        O = s.ps("O", [P, 2, 512])
        (masked, sink_in, ws_in, bs_in, s_done, maxed, exped, probs, chain, turned, pt_ok, o_done, o_taken, s_read,
         g_done, g_taken, ws_ok) = (s.sem(n) for n in (
             "masked", "sink_in", "ws_in", "bs_in", "s_done", "maxed", "exped", "probs", "chain", "turned", "pt_ok",
             "o_done", "o_taken", "s_read", "g_done", "g_taken", "ws_ok"))
        PAIRS = M * AJ

        def span(n):
            return (P, P) if n == 0 else (0, W2)

        with s.block() as block:

            @block.sync
            def _(sp):
                sp.dma_start(sink[:], a["sinks_2"].to_broadcast([P, AH]).rearrange("p (t j) -> p t j", t=2)).then_inc(sink_in, 16)
                sp.dma_start(wsT[:], a["w_spatial_2T"]).then_inc(ws_in, 16)
                bs = a["b_spatial_2"][0].rearrange("(k two) t -> two k t", two=2)
                for two in range(2):
                    sp.dma_start(bsb[64 * two:64 * two + 64, :, :],
                                 bs[two:two + 1].to_broadcast([64, 4, P])).then_inc(bs_in, 16)

            @block.gpsimd
            def _(pool):
                pool.memset(mask[:], 0.0).then_inc(masked, 1)
                pool.wait_ge(masked, 1)
                pool.affine_select(out=mask[:, 0:P], in_=mask[:, 0:P], compare_op=ALU.is_gt, fill=NEG, base=0,
                                   pattern=[[1, P]], channel_multiplier=-1).then_inc(masked, 1)
                pool.affine_select(out=mask[:, P:W2], in_=mask[:, P:W2], compare_op=ALU.is_ge, fill=NEG, base=0,
                                   pattern=[[-1, P]], channel_multiplier=1).then_inc(masked, 1)
                pool.wait_ge(ws_in, 16)
                pool.affine_select(out=wsT[:], in_=wsT[:], compare_op=ALU.is_ge, fill=0.0, base=0,
                                   pattern=[[0, GG], [1, P]], channel_multiplier=-1).then_inc(ws_ok, 1)

            @block.tensor
            def _(pe):
                def scores(i):
                    n, j = i // AJ, i % AJ
                    lo, width = span(n)
                    if i >= 2:
                        pe.wait_ge(s_read, i - 1)
                    for t in range(2):
                        h = slice(64 * t, 64 * t + 64)
                        mm = pe.matmul(S[:, i % 2, t, lo:lo + width], c.qT[h, j, n * P:n * P + P],
                                       c.kT[h, (n - 1) * P + lo:(n - 1) * P + lo + width], start=True, stop=True)
                    mm.then_inc(s_done, 1)

                def turn(i):
                    n = i // AJ
                    pe.wait_ge(probs, i + 1)
                    if i >= 2:
                        pe.wait_ge(pt_ok, i - 1)
                    for t in range(2):
                        for b in range(2):
                            if n > 0 or b == 1:
                                x = pe.transpose(X[:, i % 2, 2 * t + b, :], sc[:, i % 2, t, b * P:b * P + P], c.ident[:])
                    x.then_inc(turned, 1)

                def values(i):
                    n, j = i // AJ, i % AJ
                    pe.wait_ge(pt_ok, i + 1)
                    if i >= 2:
                        pe.wait_ge(o_taken, i - 1)
                    for t in range(2):
                        for b in range(2):
                            if n > 0 or b == 1:
                                mm = pe.matmul(O[64 * t:64 * t + 64, i % 2, 0:P], c.vtok[:, n - 1 + b, 64 * t:64 * t + 64],
                                               pT[:, i % 2, 2 * t + b, :], start=(b == 0 or n == 0), stop=(b == 1))
                    mm.then_inc(o_done, 1)

                scores(0)
                for i in range(PAIRS):
                    if i + 1 < PAIRS:
                        scores(i + 1)
                    turn(i)
                    if i >= 1:
                        values(i - 1)
                values(PAIRS - 1)
                pe.wait_ge(ws_ok, 1)
                for n in range(M):
                    if n >= 2:
                        pe.wait_ge(g_taken, n - 1)
                    else:
                        pe.wait_ge(pt_ok, PAIRS)
                    for g in range(GG):
                        mm = pe.matmul(X[64 * (g % 2):64 * (g % 2) + 64, n % 2, g // 2, :],
                                       c.gtok[:, n, 64 * g:64 * g + 64], wsT[:, g, :], start=True, stop=True)
                    mm.then_inc(g_done, 1)

            @block.scalar
            def _(act):
                def exps(i):
                    lo, width = span(i // AJ)
                    b = i % 2
                    act.wait_ge(maxed, i + 1)
                    for t in range(2):
                        act.activation(sc[:, b, t, lo:lo + width], sc[:, b, t, lo:lo + width], ACT.Exp,
                                       bias=top[:, b, t, 0:1], accum_out=top[:, b, t, 2:3])
                        ins = act.activation(top[:, b, t, 1:2], sink[:, t, i % AJ:i % AJ + 1], ACT.Exp, bias=top[:, b, t, 0:1])
                    ins.then_inc(exped, 1)

                def copies(i):
                    act.wait_ge(turned, i + 1)
                    if i >= 2:
                        act.wait_ge(o_done, i - 1)
                    if i < AJ:
                        act.activation(pT[:, i % 2, 1:4:2, :], X[:, i % 2, 1:4:2, :], ACT.Copy).then_inc(pt_ok, 1)
                    else:
                        act.activation(pT[:, i % 2, :, :], X[:, i % 2, :, :], ACT.Copy).then_inc(pt_ok, 1)

                def outs(i):
                    n, j = i // AJ, i % AJ
                    act.wait_ge(o_done, i + 1)
                    act.activation(c.mixT[:, j, n * P:n * P + P], O[:, i % 2, 0:P], ACT.Copy).then_inc(o_taken, 1)

                act.wait_ge(sink_in, 16)
                exps(0)
                for i in range(PAIRS):
                    copies(i)
                    if i + 1 < PAIRS:
                        exps(i + 1)
                    if i >= 1:
                        outs(i - 1)
                outs(PAIRS - 1)

            @block.vector
            def _(dve):
                step = chained(dve, chain)

                def maxes(i):
                    n, j, b = i // AJ, i % AJ, i % 2
                    lo, width = span(n)
                    dve.wait_ge(s_done, i + 1)
                    if i >= 2:
                        dve.wait_ge(turned, i - 1)
                    x = sc[:, b, :, lo:lo + width]
                    dve.scalar_tensor_tensor(out=x, in0=S[:, b, :, lo:lo + width], scalar=64 ** -0.5,
                                             in1=mask[:, lo:lo + width].unsqueeze(1).to_broadcast([P, 2, width]),
                                             op0=ALU.mult, op1=ALU.add).then_inc(s_read, 1)
                    dve.wait_ge(s_read, i + 1)
                    step(dve.tensor_reduce(top[:, b, :, 3], x, AX.X, ALU.max))
                    step(dve.tensor_tensor(top[:, b, :, 3], top[:, b, :, 3], sink[:, :, j], ALU.max))
                    dve.tensor_scalar(top[:, b, :, 0], top[:, b, :, 3], -1.0, None, ALU.mult).then_inc(maxed, 1)

                def norms(i):
                    b = i % 2
                    lo, width = span(i // AJ)
                    dve.wait_ge(exped, i + 1)
                    step(dve.tensor_tensor(top[:, b, :, 3], top[:, b, :, 1], top[:, b, :, 2], ALU.add))
                    step(dve.reciprocal(top[:, b, :, 3], top[:, b, :, 3]))
                    for t in range(2):
                        ins = dve.tensor_scalar(sc[:, b, t, lo:lo + width], sc[:, b, t, lo:lo + width],
                                                top[:, b, t, 3:4], None, ALU.mult)
                    ins.then_inc(probs, 1)

                dve.wait_ge(sink_in, 16)
                dve.wait_ge(masked, 3)
                maxes(0)
                for i in range(PAIRS):
                    if i + 1 < PAIRS:
                        maxes(i + 1)
                    norms(i)
                dve.wait_ge(bs_in, 32)
                for n in range(M):
                    dve.wait_ge(g_done, n + 1)
                    out = c.mixT[:, AJ:, n * P:n * P + P]
                    dve.tensor_tensor(out, X[:, n % 2, :, :], bsb[:], ALU.add).then_inc(g_taken, 1)
                    dve.wait_ge(g_taken, n + 1)
                    step(dve.tensor_tensor(out, out, c.uT2[:, :, n * P:n * P + P], ALU.mult))


def stage_route(nc, c, a):
    ME = [P, M, EXPERTS]
    with Stage(nc, "route") as s:
        wr = s.sb("wr", [P, KD, EXPERTS])
        br = s.sb("br", [P, EXPERTS])
        bd = s.sb("bd", [EXPERTS, D])
        logit = s.sb("logit", ME)
        v8 = s.sb("v8", [P, M, 8])
        i8 = s.sb("i8", [P, M, 8], U32)
        i4 = s.sb("i4", [P, M, EK])
        gate = s.sb("gate", [P, M, EK])
        tot = s.sb("tot", [P, M])
        hot = s.sb("hot", [P, M * EK, EXPERTS])
        hg = s.sb("hg", [P, M * EK, EXPERTS])
        mem = s.sb("mem", ME)
        ge = s.sb("ge", ME)
        rank = s.sb("rank", ME)
        over = s.sb("over", ME)
        tmp = s.sb("tmp", ME)
        cnt = s.sb("cnt", [P, EXPERTS])
        nb = s.sb("nb", [P, EXPERTS])
        t2 = s.sb("t2", [P, EXPERTS])
        onesE = s.sb("onesE", [P, EXPERTS])
        end = s.sb("end", [P, EXPERTS])
        start = s.sb("start", [P, EXPERTS])
        dest = s.sb("dest", [P, M * EK])
        desti = s.sb("desti", [P, M * EK], U32)
        entry = s.sb("entry", [P, M * EK, 4], I32)
        blank = s.sb("blank", [P, NBLK, 4], I32)
        ecmp = s.sb("ecmp", [1, NBLK, EXPERTS])
        ownf = s.sb("ownf", [1, NBLK])
        geT = s.sb("geT", [EXPERTS, M, P])
        ps = s.ps("ps", [P, 8, 512])
        wr_in, bd_in, br_in = s.sem("wr_in"), s.sem("bd_in"), s.sem("br_in")
        (l_done, shifted, exped, chain, mem_ok, cnt_done, ge_ok, turned, gt_ok, b_done, b_taken, blanked, blank_out,
         ids, dest_ok, scattered, back) = (s.sem(n) for n in (
             "l_done", "shifted", "exped", "chain", "mem_ok", "cnt_done", "ge_ok", "turned", "gt_ok", "b_done",
             "b_taken", "blanked", "blank_out", "ids", "dest_ok", "scattered", "back"))
        table = c.table
        with s.block() as block:

            @block.sync
            def _(sp):
                sp.dma_start(wr[:], rows(a["w_router_2"][0])).then_inc(wr_in, 16)
                sp.dma_start(br[:], a["b_router_2"].to_broadcast([P, EXPERTS])).then_inc(br_in, 16)
                sp.dma_start(bd[:], a["b_down_2"][0]).then_inc(bd_in, 16)
                sp.wait_ge(blanked, 2)
                sp.dma_start(table.rearrange("(p r) w -> p r w", p=P), blank[:]).then_inc(blank_out, 16)

            @block.gpsimd
            def _(pool):
                pool.memset(blank[:], 0).then_inc(ids, 1)
                pool.wait_ge(ids, 1)
                pool.memset(blank[:, :, 1:2], 4 * ROWS).then_inc(blanked, 1)
                pool.memset(entry[:], 0).then_inc(blanked, 1)
                pool.wait_ge(blanked, 2)
                e4 = entry[:].rearrange("p (m k) w -> p m k w", m=M)
                pool.iota(e4[:, :, :, 0], pattern=[[P, M], [0, EK]], base=0, channel_multiplier=1).then_inc(ids, 1)
                pool.iota(e4[:, :, :, 1], pattern=[[P * EK, M], [1, EK]], base=0, channel_multiplier=EK).then_inc(ids, 1)
                pool.wait_ge(blank_out, 16)
                pool.wait_ge(dest_ok, 1)
                for i in range(M * EK):
                    pool.indirect_dma_start(out=table[:, :], out_offset=bass.IndirectOffsetOnAxis(ap=desti[:, i:i + 1], axis=0),
                                            in_=entry[:, i, :], in_offset=None, bounds_check=P * NBLK - 1,
                                            oob_is_err=False).then_inc(scattered, 16)
                pool.wait_ge(scattered, 16 * M * EK)
                pool.dma_start(c.slots[:, 0:NBLK, :], table.rearrange("(p r) w -> p r w", p=P)).then_inc(back, 16)
                pool.wait_ge(back, 16)

            @block.tensor
            def _(pe):
                pe.wait_ge(wr_in, 16)
                for m in range(M):
                    for k in range(KD):
                        mm = pe.matmul(ps[:, 0, m * EXPERTS:(m + 1) * EXPERTS], c.hT[:, k, m * P:m * P + P], wr[:, k, :],
                                       start=(k == 0), stop=(k == KD - 1))
                mm.then_inc(l_done, 1)
                pe.wait_ge(mem_ok, 1)
                for m in range(M):
                    for q in range(m + 1):
                        pe.matmul(ps[:, 1, m * EXPERTS:(m + 1) * EXPERTS], c.upper[:] if q == m else c.ones[:],
                                  mem[:, q, :], start=(q == 0), stop=(q == m))
                for q in range(M):
                    mm = pe.matmul(ps[:, 2, 0:EXPERTS], c.ones[:], mem[:, q, :], start=(q == 0), stop=(q == M - 1))
                mm.then_inc(cnt_done, 1)
                pe.wait_ge(ge_ok, 1)
                for m in range(M):
                    t = pe.transpose(ps[0:EXPERTS, 3, m * P:m * P + P], ge[:, m, :], c.ident[:])
                t.then_inc(turned, 1)
                pe.wait_ge(gt_ok, 1)
                pe.wait_ge(bd_in, 16)
                for i in range(2 * M):
                    m, n = i // 2, i % 2
                    if i >= 4:
                        pe.wait_ge(b_taken, i - 3)
                    pe.matmul(ps[:, 4 + i % 4, :], geT[:, m, :], bd[:, n * 512:n * 512 + 512],
                              start=True, stop=True).then_inc(b_done, 1)

            @block.scalar
            def _(act):
                act.wait_ge(shifted, 1)
                act.activation(gate[:], gate[:], ACT.Exp).then_inc(exped, 1)
                act.wait_ge(turned, 1)
                act.activation(geT[:], ps[0:EXPERTS, 3, :].rearrange("e (m t) -> e m t", m=M), ACT.Copy).then_inc(gt_ok, 1)

            @block.vector
            def _(dve):
                step = chained(dve, chain)
                step(dve.memset(onesE[:], 1.0))
                dve.wait_ge(br_in, 16)
                dve.wait_ge(l_done, 1)
                step(dve.tensor_tensor(logit[:], ps[:, 0, 0:M * EXPERTS].rearrange("p (m e) -> p m e", m=M),
                                       br[:].unsqueeze(1).to_broadcast(ME), ALU.add))
                for m in range(M):
                    ins = dve.max(v8[:, m, :], logit[:, m, :])
                step(ins)
                for m in range(M):
                    ins = dve.max_index(i8[:, m, :], v8[:, m, :], logit[:, m, :])
                step(ins)
                dve.tensor_tensor(gate[:], v8[:, :, 0:EK], v8[:, :, 0:1].to_broadcast([P, M, EK]),
                                  ALU.subtract).then_inc(shifted, 1)
                step(dve.tensor_copy(i4[:], i8[:, :, 0:EK]))
                step(dve.tensor_tensor(hot[:], i4[:].rearrange("p m k -> p (m k)").unsqueeze(2).to_broadcast([P, M * EK, EXPERTS]),
                                       c.count[:, 0:EXPERTS].unsqueeze(1).to_broadcast([P, M * EK, EXPERTS]), ALU.is_equal))
                hot4 = hot[:].rearrange("p (m k) e -> p m k e", m=M)
                by_e = "p (m k) e -> p m e k"
                for m in range(M):
                    ins = dve.tensor_reduce(mem[:, m, :], hot[:, m * EK:(m + 1) * EK, :].rearrange("p k e -> p e k"),
                                            AX.X, ALU.add)
                ins.then_inc(mem_ok, 1)
                dve.wait_ge(mem_ok, 1)
                dve.wait_ge(exped, 1)
                step(dve.tensor_reduce(tot[:], gate[:], AX.X, ALU.add))
                step(dve.reciprocal(tot[:], tot[:]))
                step(dve.tensor_tensor(gate[:], gate[:], tot[:].unsqueeze(2).to_broadcast([P, M, EK]), ALU.mult))
                step(dve.tensor_tensor(hg[:], hot[:], gate[:].rearrange("p m k -> p (m k)").unsqueeze(2)
                                       .to_broadcast([P, M * EK, EXPERTS]), ALU.mult))
                for m in range(M):
                    ins = dve.tensor_reduce(ge[:, m, :], hg[:, m * EK:(m + 1) * EK, :].rearrange("p k e -> p e k"),
                                            AX.X, ALU.add)
                ins.then_inc(ge_ok, 1)
                dve.wait_ge(cnt_done, 1)
                step(dve.tensor_copy(cnt[:], ps[:, 2, 0:EXPERTS]))
                step(dve.tensor_scalar(nb[:], cnt[:], 0.0, None, ALU.is_gt))
                for r in range(1, T // P):
                    step(dve.tensor_scalar(t2[:], cnt[:], float(P * r), None, ALU.is_gt))
                    step(dve.tensor_tensor(nb[:], nb[:], t2[:], ALU.add))
                step(dve.tensor_tensor_scan(end[:], onesE[:], nb[:], 0.0, ALU.mult, ALU.add))
                step(dve.tensor_tensor(start[:], end[:], nb[:], ALU.subtract))
                step(dve.tensor_scalar(rank[:], ps[:, 1, 0:M * EXPERTS].rearrange("p (m e) -> p m e", m=M), -1.0, None, ALU.add))
                step(dve.tensor_scalar(over[:], rank[:], float(P), None, ALU.is_ge))
                for r in range(2, T // P):
                    step(dve.tensor_scalar(tmp[:], rank[:], float(P * r), None, ALU.is_ge))
                    step(dve.tensor_tensor(over[:], over[:], tmp[:], ALU.add))
                step(dve.tensor_scalar(over[:], over[:], -float(P * NBLK - 1), None, ALU.mult))
                step(dve.scalar_tensor_tensor(out=rank[:], in0=rank[:], scalar=float(NBLK), in1=over[:],
                                              op0=ALU.mult, op1=ALU.add))
                step(dve.tensor_tensor(rank[:], rank[:], start[:].unsqueeze(1).to_broadcast(ME), ALU.add))
                step(dve.tensor_tensor(hg[:].rearrange("p (m k) e -> p m k e", m=M), hot4,
                                       rank[:].unsqueeze(2).to_broadcast([P, M, EK, EXPERTS]), ALU.mult))
                step(dve.tensor_reduce(dest[:], hg[:], AX.X, ALU.add))
                step(dve.tensor_copy(desti[:], dest[:]))
                dve.wait_ge(ids, 3)
                dve.tensor_copy(entry[:, :, 2], gate[:].rearrange("p m k -> p (m k)").bitcast(I32)).then_inc(dest_ok, 1)
                step(dve.tensor_tensor(ecmp[:], end[0:1, :].unsqueeze(1).to_broadcast([1, NBLK, EXPERTS]),
                                       c.count[0:1, 0:NBLK].unsqueeze(2).to_broadcast([1, NBLK, EXPERTS]), ALU.is_le))
                step(dve.tensor_reduce(ownf[:], ecmp[:], AX.X, ALU.add))
                step(dve.tensor_scalar(ownf[:], ownf[:], float(EXPERTS - 1), None, ALU.min))
                step(dve.tensor_copy(c.owner[0:1, 0:NBLK], ownf[:]))
                step(dve.tensor_copy(c.owner[0:1, NBLK:NBLK + 1], end[0:1, EXPERTS - 1:EXPERTS]))
                for i in range(2 * M):
                    m, n = i // 2, i % 2
                    dve.wait_ge(b_done, i + 1)
                    out = c.h[:, m, n * 512:n * 512 + 512]
                    dve.scalar_tensor_tensor(out=out, in0=out, scalar=ALPHA, in1=ps[:, 4 + i % 4, :],
                                             op0=ALU.mult, op1=ALU.add).then_inc(b_taken, 1)


def stage_experts(nc, c, a):
    CHUNK = 512
    HT = 4
    CHUNKS, PIECES = 6, 12
    RAW, RING = 4, 4
    PIECE = KD * CHUNK // 2
    STARTED = 2 * RAW
    with Stage(nc, "moe") as s:
        raw = [s.sb(f"raw{i}", [P, KD * CHUNK])[:] for i in range(RAW - 1)] + [c.hT[:].rearrange("p k t -> p (k t)")]
        w_hi = [s.sb(f"w_hi{i}", [P, PIECE], F32R) for i in range(RING)]
        w_lo = [s.sb(f"w_lo{i}", [P, PIECE], F32R) for i in range(RING)]
        bias = s.sb("bias", [2 * EXPERTS, 2 * D], F32R)
        pick = s.sb("pick", [2 * EXPERTS, P], F32R)
        slot = s.sb("slot", [P, 2, 4], I32)
        xg = s.sb("xg", [P, 2, D])
        x_hi = s.sb("x_hi", [P, KD, P], F32R)
        x_lo = s.sb("x_lo", [P, KD, P], F32R)
        ga = s.sb("ga", [P, CHUNK])
        up = s.sb("up", [P, CHUNK])
        sg = s.sb("sg", [P, CHUNK])
        hid = s.sb("hid", [P, CHUNK])
        hid_hi = s.sb("hid_hi", [P, KD, P], F32R)
        hid_lo = s.sb("hid_lo", [P, KD, P], F32R)
        y = s.sb("y", [P, 2, D])
        GU = s.ps("GU", [P, 4, CHUNK])
        Y = s.ps("Y", [P, 2, CHUNK])
        X = s.ps("X", [P, 2, 4, P])
        raw_in = [s.sem(f"raw_in{i}") for i in range(RAW)]
        bias_in = s.sem("bias_in")
        gathered = [s.sem(f"gathered{i}") for i in range(2)]
        (slotted, paced, bias_high, bias_ok, picked, x_done, x_high, x_low, w_high, w_low, piece_done,
         g_ok, sig, h_chain, h_ok, turned, h_high, h_low, y_ok, stored) = (s.sem(n) for n in (
             "slotted", "paced", "bias_high", "bias_ok", "picked", "x_done", "x_high", "x_low", "w_high",
             "w_low", "piece_done", "g_ok", "sig", "h_chain", "h_ok", "turned", "h_high", "h_low", "y_ok", "stored"))
        wg_d, wu_d, wd_d = (a[n][0] for n in ("w_gate_2", "w_up_2", "w_down_2"))

        def n_blocks(eng):
            return eng.value_load(c.owner[0:1, NBLK:NBLK + 1], min_val=1, max_val=BLOCKS)

        def owner_of(eng, j):
            return eng.value_load(c.owner[0:1, ds(j, 1)], min_val=0, max_val=EXPERTS - 1)

        def chunk_of(it, u, q):
            i = CHUNKS * u + q
            return i % RAW, it * (2 * CHUNKS // RAW) + i // RAW

        def cut(w, q):
            return w.rearrange("p (k n) -> p k n", n=CHUNK if q < 4 else D)

        def piece_of(r, p):
            return raw[r][:, p % 2 * PIECE:(p % 2 + 1) * PIECE]

        def h_turned(half):
            return GU[:, 2 * half, :].rearrange("p (f t) -> p f t", f=HT)

        def h_split(h, half):
            return h[:, HT * half:HT * half + HT, :]

        with s.block() as block:

            @block.sync
            def _(sp):
                for part in range(2):
                    sp.dma_start(y[EXPERTS * part:EXPERTS * part + EXPERTS, :, :],
                                 a["bias_gate_up"]).then_inc(bias_in, 16)
                n = n_blocks(sp)
                with sp.Fori(0, NBLK // 2) as it:
                    for u in range(2):
                        j = it * 2 + u
                        with sp.If(j < n):
                            e = owner_of(sp, j)
                            for q in range(CHUNKS):
                                r, _ = chunk_of(it, u, q)
                                if q < 4:
                                    w_d, half = (wg_d, wu_d)[q % 2], q // 2
                                    src = w_d[ds(e, 1), :, half * CHUNK:(half + 1) * CHUNK]
                                else:
                                    src = wd_d[ds(e, 1), (q - 4) * CHUNK:(q - 3) * CHUNK, :]
                                sp.wait_ge(w_low, j * PIECES + (STARTED + 2 * (q - RAW) + 2))
                                sp.dma_start(cut(raw[r], q), src.rearrange("o (k p) n -> p (o k) n", p=P)).then_inc(raw_in[r], 16)

            @block.gpsimd
            def _(pool):
                n = n_blocks(pool)

                def gather(j, b):
                    pool.tensor_copy(slot[:, b, :], c.slots[:, ds(j, 1), :].rearrange("p o w -> p (o w)")).then_inc(slotted, 1)
                    pool.wait_ge(slotted, j + 1)
                    pool.sem_inc(paced, 1)
                    pool.indirect_dma_start(out=xg[:, b, :], out_offset=None, in_=c.h_rows[:, :],
                                            in_offset=bass.IndirectOffsetOnAxis(ap=slot[:, b, 0:1].bitcast(U32), axis=0),
                                            bounds_check=T - 1, oob_is_err=False).then_inc(gathered[b], 16)

                gather(0, 0)
                with pool.Fori(0, NBLK // 2) as it:
                    for u in range(2):
                        j = it * 2 + u
                        with pool.If(j + 1 < n):
                            gather(j + 1, 1 - u)
                        with pool.If(j < n):
                            pool.wait_ge(y_ok, j + 2)
                            pool.sem_inc(paced, 1)
                            pool.indirect_dma_start(out=c.pair_rows[:, :],
                                                    out_offset=bass.IndirectOffsetOnAxis(ap=slot[:, u, 1:2].bitcast(U32), axis=0),
                                                    in_=y[:, u, :], in_offset=None, bounds_check=ROWS - 1,
                                                    oob_is_err=False).then_inc(stored, 16)
                            pool.wait_ge(stored, j * 16 + 16)

            @block.tensor
            def _(pe):
                n = n_blocks(pe)

                def turn(b, nth):
                    pe.wait_ge(gathered[b], nth * 16 + 16)
                    for h in range(2):
                        for k in range(4):
                            t = pe.transpose(X[:, h, k, :], xg[:, b, (4 * h + k) * P:(4 * h + k + 1) * P], c.ident[:])
                    t.then_inc(x_done, 1)

                def turn_hidden(j, half):
                    pe.wait_ge(h_ok, j * 2 + (half + 1))
                    for f in range(HT):
                        t = pe.transpose(h_turned(half)[:, f, :], hid[:, f * P:f * P + P], c.ident[:])
                    t.then_inc(turned, 1)

                turn(0, 0)
                pe.wait_ge(bias_ok, 1)
                with pe.Fori(0, NBLK // 2) as it:
                    for u in range(2):
                        j = it * 2 + u
                        with pe.If(j < n):
                            pe.wait_ge(x_low, j + 1)
                            pe.wait_ge(picked, j + 1)
                            for p in range(PIECES):
                                q, second = p // 2, p % 2
                                hi, lo = cut(w_hi[p % RING][:], q), cut(w_lo[p % RING][:], q)
                                if p == 8:
                                    pe.wait_ge(y_ok, j + 1)
                                    pe.wait_ge(h_low, j * 2 + 1)
                                if p == 10:
                                    pe.wait_ge(h_low, j * 2 + 2)
                                pe.wait_ge(w_low, j * PIECES + (STARTED + p + 1))
                                if q < 4:
                                    out = GU[:, q, :]
                                    if not second:
                                        o = D * (q % 2) + CHUNK * (q // 2)
                                        pe.matmul(out, pick[:], bias[:, o:o + CHUNK], start=True, stop=False)
                                    for k in range(4):
                                        kx = 4 * second + k
                                        pe.matmul(out, x_hi[:, kx, :], hi[:, k, :], start=False, stop=False)
                                        pe.matmul(out, x_hi[:, kx, :], lo[:, k, :], start=False, stop=False)
                                        mm = pe.matmul(out, x_lo[:, kx, :], hi[:, k, :], start=False, stop=(kx == KD - 1))
                                else:
                                    for f in range(2):
                                        h = HT * (q - 4) + 2 * second + f
                                        for b in range(2):
                                            cols = slice(b * CHUNK, (b + 1) * CHUNK)
                                            pe.matmul(Y[:, b, :], hid_hi[:, h, :], hi[:, f, cols], start=(h == 0), stop=False)
                                            pe.matmul(Y[:, b, :], hid_hi[:, h, :], lo[:, f, cols], start=False, stop=False)
                                            mm = pe.matmul(Y[:, b, :], hid_lo[:, h, :], hi[:, f, cols], start=False, stop=(h == KD - 1))
                                mm.then_inc(piece_done, 1)
                                if p == 5:
                                    turn_hidden(j, 0)
                                if p == 8:
                                    turn_hidden(j, 1)
                                if p == 9:
                                    with pe.If(j + 1 < n):
                                        turn(1 - u, it + u)

            @block.scalar
            def _(act):
                n = n_blocks(act)

                def high(it, u, p, first=False):
                    r, nth = chunk_of(it, u, p // 2)
                    if p % 2 == 0:
                        act.wait_ge(raw_in[r], nth * 16 + 16)
                    if not first:
                        act.wait_ge(piece_done, it * (2 * PIECES) + (PIECES * u + p + 1 - RING))
                    act.activation(w_hi[p % RING][:], piece_of(r, p), ACT.Copy).then_inc(w_high, 1)

                def x_part(nth):
                    act.wait_ge(x_done, nth + 1)
                    act.activation(x_hi[:, 0:4, :], X[:, 0, :, :], ACT.Copy)
                    act.activation(x_hi[:, 4:8, :], X[:, 1, :, :], ACT.Copy).then_inc(x_high, 1)

                def sigmoid(j, half):
                    act.wait_ge(g_ok, j * 2 + (half + 1))
                    act.activation(sg[:], ga[:], ACT.Sigmoid, scale=SWIGLU).then_inc(sig, 1)

                def hidden(j, half):
                    act.wait_ge(turned, j * 2 + (half + 1))
                    act.activation(h_split(hid_hi, half), h_turned(half), ACT.Copy).then_inc(h_high, 1)

                act.sem_inc(y_ok, 1)
                act.wait_ge(bias_in, 32)
                act.activation(bias[:].rearrange("e (g n) -> e g n", g=2), y[0:2 * EXPERTS, :, :], ACT.Copy).then_inc(bias_high, 1)
                x_part(0)
                for p in range(RING):
                    high(0, 0, p, first=True)
                with act.Fori(0, NBLK // 2) as it:
                    for u in range(2):
                        j = it * 2 + u
                        with act.If(j < n):
                            for p in (4, 5, 6):
                                high(it, u, p)
                            sigmoid(j, 0)
                            high(it, u, 7)
                            high(it, u, 8)
                            hidden(j, 0)
                            high(it, u, 9)
                            high(it, u, 10)
                            sigmoid(j, 1)
                            high(it, u, 11)
                            hidden(j, 1)
                            with act.If(j + 1 < n):
                                high(it + u, 1 - u, 0)
                                x_part(j + 1)
                                for p in range(1, RING):
                                    high(it + u, 1 - u, p)
                            act.wait_ge(piece_done, j * PIECES + PIECES)
                            for b in range(2):
                                ins = act.activation(y[:, u, b * CHUNK:(b + 1) * CHUNK], Y[:, b, :], ACT.Copy,
                                                     scale=slot[:, u, 2:3].bitcast(F32))
                            ins.then_inc(y_ok, 1)

            @block.vector
            def _(dve):
                n = n_blocks(dve)

                def low(it, u, p):
                    r, _ = chunk_of(it, u, p // 2)
                    dve.wait_ge(w_high, it * (2 * PIECES) + (PIECES * u + p + 1))
                    dve.tensor_tensor(w_lo[p % RING][:], piece_of(r, p), w_hi[p % RING][:].bitcast(F32),
                                      ALU.subtract).then_inc(w_low, 1)

                def x_part(nth):
                    dve.wait_ge(x_high, nth + 1)
                    dve.tensor_tensor(x_lo[:, 0:4, :], X[:, 0, :, :], x_hi[:, 0:4, :].bitcast(F32), ALU.subtract)
                    dve.tensor_tensor(x_lo[:, 4:8, :], X[:, 1, :, :], x_hi[:, 4:8, :].bitcast(F32), ALU.subtract).then_inc(x_low, 1)

                def pick_bias(j):
                    e = owner_of(dve, j)
                    E2 = 2 * EXPERTS
                    dve.tensor_tensor(pick[:], c.ident[0:E2, ds(e, 1)].to_broadcast([E2, P]),
                                      c.ident[0:E2, ds(e + EXPERTS, 1)].to_broadcast([E2, P]), ALU.add).then_inc(picked, 1)

                def gate(j, half):
                    dve.wait_ge(piece_done, j * PIECES + (4 * half + 2))
                    dve.tensor_scalar(ga[:], GU[:, 2 * half, :], LIMIT, None, ALU.min).then_inc(g_ok, 1)

                def unit(j, half):
                    dve.wait_ge(piece_done, j * PIECES + (4 * half + 4))
                    dve.tensor_scalar(up[:], GU[:, 2 * half + 1, :], LIMIT, -LIMIT, ALU.min, ALU.max).then_inc(h_chain, 1)
                    dve.wait_ge(sig, j * 2 + (half + 1))
                    dve.tensor_tensor(ga[:], ga[:], sg[:], ALU.mult).then_inc(h_chain, 1)
                    dve.wait_ge(h_chain, j * 4 + (2 * half + 2))
                    dve.scalar_tensor_tensor(out=hid[:], in0=up[:], scalar=1.0, in1=ga[:],
                                             op0=ALU.add, op1=ALU.mult).then_inc(h_ok, 1)

                def hidden(j, half):
                    dve.wait_ge(h_high, j * 2 + (half + 1))
                    dve.tensor_tensor(h_split(hid_lo, half), h_turned(half), h_split(hid_hi, half).bitcast(F32),
                                      ALU.subtract).then_inc(h_low, 1)

                dve.sem_inc(w_low, STARTED)
                dve.wait_ge(bias_high, 1)
                lows = slice(EXPERTS, 2 * EXPERTS)
                lo_rows = bias[lows, :].rearrange("e (g n) -> e g n", g=2)
                dve.tensor_tensor(lo_rows, y[lows, :, :], lo_rows.bitcast(F32), ALU.subtract).then_inc(bias_ok, 1)
                pick_bias(0)
                x_part(0)
                for p in range(RING):
                    low(0, 0, p)
                with dve.Fori(0, NBLK // 2) as it:
                    for u in range(2):
                        j = it * 2 + u
                        with dve.If(j < n):
                            low(it, u, 4)
                            low(it, u, 5)
                            gate(j, 0)
                            low(it, u, 6)
                            unit(j, 0)
                            low(it, u, 7)
                            low(it, u, 8)
                            hidden(j, 0)
                            low(it, u, 9)
                            gate(j, 1)
                            low(it, u, 10)
                            unit(j, 1)
                            low(it, u, 11)
                            hidden(j, 1)
                            with dve.If(j + 1 < n):
                                pick_bias(j + 1)
                                low(it + u, 1 - u, 0)
                                x_part(j + 1)
                                for p in range(1, RING):
                                    low(it + u, 1 - u, p)


def stage_combine(nc, c, a):
    with Stage(nc, "comb") as s:
        r = s.sb("r", [P, M, EK, D])
        loaded = [s.sem(f"loaded{m}") for m in range(M)]
        chain = s.sem("chain")
        src = c.pair_rows.rearrange("(m p k) d -> p m k d", p=P, k=EK)
        with s.block() as block:

            @block.sync
            def _(sp):
                for m in range(M):
                    sp.dma_start(r[:, m, :, :], src[:, m, :, :]).then_inc(loaded[m], 16)

            @block.vector
            def _(dve):
                step = chained(dve, chain)
                for m in range(M):
                    dve.wait_ge(loaded[m], 16)
                    for k in range(EK):
                        step(dve.tensor_tensor(c.h[:, m, :], c.h[:, m, :], r[:, m, k, :], ALU.add))


def program(nc, a, out):
    with ExitStack() as ctx:
        c = Common(nc, ctx)
        c.stream(ctx)
        stage_constants(nc, c)
        with ExitStack() as front:
            c.front(front)
            stage_norm_in(nc, c, a)
            stage_project(nc, c, a)
            stage_conf_norm(nc, c, a)
            stage_ssd(nc, c, a)
            stage_out_proj(nc, c, a, "out1", c.yT, a["w_out"][0], 2 * KD, a["x"][0], 1.0)
        with ExitStack() as peer:
            c.peer(peer)
            with ExitStack() as tmp:
                xn = c.sb(tmp, "xn", [P, M, D])
                stage_token_norm(nc, c, a, "nffn", xn, c.hT, col_w=a["norm_ffn_w"])
            stage_peer_scores(nc, c, a)
            stage_gate_matrix(nc, c, a)
            with ExitStack() as split:
                c.split(split)
                stage_split_x(nc, c)
                stage_peer_experts(nc, c, a)
        stage_token_norm(nc, c, a, "nfin", c.h, c.hT, row_w=a["norm_final_w"])
        second_block(nc, c, a, out)


def second_block(nc, c, a, out):
    with ExitStack() as mix:
        c.second(mix)
        stage_project2(nc, c, a)
        stage_attention(nc, c, a)
        stage_out_proj(nc, c, a, "out2", c.mixT, a["w_out_2"], KD, None, ALPHA, bias=a["b_out_2"])
    with ExitStack() as moe:
        c.routed(moe)
        stage_token_norm(nc, c, a, "ln1", c.h, c.hT, centre=True, row_w=a["ln1_g_2"], row_b=a["ln1_b_2"], save=c.h_rows)
        stage_route(nc, c, a)
        stage_experts(nc, c, a)
        stage_combine(nc, c, a)
        stage_token_norm(nc, c, a, "ln2", c.h, centre=True, row_w=a["ln2_g_2"], row_b=a["ln2_b_2"], save=out[0])


class Common:

    def __init__(self, nc, ctx):
        self.nc = nc
        self.ident = self.sb(ctx, "ident", [P, P])
        self.ones = self.sb(ctx, "ones", [P, P])
        self.upper = self.sb(ctx, "upper", [P, P])
        self.count = self.sb(ctx, "count", [P, P])
        self.count_i = self.sb(ctx, "count_i", [P, P], I32)

    def sb(self, ctx, name, shape, dt=F32):
        return ctx.enter_context(self.nc.sbuf_tensor(f"all_{name}", shape, dt))

    def stream(self, ctx):
        self.h = self.sb(ctx, "h", [P, M, D])
        self.hT = self.sb(ctx, "hT", [P, KD, T])

    def peer(self, ctx):
        self.idxT = self.sb(ctx, "idxT", [P, 3, T])
        self.gates = self.nc.dram_tensor("peer_gates", [BATCHES, NK, NK * TB], F32, kind="Internal").ap()

    def split(self, ctx):
        self.x_hi = self.sb(ctx, "x_hi", [P, KD, T], F32R)
        self.x_lo = self.sb(ctx, "x_lo", [P, KD, T], F32R)

    def second(self, ctx):
        self.qT = self.sb(ctx, "qT", [P, AJ, T])
        self.kT = self.sb(ctx, "kT", [P, T])
        self.uT2 = self.sb(ctx, "uT2", [P, 4, T])
        self.vtok = self.sb(ctx, "vtok", [P, M, P])
        self.gtok = self.sb(ctx, "gtok", [P, M, 512])
        self.mixT = self.sb(ctx, "mixT", [P, KD, T])

    def routed(self, ctx):
        self.slots = self.sb(ctx, "slots", [P, NBLK + 1, 4], I32)
        self.owner = self.sb(ctx, "owner", [1, NBLK + 1], I32)
        self.table = self.nc.dram_tensor("slot_table", [P * NBLK, 4], I32, kind="Internal").ap()
        self.h_rows = self.nc.dram_tensor("h_rows", [T, D], F32, kind="Internal").ap()
        self.pair_rows = self.nc.dram_tensor("pair_rows", [ROWS, D], F32, kind="Internal").ap()

    def front(self, ctx):
        self.yT = self.sb(ctx, "yT", [P, 2 * KD, T])
        self.uT = self.sb(ctx, "uT", [P, KD, TA])
        self.xbcT = self.sb(ctx, "xbcT", [P, 16, TA])
        self.zT = self.sb(ctx, "zT", [P, KD, T])
        self.dt = self.sb(ctx, "dt", [P, M + 1, HEADS])
        self.dta = self.sb(ctx, "dta", [P, M + 1, HEADS])


FRONT = ("x", "meta_tokens", "norm_mix_w", "w_in", "ssd_dt_bias", "conf_taps", "conf_conv_b", "ssd_taps",
         "ssd_conv_b", "ssd_A_log", "ssd_D", "ssd_norm_w", "conf_ln_g", "conf_ln_b")


def layout(inputs):
    import numpy as np
    v = {k: np.asarray(x) for k, x in inputs.items()}

    def channels(x):
        return np.ascontiguousarray(x.reshape(-1, P).T)

    def channel_rows(x):
        return np.ascontiguousarray(x.reshape(x.shape[0], -1, P).transpose(2, 1, 0))

    out = {k: v[k] for k in ("x", "meta_tokens", "w_in", "ssd_dt_bias", "ssd_A_log")}
    for k in ("norm_mix_w", "conf_conv_b", "ssd_conv_b", "ssd_norm_w", "conf_ln_g", "conf_ln_b"):
        out[k] = channels(v[k][0])
    out["conf_taps"] = channel_rows(v["conf_conv_w"][0])
    out["ssd_taps"] = channel_rows(v["ssd_conv_w"][0])
    out["ssd_D"] = channels(np.repeat(v["ssd_D"][0], 64))
    keys = np.stack([v["peer_sub_keys_1"][0], v["peer_sub_keys_2"][0]], 1)
    out["peer_keysT"] = np.ascontiguousarray(keys.reshape(2 * PH, NK, P).transpose(2, 0, 1))
    for k in ("w_out", "peer_w_query", "peer_w_up"):
        out[k] = v[k]
    out["peer_w_downT"] = np.ascontiguousarray(v["peer_w_down"][0].T)
    out["norm_ffn_w"] = channels(v["norm_ffn_w"][0])
    out["norm_final_w"] = v["norm_final_w"][None]
    heads = np.arange(AH * 64).reshape(2, AJ, 64).transpose(1, 0, 2).reshape(-1)
    cols = np.concatenate([heads, np.arange(AH * 64, 1792)])
    out["w_in_2"] = np.ascontiguousarray(v["w_in_2"][0][:, cols])
    out["b_in_2_col"] = channels(v["b_in_2"][0][cols])
    out["b_in_2_row"] = np.concatenate([v["b_in_2"][:, COL_V:COL_U], v["b_in_2"][:, COL_S:]], 1)
    out["w_out_2"] = np.ascontiguousarray(v["w_out_2"][0][np.concatenate([heads, np.arange(AH * 64, D)])])
    out["w_spatial_2T"] = np.ascontiguousarray(v["w_spatial_2"][0].transpose(2, 0, 1))
    bias = np.stack([v["b_gate_2"][0], v["b_up_2"][0]], 1)
    out["bias_gate_up"] = np.ascontiguousarray(bias)
    for k in ("ln_v_g_2", "ln_v_b_2", "sinks_2", "b_spatial_2", "b_out_2", "ln1_g_2", "ln1_b_2", "w_router_2",
              "b_router_2", "w_gate_2", "w_up_2", "w_down_2", "b_down_2", "ln2_g_2", "ln2_b_2"):
        out[k] = v[k]
    return out


def kernel(**inputs):
    from concourse import bacc
    from concourse.bass_utils import run_bass_kernel_spmd

    nc = bacc.Bacc("TRN2", target_bir_lowering=False, num_devices=1)
    arrays = {f"in_{k}": x for k, x in layout(inputs).items()}
    a = {k[3:]: nc.dram_tensor(k, x.shape, F32, kind="ExternalInput").ap() for k, x in arrays.items()}
    out = nc.dram_tensor("out", (1, T, D), F32, kind="ExternalOutput").ap()
    program(nc, a, out)
    r = run_bass_kernel_spmd(nc, [arrays], core_ids=[0])
    return r.results[0]["out"]
```

```python
from contextlib import ExitStack

import concourse.bass as bass
from concourse import mybir

F32 = mybir.dt.float32
F32R = mybir.dt.float32r
I32 = mybir.dt.int32
U32 = mybir.dt.uint32
ACT = mybir.ActivationFunctionType
ALU = mybir.AluOpType
AX = mybir.AxisListType

P = 128
D = 1024
KD = D // P
T = 512
M = T // P
META = 16
TA = T + META
HALF = TA // 2
EPS = 1e-5
D_XBC = 2048
HEADS = 16
GROUPS = 4
XT = KD
NB, NC_ = 4, 4
CONV = 4
CK = 31
COL_XBC, COL_DT, COL_A, COL_G = 1024, 3072, 3088, 4112
PH = 8
TOPK = 16
NK = 128
ds = bass.ds


def chained(eng, sem, start=0):
    n = [start]

    def step(ins):
        n[0] += 1
        ins.then_inc(sem, 1)
        eng.wait_ge(sem, n[0])
    return step


class Stage:

    def __init__(self, nc, name):
        self.nc, self.name, self.ctx, self.sems = nc, name, ExitStack(), []

    def __enter__(self):
        self.ctx.__enter__()
        return self

    def __exit__(self, *a):
        if a[0] is None:
            self.nc.clear_and_free_semaphores(self.sems)
            self.nc.all_engine_barrier()
        return self.ctx.__exit__(*a)

    def sb(self, name, shape, dt=F32):
        return self.ctx.enter_context(self.nc.sbuf_tensor(f"{self.name}_{name}", shape, dt))

    def ps(self, name, shape, dt=F32):
        return self.ctx.enter_context(self.nc.psum_tensor(f"{self.name}_{name}", shape, dt))

    def sem(self, name):
        self.sems.append(self.nc.alloc_semaphore(f"{self.name}_{name}"))
        return self.sems[-1]

    def block(self):
        return self.nc.Block()


def tokens(ap):
    return ap.rearrange("(m p) d -> p m d", p=P)


def rows(ap):
    return ap.rearrange("(k p) n -> p k n", p=P)


def stage_constants(nc, c):
    with Stage(nc, "const") as s:
        made = s.sem("made")
        with s.block() as block:

            @block.gpsimd
            def _(pool):
                pool.memset(c.ident[:], 0.0).then_inc(made, 1)
                pool.memset(c.ones[:], 1.0).then_inc(made, 1)
                pool.wait_ge(made, 2)
                pool.affine_select(out=c.ident[:], in_=c.ident[:], compare_op=ALU.not_equal, fill=1.0, base=0,
                                   pattern=[[-1, P]], channel_multiplier=1).then_inc(made, 1)
                pool.affine_select(out=c.upper[:], in_=c.ones[:], compare_op=ALU.is_ge, fill=0.0, base=0,
                                   pattern=[[1, P]], channel_multiplier=-1).then_inc(made, 1)
                pool.iota(c.count_i[:], pattern=[[1, P]], base=0, channel_multiplier=0).then_inc(made, 1)
                pool.wait_ge(made, 5)
                pool.tensor_copy(c.count[:], c.count_i[:]).then_inc(made, 1)
                pool.wait_ge(made, 6)


def stage_norm_in(nc, c, a):
    with Stage(nc, "norm") as s:
        x = s.sb("x", [P, M + 1, D])
        junk = s.sb("junk", [P, D])
        wn = s.sb("wn", [P, KD])
        ss = s.sb("ss", [P, M + 1])
        root = s.sb("root", [P, M + 1])
        ut = s.sb("ut", [P, 2, 4, P])
        tp = s.ps("tp", [P, 4, 4, P])
        loaded = [s.sem(f"loaded{m}") for m in range(M + 1)]
        wn_in = s.sem("wn_in")
        cleared, squared, rooted, scaled = (s.sem(n) for n in ("cleared", "squared", "rooted", "scaled"))
        chain, turned, copied, high, low = (s.sem(n) for n in ("chain", "turned", "copied", "high", "low"))

        def part(i):
            m = (M, *range(M))[i // 2]
            n, at = (P, META + m * P) if m < M else (META, 0)
            return n, slice(4 * (i % 2), 4 * (i % 2) + 4), slice(at, at + n)

        with s.block() as block:

            @block.sync
            def _(sp):
                for m in range(M):
                    sp.dma_start(x[:, m, :], tokens(a["x"][0])[:, m, :]).then_inc(loaded[m], 16)
                sp.dma_start(x[0:META, M, :], a["meta_tokens"]).then_inc(loaded[M], 16)
                sp.dma_start(wn[:], a["norm_mix_w"]).then_inc(wn_in, 16)

            @block.scalar
            def _(act):
                act.wait_ge(cleared, 1)
                for m in range(M + 1):
                    n = P if m < M else META
                    act.wait_ge(loaded[m], 16)
                    act.activation(junk[0:n, :], x[0:n, m, :], ACT.Square,
                                   accum_out=ss[0:n, m:m + 1]).then_inc(squared, 1)
                    act.wait_ge(squared, m + 1)
                act.wait_ge(scaled, 1)
                act.activation(root[:], root[:], ACT.Sqrt).then_inc(rooted, 1)
                for i in range(2 * (M + 1)):
                    n, ks, cols = part(i)
                    act.wait_ge(copied, i + 1)
                    act.activation(c.u_hi[:, ks, cols], ut[:, i % 2, :, 0:n], ACT.Copy).then_inc(high, 1)

            @block.vector
            def _(dve):
                step = chained(dve, chain)
                dve.memset(ss[:], 1.0).then_inc(cleared, 1)
                dve.wait_ge(squared, M + 1)
                dve.tensor_scalar(root[:], ss[:], 1.0 / D, EPS, ALU.mult, ALU.add).then_inc(scaled, 1)
                dve.wait_ge(rooted, 1)
                step(dve.reciprocal(ss[:], root[:]))
                for m in (M, *range(M)):
                    n = P if m < M else META
                    dve.tensor_scalar(x[0:n, m, :], x[0:n, m, :], ss[0:n, m:m + 1], None,
                                      ALU.mult).then_inc(scaled, 1)
                dve.wait_ge(wn_in, 16)
                for i in range(2 * (M + 1) + 1):
                    if i < 2 * (M + 1):
                        n, ks, _ = part(i)
                        dve.wait_ge(turned, i + 1)
                        if i >= 2:
                            dve.wait_ge(low, i - 1)
                        dve.tensor_tensor(ut[:, i % 2, :, 0:n], tp[:, i % 4, :, 0:n],
                                          wn[:, ks].unsqueeze(2).to_broadcast([P, 4, n]), ALU.mult).then_inc(copied, 1)
                    if i >= 1:
                        n, ks, cols = part(i - 1)
                        dve.wait_ge(high, i)
                        dve.tensor_tensor(c.u_lo[:, ks, cols], ut[:, (i - 1) % 2, :, 0:n],
                                          c.u_hi[:, ks, cols].bitcast(F32), ALU.subtract).then_inc(low, 1)

            @block.tensor
            def _(pe):
                i = 0
                for j, m in enumerate((M, *range(M))):
                    n = P if m < M else META
                    pe.wait_ge(scaled, 2 + j)
                    for h in range(2):
                        if i >= 4:
                            pe.wait_ge(copied, i - 3)
                        for k in range(4):
                            t = pe.transpose(tp[:, i % 4, k, 0:n], x[0:n, m, (4 * h + k) * P:(4 * h + k + 1) * P],
                                             c.ident[0:n, 0:n])
                        t.then_inc(turned, 1)
                        i += 1


def stage_project(nc, c, a):
    w_in = rows(a["w_in"][0])
    ROUNDS = KD
    jobs = []
    for i in range(ROUNDS + 1):
        if i < ROUNDS:
            jobs += [("a", i), ("g", i)]
        if i >= 1:
            jobs += [("x", 2 * i - 2), ("x", 2 * i - 1), ("z", i - 1)]
    JOBS = len(jobs)
    DT_JOB = 7
    RING = 4
    with Stage(nc, "proj") as s:
        w = [c.hT[:].rearrange("p k t -> p (k t)")[:, i * D:i * D + D].rearrange("p (k n) -> p k n", k=KD)
             for i in range(RING)]
        spare = c.h[:].rearrange("p m d -> p (m d)")
        w_hi = s.sb("w_hi", [P, RING, KD, P], F32R)
        w_lo = s.sb("w_lo", [P, RING, KD, P], F32R)
        wdt = s.sb("wdt", [P, KD, HEADS])
        wdt_hi = s.sb("wdt_hi", [P, KD, HEADS], F32R)
        wdt_lo = s.sb("wdt_lo", [P, KD, HEADS], F32R)
        tap_out = spare[:, 6 * TA:7 * TA]
        taps = s.sb("taps", [P, KD, CK])
        cbias = s.sb("cbias", [P, KD])
        xtaps = s.sb("xtaps", [P, 16, CONV])
        xbias = s.sb("xbias", [P, 16])
        dtb = s.sb("dtb", [P, HEADS])
        sg = spare[:, 0:2 * TA].rearrange("p (b t) -> p b t", b=2)
        acc = spare[:, 2 * TA:6 * TA].rearrange("p (b t) -> p b t", b=4)
        pad = CK - 1 - META
        gated = s.sb("gated", [P, 2, pad + TA])
        raw = s.sb("raw", [P, 4, CONV - 1 + TA])
        e1 = s.sb("e1", [P, M + 1, HEADS])
        e2 = s.sb("e2", [P, M + 1, HEADS])
        e3 = s.sb("e3", [P, M + 1, HEADS])
        ps = s.ps("ps", [P, 8, 512])
        w_in_sem = [s.sem(f"w_in{b}") for b in range(RING)]
        high, low, dt_high, dt_low = (s.sem(n) for n in ("high", "low", "dt_high", "dt_low"))
        consts_in = s.sem("consts_in")
        pair_done = s.sem("pair_done")
        sig, g_ready, chain, pool_chain = (s.sem(n) for n in ("sig", "g_ready", "chain", "pool_chain"))
        raw_in, silu_out, z_out = (s.sem(n) for n in ("raw_in", "silu_out", "z_out"))
        conv_out = (s.sem("even_conv_out"), s.sem("odd_conv_out"))
        zeroed = s.sem("zeroed")
        dt_done, dt_raw, dt_e, dt_l, dt_ok = (s.sem(n) for n in ("dt_done", "dt_raw", "dt_e", "dt_l", "dt_ok"))

        def column(job):
            kind, i = jobs[job]
            return {"a": COL_A, "g": COL_G, "x": COL_XBC, "z": 0}[kind] + P * i

        def released(job):
            kind, i = jobs[job]
            return {"a": g_ready, "g": sig, "x": raw_in, "z": z_out}[kind], i + 1

        def pair(job):
            b = 2 * (job % 4)
            return ps[:, b:b + 2, 0:HALF]

        def halves(t):
            return t.rearrange("p (h n) -> p h n", h=2)

        with s.block() as block:

            @block.sync
            def _(sp):
                def load(n):
                    sp.dma_start(w[n % RING], w_in[:, :, column(n):column(n) + P]).then_inc(w_in_sem[n % RING], 16)

                for n in range(RING):
                    load(n)
                sp.dma_start(wdt[:], w_in[:, :, COL_DT:COL_DT + HEADS]).then_inc(consts_in, 16)
                sp.dma_start(dtb[:], a["ssd_dt_bias"].to_broadcast([P, HEADS])).then_inc(consts_in, 16)
                sp.dma_start(taps[:], a["conf_taps"]).then_inc(consts_in, 16)
                sp.dma_start(cbias[:], a["conf_conv_b"]).then_inc(consts_in, 16)
                sp.dma_start(xtaps[:], a["ssd_taps"]).then_inc(consts_in, 16)
                sp.dma_start(xbias[:], a["ssd_conv_b"]).then_inc(consts_in, 16)
                for n in range(RING, JOBS):
                    sp.wait_ge(low, n - RING + 1)
                    load(n)

            @block.gpsimd
            def _(pool):
                step = chained(pool, pool_chain)

                def short_conv(x):
                    pool.wait_ge(raw_in, x + 1)
                    if x >= 4:
                        pool.wait_ge(silu_out, x - 3)
                    y = acc[:, x % 4, :]
                    step(pool.tensor_scalar(y, raw[:, x % 4, 0:TA], xtaps[:, x, 0:1], xbias[:, x:x + 1],
                                            ALU.mult, ALU.add))
                    for k in range(1, CONV):
                        step(pool.tensor_scalar(tap_out, raw[:, x % 4, k:k + TA], xtaps[:, x, k:k + 1], None, ALU.mult))
                        ins = pool.tensor_tensor(y, y, tap_out, ALU.add)
                        if k < CONV - 1:
                            step(ins)
                    ins.then_inc(conv_out[0], 1)

                for b in range(4):
                    pool.memset(raw[:, b, 0:CONV - 1], 0.0).then_inc(zeroed, 1)
                for n in range(JOBS):
                    if n == 4:
                        pool.wait_ge(dt_high, 1)
                        pool.tensor_tensor(wdt_lo[:], wdt[:], wdt_hi[:].bitcast(F32), ALU.subtract).then_inc(dt_low, 1)
                    if n >= RING and jobs[n - RING][0] == "x" and jobs[n - RING][1] % 2 == 0:
                        short_conv(jobs[n - RING][1])
                    pool.wait_ge(high, n + 1)
                    pool.tensor_tensor(w_lo[:, n % RING, :, :], w[n % RING], w_hi[:, n % RING, :, :].bitcast(F32),
                                       ALU.subtract).then_inc(low, 1)
                for n in range(JOBS - RING, JOBS):
                    if jobs[n][0] == "x" and jobs[n][1] % 2 == 0:
                        short_conv(jobs[n][1])

            @block.tensor
            def _(pe):
                def project_dt():
                    pe.wait_ge(dt_low, 1)
                    pe.wait_ge(*released(DT_JOB - 4))
                    for m in range(M + 1):
                        n, at = (META, 0) if m == 0 else (P, META + (m - 1) * P)
                        out = ps[0:n, 7, 16 * m:16 * m + 16]
                        for k in range(KD):
                            hi, lo = c.u_hi[:, k, at:at + n], c.u_lo[:, k, at:at + n]
                            pe.matmul(out, hi, wdt_hi[:, k, :], start=(k == 0), stop=False)
                            pe.matmul(out, hi, wdt_lo[:, k, :], start=False, stop=False)
                            mm = pe.matmul(out, lo, wdt_hi[:, k, :], start=False, stop=(k == KD - 1))
                    mm.then_inc(dt_done, 1)

                for n in range(JOBS):
                    if n == DT_JOB:
                        project_dt()
                        pe.wait_ge(dt_raw, 1)
                    pe.wait_ge(low, n + 1)
                    if n >= 4:
                        pe.wait_ge(*released(n - 4))
                    for k in range(KD):
                        hi, lo = w_hi[:, n % RING, k, :], w_lo[:, n % RING, k, :]
                        for left, right in ((hi, c.u_hi), (hi, c.u_lo), (lo, c.u_hi)):
                            for h in range(2):
                                mm = pe.matmul(ps[:, 2 * (n % 4) + h, 0:HALF], left, right[:, k, h * HALF:(h + 1) * HALF],
                                               start=(k == 0 and left is hi and right is c.u_hi),
                                               stop=(k == KD - 1 and left is lo))
                    mm.then_inc(pair_done, 1)

            @block.scalar
            def _(act):
                def split(n):
                    act.wait_ge(w_in_sem[n % RING], 16 * (n // RING + 1))
                    act.activation(w_hi[:, n % RING, :, :], w[n % RING], ACT.Copy).then_inc(high, 1)

                def silu(i):
                    act.wait_ge(conv_out[i % 2], i // 2 + 1)
                    act.activation(c.xbcT[:, i, :], acc[:, i % 4, :], ACT.Silu).then_inc(silu_out, 1)

                for n in range(RING):
                    split(n)
                act.wait_ge(consts_in, 96)
                act.activation(wdt_hi[:], wdt[:], ACT.Copy).then_inc(dt_high, 1)
                act.wait_ge(zeroed, 6)
                for n in range(JOBS):
                    if n == DT_JOB + 1:
                        act.wait_ge(dt_raw, 2)
                        act.activation(e2[:], e1[:], ACT.Exp, scale=-1.0).then_inc(dt_e, 1)
                        act.wait_ge(dt_e, 1)
                        act.activation(e3[:], e2[:], ACT.Ln, bias=1.0).then_inc(dt_l, 1)
                    kind, i = jobs[n]
                    act.wait_ge(pair_done, n + 1)
                    if kind == "g":
                        if i >= 2:
                            act.wait_ge(g_ready, i - 1)
                        act.activation(halves(sg[:, i % 2, :]), pair(n), ACT.Sigmoid).then_inc(sig, 1)
                    elif kind == "x":
                        if i >= 4:
                            act.wait_ge(conv_out[i % 2], i // 2 - 1)
                        act.activation(halves(raw[:, i % 4, CONV - 1:]), pair(n), ACT.Copy).then_inc(raw_in, 1)
                    elif kind == "z":
                        act.activation(c.zT[:, i, 0:HALF - META], pair(n)[:, 0, META:HALF], ACT.Silu)
                        act.activation(c.zT[:, i, HALF - META:T], pair(n)[:, 1, :], ACT.Silu).then_inc(z_out, 1)
                        if i >= 1:
                            silu(2 * i - 2)
                            silu(2 * i - 1)
                    if n + RING < JOBS:
                        split(n + RING)
                silu(2 * ROUNDS - 2)
                silu(2 * ROUNDS - 1)

            @block.vector
            def _(dve):
                step = chained(dve, chain)
                for b in range(2):
                    dve.memset(gated[:, b, 0:pad], 0.0).then_inc(zeroed, 1)
                step(dve.memset(e1[:], 0.0))
                step(dve.memset(c.dt[:], 0.0))
                dve.wait_ge(consts_in, 96)

                def dt_start():
                    dve.wait_ge(dt_done, 1)
                    dtp = ps[:, 7, 0:16 * (M + 1)].rearrange("p (m h) -> p m h", m=M + 1)
                    bias = dtb[:].unsqueeze(1).to_broadcast([P, M, HEADS])
                    step(dve.tensor_tensor(c.dt[:, 1:M + 1, :], dtp[:, 1:M + 1, :], bias, ALU.add))
                    dve.tensor_tensor(c.dt[0:META, 0, :], dtp[0:META, 0, :], dtb[0:META, :], ALU.add).then_inc(dt_raw, 1)
                    dve.wait_ge(dt_raw, 1)
                    step(dve.tensor_scalar(e2[:], c.dt[:], -1.0, None, ALU.mult))
                    dve.tensor_tensor(e1[:], e2[:], c.dt[:], ALU.max).then_inc(dt_raw, 1)

                def dt_finish():
                    dve.wait_ge(dt_l, 1)
                    step(dve.tensor_scalar(e1[:], e2[:], 1.0, None, ALU.add))
                    step(dve.tensor_scalar(e1[:], e1[:], -1.0, None, ALU.add))
                    step(dve.tensor_scalar(c.dta[:], e1[:], 0.0, None, ALU.is_equal))
                    step(dve.tensor_tensor(e1[:], e1[:], c.dta[:], ALU.add))
                    step(dve.tensor_tensor(e3[:], e3[:], c.dta[:], ALU.add))
                    step(dve.reciprocal(e1[:], e1[:]))
                    step(dve.tensor_tensor(e3[:], e3[:], e1[:], ALU.mult))
                    step(dve.tensor_tensor(e3[:], e3[:], e2[:], ALU.mult))
                    for n, m in ((META, slice(0, 1)), (P, slice(1, M + 1))):
                        step(dve.scalar_tensor_tensor(out=c.dt[0:n, m, :], in0=c.dt[0:n, m, :], scalar=0.0,
                                                      in1=e3[0:n, m, :], op0=ALU.max, op1=ALU.add))

                def short_conv(x):
                    dve.wait_ge(raw_in, x + 1)
                    if x >= 4:
                        dve.wait_ge(silu_out, x - 3)
                    y = acc[:, x % 4, :]
                    step(dve.tensor_scalar(y, raw[:, x % 4, 0:TA], xtaps[:, x, 0:1], xbias[:, x:x + 1],
                                           ALU.mult, ALU.add))
                    for k in range(1, CONV):
                        ins = dve.scalar_tensor_tensor(out=y, in0=raw[:, x % 4, k:k + TA], scalar=xtaps[:, x, k:k + 1],
                                                       in1=y, op0=ALU.mult, op1=ALU.add)
                        if k < CONV - 1:
                            step(ins)
                    ins.then_inc(conv_out[1], 1)

                for i in range(ROUNDS):
                    if i == 2:
                        dt_start()
                    if i == 3:
                        dt_finish()
                    dve.wait_ge(sig, i + 1)
                    dve.tensor_tensor(halves(gated[:, i % 2, pad:]), pair(jobs.index(("a", i))), halves(sg[:, i % 2, :]),
                                      ALU.mult).then_inc(g_ready, 1)
                    dve.wait_ge(g_ready, i + 1)
                    y = c.yT[:, KD + i, :]
                    step(dve.tensor_scalar(y, gated[:, i % 2, 0:T], taps[:, i, 0:1], cbias[:, i:i + 1],
                                           ALU.mult, ALU.add))
                    for k in range(1, CK):
                        step(dve.scalar_tensor_tensor(out=y, in0=gated[:, i % 2, k:k + T], scalar=taps[:, i, k:k + 1],
                                                      in1=y, op0=ALU.mult, op1=ALU.add))
                    if i >= 1:
                        short_conv(2 * i - 1)
                short_conv(2 * ROUNDS - 1)


def stage_conf_norm(nc, c, a):
    with Stage(nc, "cnorm") as s:
        sq = s.sb("sq", [P, KD, T])
        rstd = s.sb("rstd", [P, T])
        gam = s.sb("gam", [P, KD])
        bet = s.sb("bet", [P, KD])
        tot = s.ps("tot", [P, 2, T])
        consts_in = s.sem("consts_in")
        summed, centred, squared, var, root, chain, normed, done = (
            s.sem(n) for n in ("summed", "centred", "squared", "var", "root", "chain", "normed", "done"))
        with s.block() as block:

            @block.sync
            def _(sp):
                sp.dma_start(gam[:], a["conf_ln_g"]).then_inc(consts_in, 16)
                sp.dma_start(bet[:], a["conf_ln_b"]).then_inc(consts_in, 16)

            @block.tensor
            def _(pe):
                for i in range(KD):
                    mm = pe.matmul(tot[:, 0, :], c.ones[:], c.yT[:, KD + i, :], start=(i == 0), stop=(i == KD - 1))
                mm.then_inc(summed, 1)
                for i in range(KD):
                    pe.wait_ge(squared, i + 1)
                    mm = pe.matmul(tot[:, 1, :], c.ones[:], sq[:, i, :], start=(i == 0), stop=(i == KD - 1))
                mm.then_inc(summed, 1)

            @block.vector
            def _(dve):
                step = chained(dve, chain)
                dve.wait_ge(summed, 1)
                for i in range(KD):
                    y = c.yT[:, KD + i, :]
                    dve.scalar_tensor_tensor(out=y, in0=tot[:, 0, :], scalar=-1.0 / D, in1=y,
                                             op0=ALU.mult, op1=ALU.add).then_inc(centred, 1)
                dve.wait_ge(summed, 2)
                dve.tensor_scalar(rstd[:], tot[:, 1, :], 1.0 / D, EPS, ALU.mult, ALU.add).then_inc(var, 1)
                dve.wait_ge(root, 1)
                step(dve.reciprocal(rstd[:], rstd[:]))
                for i in range(KD):
                    y = c.yT[:, KD + i, :]
                    dve.tensor_tensor(y, y, rstd[:], ALU.mult).then_inc(normed, 1)

            @block.scalar
            def _(act):
                for i in range(KD):
                    act.wait_ge(centred, i + 1)
                    act.activation(sq[:, i, :], c.yT[:, KD + i, :], ACT.Square).then_inc(squared, 1)
                act.wait_ge(var, 1)
                act.activation(rstd[:], rstd[:], ACT.Sqrt).then_inc(root, 1)
                act.wait_ge(consts_in, 32)
                for i in range(KD):
                    act.wait_ge(normed, i + 1)
                    y = c.yT[:, KD + i, :]
                    act.activation(y, y, ACT.Silu, scale=gam[:, i:i + 1], bias=bet[:, i:i + 1]).then_inc(done, 1)


def stage_ssd(nc, c, a):
    CH = M + 1
    with Stage(nc, "ssd") as s:
        alog = s.sb("alog", [P, HEADS])
        dsk = s.sb("dsk", [P, KD])
        nw = s.sb("nw", [P, KD])
        acs = s.sb("acs", [P, CH, HEADS])
        keep = s.sb("keep", [P, CH, HEADS])
        dec = s.sb("dec", [P, CH, HEADS])
        xdt = s.sb("xdt", [P, HEADS, 64])
        xw = s.sb("xw", [P, HEADS, 64])
        btok = s.sb("btok", [P, GROUPS, P])
        state = s.sb("state", [P, HEADS, 64])
        lmat = s.sb("lmat", [P, 2, 4, P])
        cw = s.sb("cw", [P, 2, 4, P])
        cbm = s.sb("cbm", [P, 2, P])
        sq = s.sb("sq", [P, KD, T])
        rstd = s.sb("rstd", [P, GROUPS, T])
        X = s.ps("X", [P, 2, 512])
        A_ = s.ps("A", [P, 512])
        R = s.ps("R", [P, 2, 4, P])
        CB = s.ps("CB", [P, 4, P])
        Y = s.ps("Y", [P, 2, 512])
        consts_in = s.sem("consts_in")
        aneg, dta_ok, cs_done, cs_ok, w_exp, chain, dve_w = (
            s.sem(n) for n in ("aneg", "dta_ok", "cs_done", "cs_ok", "w_exp", "chain", "dve_w"))
        x_turned, b_turned, b_taken, xdt_ok, xw_ok = (
            s.sem(n) for n in ("x_turned", "b_turned", "b_taken", "xdt_ok", "xw_ok"))
        r_done, e_ok, e_exp, q_exp, w_ok = (s.sem(n) for n in ("r_done", "e_ok", "e_exp", "q_exp", "w_ok"))
        y_done, y_taken, st_done, s_ok = (s.sem(n) for n in ("y_done", "y_taken", "st_done", "s_ok"))
        squared, sums, var, root = (s.sem(n) for n in ("squared", "sums", "var", "root"))

        def cols(ch):
            return (0, META) if ch == 0 else (META + (ch - 1) * P, P)

        with s.block() as block:

            @block.sync
            def _(sp):
                sp.dma_start(alog[:], a["ssd_A_log"].to_broadcast([P, HEADS])).then_inc(consts_in, 16)
                sp.dma_start(dsk[:], a["ssd_D"]).then_inc(consts_in, 16)
                sp.dma_start(nw[:], a["ssd_norm_w"]).then_inc(consts_in, 16)

            @block.tensor
            def _(pe):
                pe.wait_ge(dta_ok, 1)
                dta = c.dta[:].rearrange("p c h -> p (c h)")
                pe.matmul(A_[:, 0:CH * HEADS], c.upper[:], dta, start=True, stop=True)
                pe.matmul(A_[:, 128:128 + CH * HEADS], c.ones[:], dta, start=True, stop=True).then_inc(cs_done, 1)

                def turn(ch):
                    at, n = cols(ch)
                    if ch > 0:
                        pe.wait_ge(s_ok, ch)
                    for h in range(2):
                        for k in range(4):
                            t = pe.transpose(X[0:n, h, k * P:(k + 1) * P], c.xbcT[:, 4 * h + k, at:at + n], c.ident[:])
                        t.then_inc(x_turned, 1)
                    if ch == M:
                        return
                    pe.wait_ge(cs_ok, 1) if ch == 0 else pe.wait_ge(b_taken, ch)
                    for g in range(GROUPS):
                        t = pe.transpose(A_[0:n, g * P:(g + 1) * P], c.xbcT[:, XT + g, at:at + n], c.ident[:])
                    t.then_inc(b_turned, 1)

                def new_state(ch):
                    n = cols(ch)[1]
                    pe.wait_ge(xw_ok, ch + 1)
                    pe.wait_ge(b_taken, ch + 1)
                    for g in range(GROUPS):
                        mm = pe.matmul(X[:, g // 2, (g % 2) * 256:(g % 2) * 256 + 256], btok[0:n, g, :],
                                       xw[0:n, 4 * g:4 * g + 4, :].rearrange("p h d -> p (h d)"), start=True, stop=True)
                    mm.then_inc(st_done, 1)

                def decays(n):
                    ch, g = n // 4 + 1, n % 4
                    at, _ = cols(ch)
                    if n >= 2:
                        pe.wait_ge(e_ok, n - 1)
                        pe.wait_ge(q_exp, n - 1)
                        pe.wait_ge(w_ok, n - 1)
                    for r in range(4):
                        pe.matmul(R[:, n % 2, r, :], c.dta[:, ch, 4 * g + r:4 * g + r + 1].to_broadcast([P, P]),
                                  c.upper[:], start=True, stop=True)
                    if n >= 1:
                        pe.wait_ge(dve_w, n)
                    pe.matmul(CB[:, n % 2, :], c.xbcT[:, XT + g, at:at + P], c.xbcT[:, XT + 4 + g, at:at + P],
                              start=True, stop=True).then_inc(r_done, 1)

                turn(0)
                new_state(0)
                turn(1)
                decays(0)
                for n in range(16):
                    ch, g = n // 4 + 1, n % 4
                    if n + 1 < 16:
                        decays(n + 1)
                    pe.wait_ge(w_ok, n + 1)
                    pe.wait_ge(xdt_ok, ch + 1)
                    pe.wait_ge(s_ok, ch)
                    if n >= 2:
                        pe.wait_ge(y_taken, n - 1)
                    for r in range(4):
                        h = 4 * g + r
                        out = Y[64 * (r % 2):64 * (r % 2) + 64, n % 2, (r // 2) * P:(r // 2) * P + P]
                        pe.matmul(out, xdt[:, h, :], lmat[:, n % 2, r, :], start=True, stop=False)
                        mm = pe.matmul(out, state[:, h, :], cw[:, n % 2, r, :], start=False, stop=True)
                    mm.then_inc(y_done, 1)
                    if g == 3 and ch < M:
                        new_state(ch)
                        turn(ch + 1)
                for g in range(GROUPS):
                    pe.wait_ge(squared, g + 1)
                    pe.wait_ge(y_taken, 16)
                    if g >= 2:
                        pe.wait_ge(var, g - 1)
                    for k in range(2):
                        mm = pe.matmul(Y[:, g % 2, :], c.ones[:], sq[:, 2 * g + k, :], start=(k == 0), stop=(k == 1))
                    mm.then_inc(sums, 1)

            @block.scalar
            def _(act):
                act.wait_ge(consts_in, 48)
                act.activation(alog[:], alog[:], ACT.Exp).then_inc(aneg, 1)
                act.wait_ge(cs_ok, 2)
                act.activation(keep[:], keep[:], ACT.Exp).then_inc(w_exp, 1)
                act.activation(dec[:], dec[:], ACT.Exp).then_inc(w_exp, 1)

                def take_b(ch):
                    n = cols(ch)[1]
                    act.wait_ge(b_turned, ch + 1)
                    act.activation(btok[0:n, :, :], A_[0:n, :].rearrange("p (g n) -> p g n", g=GROUPS),
                                   ACT.Copy).then_inc(b_taken, 1)

                take_b(0)
                take_b(1)
                for n in range(16):
                    act.wait_ge(r_done, n + 1)
                    if n >= 2:
                        act.wait_ge(y_done, n - 1)
                    act.activation(cw[:, n % 2, :, :], R[:, n % 2, :, :], ACT.Exp).then_inc(q_exp, 1)
                    act.wait_ge(e_ok, n + 1)
                    act.activation(lmat[:, n % 2, :, :], lmat[:, n % 2, :, :], ACT.Exp).then_inc(e_exp, 1)
                    if n % 4 == 0 and 1 < n // 4 + 1 < M:
                        take_b(n // 4 + 1)
                for g in range(GROUPS):
                    act.wait_ge(y_taken, 16)
                    act.activation(sq[:, 2 * g:2 * g + 2, :], c.yT[:, 2 * g:2 * g + 2, :], ACT.Square).then_inc(squared, 1)
                act.wait_ge(var, GROUPS)
                act.activation(rstd[:], rstd[:], ACT.Sqrt).then_inc(root, 1)

            @block.vector
            def _(dve):
                step = chained(dve, chain)
                dve.wait_ge(aneg, 1)
                dve.scalar_tensor_tensor(out=c.dta[:], in0=c.dt[:], scalar=-1.0,
                                         in1=alog[:].unsqueeze(1).to_broadcast([P, CH, HEADS]),
                                         op0=ALU.mult, op1=ALU.mult).then_inc(dta_ok, 1)
                dve.wait_ge(cs_done, 1)
                n_ = CH * HEADS
                step(dve.tensor_copy(acs[:].rearrange("p c h -> p (c h)"), A_[:, 0:n_]))
                step(dve.tensor_copy(dec[:].rearrange("p c h -> p (c h)"), A_[:, 128:128 + n_]))
                dve.tensor_tensor(keep[:], dec[:], acs[:], ALU.subtract).then_inc(cs_ok, 2)
                dve.wait_ge(w_exp, 2)

                def take_x(ch):
                    n = cols(ch)[1]
                    for h in range(2):
                        dve.wait_ge(x_turned, 2 * ch + h + 1)
                        ins = dve.tensor_tensor(xdt[0:n, 8 * h:8 * h + 8, :],
                                                X[0:n, h, :].rearrange("p (h d) -> p h d", h=8),
                                                c.dt[0:n, ch, 8 * h:8 * h + 8].unsqueeze(2).to_broadcast([n, 8, 64]), ALU.mult)
                        if h == 0:
                            step(ins)
                    ins.then_inc(xdt_ok, 1)
                    dve.wait_ge(xdt_ok, ch + 1)
                    dve.tensor_tensor(xw[0:n, :, :], xdt[0:n, :, :],
                                      keep[0:n, ch, :].unsqueeze(2).to_broadcast([n, HEADS, 64]), ALU.mult).then_inc(xw_ok, 1)

                def take_state(ch):
                    dve.wait_ge(st_done, ch + 1)
                    new = X[:].rearrange("p b (h d) -> p (b h) d", d=64)
                    if ch == 0:
                        dve.tensor_copy(state[:], new).then_inc(s_ok, 1)
                        return
                    step(dve.tensor_tensor(state[:], state[:], dec[:, ch, :].unsqueeze(2).to_broadcast([P, HEADS, 64]),
                                           ALU.mult))
                    dve.tensor_tensor(state[:], state[:], new, ALU.add).then_inc(s_ok, 1)

                def prepare(n):
                    ch, g = n // 4 + 1, n % 4
                    at, _ = cols(ch)
                    dve.wait_ge(r_done, n + 1)
                    if n >= 2:
                        dve.wait_ge(y_done, n - 1)
                    dve.tensor_tensor(cbm[:, n % 2, :], CB[:, n % 2, :], c.upper[:], ALU.mult).then_inc(dve_w, 1)
                    dve.wait_ge(q_exp, n + 1)
                    for r in range(4):
                        h = 4 * g + r
                        ins = dve.tensor_scalar(lmat[:, n % 2, r, :], R[:, n % 2, r, :], acs[:, ch, h:h + 1], 0.0,
                                                ALU.subtract, ALU.min)
                    ins.then_inc(e_ok, 1)
                    dve.tensor_tensor(cw[:, n % 2, :, :], cw[:, n % 2, :, :],
                                      c.xbcT[:, XT + 4 + g, at:at + P].unsqueeze(1).to_broadcast([P, 4, P]), ALU.mult)
                    dve.wait_ge(e_exp, n + 1)
                    dve.wait_ge(dve_w, n + 1)
                    dve.tensor_tensor(lmat[:, n % 2, :, :], lmat[:, n % 2, :, :],
                                      cbm[:, n % 2, :].unsqueeze(1).to_broadcast([P, 4, P]), ALU.mult).then_inc(w_ok, 1)

                take_x(0)
                take_state(0)
                take_x(1)
                prepare(0)
                for n in range(16):
                    ch, g = n // 4 + 1, n % 4
                    at, _ = cols(ch)
                    if n + 1 < 16:
                        prepare(n + 1)
                    dve.wait_ge(y_done, n + 1)
                    for k in range(2):
                        j = 2 * g + k
                        ins = dve.scalar_tensor_tensor(out=c.yT[:, j, at - META:at - META + P],
                                                       in0=c.xbcT[:, j, at:at + P], scalar=dsk[:, j:j + 1],
                                                       in1=Y[:, n % 2, k * P:k * P + P], op0=ALU.mult, op1=ALU.add)
                    step(ins)
                    y = c.yT[:, 2 * g:2 * g + 2, at - META:at - META + P]
                    dve.tensor_tensor(y, y, c.zT[:, 2 * g:2 * g + 2, at - META:at - META + P],
                                      ALU.mult).then_inc(y_taken, 1)
                    if g == 3 and ch < M:
                        take_state(ch)
                        take_x(ch + 1)
                for g in range(GROUPS):
                    dve.wait_ge(sums, g + 1)
                    dve.tensor_scalar(rstd[:, g, :], Y[:, g % 2, :], 1.0 / 256, EPS, ALU.mult, ALU.add).then_inc(var, 1)
                dve.wait_ge(root, 1)
                step(dve.reciprocal(rstd[:], rstd[:]))
                for j in range(KD):
                    dve.scalar_tensor_tensor(out=c.yT[:, j, :], in0=c.yT[:, j, :], scalar=nw[:, j:j + 1],
                                             in1=rstd[:, j // 2, :], op0=ALU.mult, op1=ALU.mult).then_inc(chain, 1)


def stage_out_proj(nc, c, a, name, yT, w_dram, kt, resid, resid_scale, bias=None):
    RAW, RING = 4, 3
    with Stage(nc, name) as s:
        w = s.sb("w", [P, RAW, 2, D])
        w_hi = s.sb("w_hi", [P, RING, 2, D], F32R)
        w_lo = s.sb("w_lo", [P, RING, 2, D], F32R)
        y_hi = s.sb("y_hi", [P, RING, 2, T], F32R)
        y_lo = s.sb("y_lo", [P, RING, 2, T], F32R)
        acc = s.ps("acc", [P, M, 2, 512])
        bb = s.sb("bb", [P, D]) if bias is not None else None
        loaded = [s.sem(f"loaded{b}") for b in range(RAW)]
        res_in, bias_in, used, done, y_high, w_high, y_low, w_low, chain = (s.sem(n) for n in (
            "res_in", "bias_in", "used", "done", "y_high", "w_high", "y_low", "w_low", "chain"))
        pairs = kt // 2
        with s.block() as block:

            @block.sync
            def _(sp):
                for q in range(pairs):
                    if q >= RAW:
                        sp.wait_ge(w_low, q - RAW + 1)
                    sp.dma_start(w[:, q % RAW, :, :], rows(w_dram)[:, 2 * q:2 * q + 2, :]).then_inc(loaded[q % RAW], 16)
                    if q == RAW - 1:
                        if resid is not None:
                            sp.dma_start(c.h[:], tokens(resid)).then_inc(res_in, 16)
                        if bias is not None:
                            sp.dma_start(bb[:], bias.to_broadcast([P, D])).then_inc(bias_in, 16)

            @block.scalar
            def _(act):
                for q in range(pairs):
                    if q >= RING:
                        act.wait_ge(used, q - RING + 1)
                    act.activation(y_hi[:, q % RING, :, :], yT[:, 2 * q:2 * q + 2, :], ACT.Copy).then_inc(y_high, 1)
                    act.wait_ge(loaded[q % RAW], 16 * (q // RAW + 1))
                    act.activation(w_hi[:, q % RING, :, :], w[:, q % RAW, :, :], ACT.Copy).then_inc(w_high, 1)

            @block.tensor
            def _(pe):
                for q in range(pairs):
                    r = q % RING
                    pe.wait_ge(y_low, q + 1)
                    pe.wait_ge(w_low, q + 1)
                    for m in range(M):
                        for n in range(2):
                            out, cols = acc[:, m, n, :], slice(n * 512, n * 512 + 512)
                            for j in range(2):
                                k = 2 * q + j
                                hi, lo = y_hi[:, r, j, m * P:m * P + P], y_lo[:, r, j, m * P:m * P + P]
                                pe.matmul(out, hi, w_hi[:, r, j, cols], start=(k == 0), stop=False)
                                pe.matmul(out, hi, w_lo[:, r, j, cols], start=False, stop=False)
                                mm = pe.matmul(out, lo, w_hi[:, r, j, cols], start=False, stop=(k == kt - 1))
                            if q == pairs - 1:
                                mm.then_inc(done, 1)
                    if q < pairs - 1:
                        mm.then_inc(used, 1)

            @block.vector
            def _(dve):
                step = chained(dve, chain)
                for q in range(pairs):
                    r = q % RING
                    dve.wait_ge(y_high, q + 1)
                    dve.tensor_tensor(y_lo[:, r, :, :], yT[:, 2 * q:2 * q + 2, :], y_hi[:, r, :, :].bitcast(F32),
                                      ALU.subtract).then_inc(y_low, 1)
                    dve.wait_ge(w_high, q + 1)
                    dve.tensor_tensor(w_lo[:, r, :, :], w[:, q % RAW, :, :], w_hi[:, r, :, :].bitcast(F32),
                                      ALU.subtract).then_inc(w_low, 1)
                if resid is not None:
                    dve.wait_ge(res_in, 16)
                if bias is not None:
                    dve.wait_ge(bias_in, 16)
                for m in range(M):
                    for n in range(2):
                        dve.wait_ge(done, 2 * m + n + 1)
                        out = c.h[:, m, n * 512:n * 512 + 512]
                        step(dve.scalar_tensor_tensor(out=out, in0=out, scalar=resid_scale, in1=acc[:, m, n, :],
                                                      op0=ALU.mult, op1=ALU.add))
                        if bias is not None:
                            step(dve.tensor_tensor(out, out, bb[:, n * 512:n * 512 + 512], ALU.add))


def stage_token_norm(nc, c, a, name, dst, dstT=None, centre=False, norm=True, row_w=None, row_b=None, col_w=None,
                     save=None):
    src = c.h
    with Stage(nc, name) as s:
        junk = s.sb("junk", [P, 2, D])
        rw = s.sb("rw", [P, D]) if row_w is not None else None
        rb = s.sb("rb", [P, D]) if row_b is not None else None
        cwt = s.sb("cwt", [P, KD]) if col_w is not None else None
        stat = s.sb("stat", [P, 2, M])
        tp = s.ps("tp", [P, 4, 4, P])
        (w_in, summed, meaned, centred, squared, var, root, inv, scaled, turned, copied, saved, chain) = (
            s.sem(n) for n in ("w_in", "summed", "meaned", "centred", "squared", "var", "root", "inv", "scaled",
                               "turned", "copied", "saved", "chain"))
        n_w = 16 * sum(v is not None for v in (row_w, row_b, col_w))
        with s.block() as block:

            @block.sync
            def _(sp):
                if row_w is not None:
                    sp.dma_start(rw[:], row_w.to_broadcast([P, D])).then_inc(w_in, 16)
                if row_b is not None:
                    sp.dma_start(rb[:], row_b.to_broadcast([P, D])).then_inc(w_in, 16)
                if col_w is not None:
                    sp.dma_start(cwt[:], col_w).then_inc(w_in, 16)
                if save is not None:
                    for m in range(M):
                        sp.wait_ge(scaled, m + 1)
                        sp.dma_start(tokens(save)[:, m, :], dst[:, m, :]).then_inc(saved, 16)
                    sp.wait_ge(saved, 16 * M)

            @block.scalar
            def _(act):
                if not norm:
                    return
                if centre:
                    for m in range(M):
                        act.activation(junk[:, m % 2, :], src[:, m, :], ACT.Copy, accum_out=stat[:, 0, m:m + 1]).then_inc(summed, 1)
                        act.wait_ge(summed, m + 1)
                for m in range(M):
                    if centre:
                        act.wait_ge(centred, m + 1)
                    act.activation(junk[:, m % 2, :], dst[:, m, :] if centre else src[:, m, :], ACT.Square,
                                   accum_out=stat[:, 1, m:m + 1]).then_inc(squared, 1)
                    act.wait_ge(squared, m + 1)
                act.wait_ge(var, 1)
                act.activation(stat[:, 1, :], stat[:, 1, :], ACT.Sqrt).then_inc(root, 1)

            @block.vector
            def _(dve):
                step = chained(dve, chain)
                if norm:
                    if centre:
                        dve.wait_ge(summed, M)
                        step(dve.tensor_scalar(stat[:, 0, :], stat[:, 0, :], 1.0 / D, None, ALU.mult))
                        for m in range(M):
                            dve.tensor_scalar(dst[:, m, :], src[:, m, :], stat[:, 0, m:m + 1], None,
                                              ALU.subtract).then_inc(centred, 1)
                    dve.wait_ge(squared, M)
                    dve.tensor_scalar(stat[:, 1, :], stat[:, 1, :], 1.0 / D, EPS, ALU.mult, ALU.add).then_inc(var, 1)
                    dve.wait_ge(root, 1)
                    step(dve.reciprocal(stat[:, 1, :], stat[:, 1, :]))
                if n_w:
                    dve.wait_ge(w_in, n_w)
                for m in range(M if norm else 0):
                    x = (dst if centre else src)[:, m, :]
                    if rw is None:
                        dve.tensor_scalar(dst[:, m, :], x, stat[:, 1, m:m + 1], None, ALU.mult).then_inc(scaled, 1)
                    else:
                        ins = dve.scalar_tensor_tensor(out=dst[:, m, :], in0=x, scalar=stat[:, 1, m:m + 1], in1=rw[:],
                                                       op0=ALU.mult, op1=ALU.mult)
                        if rb is not None:
                            step(ins)
                            ins = dve.tensor_tensor(dst[:, m, :], dst[:, m, :], rb[:], ALU.add)
                        ins.then_inc(scaled, 1)
                if dstT is None:
                    return
                for i in range(2 * M):
                    m, h = i // 2, i % 2
                    dve.wait_ge(turned, i + 1)
                    out = dstT[:, 4 * h:4 * h + 4, m * P:m * P + P]
                    if cwt is not None:
                        ins = dve.tensor_tensor(out, tp[:, i % 4, :, :],
                                                cwt[:, 4 * h:4 * h + 4].unsqueeze(2).to_broadcast([P, 4, P]), ALU.mult)
                    else:
                        ins = dve.tensor_copy(out, tp[:, i % 4, :, :])
                    ins.then_inc(copied, 1)

            @block.tensor
            def _(pe):
                if dstT is None:
                    return
                for i in range(2 * M):
                    m, h = i // 2, i % 2
                    if h == 0 and norm:
                        pe.wait_ge(scaled, m + 1)
                    if i >= 4:
                        pe.wait_ge(copied, i - 3)
                    for k in range(4):
                        t = pe.transpose(tp[:, i % 4, k, :], dst[:, m, (4 * h + k) * P:(4 * h + k + 1) * P], c.ident[:])
                    t.then_inc(turned, 1)


NQ = 2 * PH
G = 4
GROUPS_ALL = NK // G
EARLY = 8


def stage_queries(nc, c, a):
    with Stage(nc, "query") as s:
        w = s.sb("w", [P, 2, KD, 512])
        w_hi = s.sb("w_hi", [P, KD, 512], F32R)
        w_lo = s.sb("w_lo", [P, KD, 512], F32R)
        q_ps = s.ps("q_ps", [P, 4, 512])
        w_in = [s.sem(f"w_in{b}") for b in range(2)]
        q_done, q_taken, high, low = (s.sem(n) for n in ("q_done", "q_taken", "high", "low"))
        wq = rows(a["peer_w_query"][0])

        def cols(t, n):
            return t[:, :, (n % 4) * P:(n % 4) * P + P]

        with s.block() as block:

            @block.sync
            def _(sp):
                for n in range(NQ // 4):
                    if n >= 2:
                        sp.wait_ge(low, 4 * (n - 1))
                    sp.dma_start(w[:, n % 2, :, :], wq[:, :, n * 512:n * 512 + 512]).then_inc(w_in[n % 2], 16)

            @block.scalar
            def _(act):
                def split(n):
                    act.wait_ge(w_in[n // 4 % 2], 16 * (n // 8 + 1))
                    if n >= 4:
                        act.wait_ge(q_done, n - 3)
                    act.activation(cols(w_hi, n), cols(w[:, n // 4 % 2, :, :], n), ACT.Copy).then_inc(high, 1)

                for n in range(4):
                    split(n)
                for n in range(NQ):
                    act.wait_ge(q_done, n + 1)
                    act.activation(c.qT[:, n, :], q_ps[:, n % 4, :], ACT.Copy).then_inc(q_taken, 1)
                    if n + 4 < NQ:
                        split(n + 4)

            @block.vector
            def _(dve):
                for n in range(NQ):
                    dve.wait_ge(high, n + 1)
                    dve.tensor_tensor(cols(w_lo, n), cols(w[:, n // 4 % 2, :, :], n), cols(w_hi, n).bitcast(F32),
                                      ALU.subtract).then_inc(low, 1)

            @block.tensor
            def _(pe):
                for n in range(NQ):
                    pe.wait_ge(low, n + 1)
                    if n >= 4:
                        pe.wait_ge(q_taken, n - 3)
                    for k in range(KD):
                        hi, lo = cols(w_hi, n)[:, k, :], cols(w_lo, n)[:, k, :]
                        pe.matmul(q_ps[:, n % 4, :], hi, c.x_hi[:, k, :], start=(k == 0), stop=False)
                        pe.matmul(q_ps[:, n % 4, :], hi, c.x_lo[:, k, :], start=False, stop=False)
                        mm = pe.matmul(q_ps[:, n % 4, :], lo, c.x_hi[:, k, :], start=False, stop=(k == KD - 1))
                    mm.then_inc(q_done, 1)


def stage_peer_scores(nc, c, a):
    PER = EARLY * G // M
    with Stage(nc, "score") as s:
        wd = c.hT
        wd_hi = s.sb("wd_hi", [P, KD, G * P], F32R)
        wd_lo = s.sb("wd_lo", [P, KD, G * P], F32R)
        stash = s.sb("stash", [P, 2, G, T])
        keysT = s.sb("keysT", [P, NQ, NK])
        S = s.sb("S", [P, 2, NQ, NK])
        v = s.sb("v", [P, NQ, TOPK])
        iu = s.sb("iu", [P, NQ, TOPK], U32)
        fi = s.sb("fi", [P, NQ, TOPK])
        cand = s.sb("cand", [P, PH, TOPK * TOPK])
        best = s.sb("best", [P, PH, TOPK])
        pos = s.sb("pos", [P, PH, TOPK], U32)
        hi = s.sb("hi", [P, PH, TOPK], U32)
        posf = s.sb("posf", [P, 2, PH, TOPK])
        gate = s.sb("gate", [P, PH, TOPK])
        total = s.sb("total", [P, PH])
        eq = s.sb("eq", [P, PH, TOPK, TOPK])
        pick = s.sb("pick", [P, 3, PH * TOPK])
        H = s.ps("H", [P, 2, T])
        s_ps = s.ps("s_ps", [P, 4, 4, NK])
        t_ps = s.ps("t_ps", [P, 4, P])
        stashed = [s.sem(f"stashed{b}") for b in range(2)]
        wd_in, wd_h, wd_l, h_done, gelued = (s.sem(n) for n in ("wd_in", "wd_h", "wd_l", "h_done", "gelued"))
        (keys_in, s_done, s_taken, s_used, chain, centred, exped, picks, turned, copied) = (
            s.sem(n) for n in ("keys_in", "s_done", "s_taken", "s_used", "chain", "centred",
                               "exped", "picks", "turned", "copied"))
        wd_d = rows(a["peer_w_downT"])
        LOW = -3.0e38

        def tile(w, t):
            return w[:, :, t % G * P:(t % G + 1) * P]

        with s.block() as block:

            @block.sync
            def _(sp):
                def save(g):
                    sp.wait_ge(gelued, G * g + G)
                    sp.dma_start(c.early[g], stash[:, g % 2, :, :].rearrange("p j t -> p (j t)")).then_inc(stashed[g % 2], 16)

                sp.dma_start(keysT[:], a["peer_keysT"]).then_inc(keys_in, 16)
                for g in range(EARLY):
                    if g >= 1:
                        sp.wait_ge(wd_l, G * g)
                    sp.dma_start(wd[:], wd_d[:, :, g * G * P:(g + 1) * G * P]).then_inc(wd_in, 16)
                    if g >= 1:
                        save(g - 1)
                save(EARLY - 1)
                for b in range(2):
                    sp.wait_ge(stashed[b], 16 * (EARLY // 2))

            @block.gpsimd
            def _(pool):
                for t in range(EARLY * G):
                    pool.wait_ge(wd_h, t + 1)
                    pool.tensor_tensor(tile(wd_lo, t), tile(wd, t), tile(wd_hi, t).bitcast(F32),
                                       ALU.subtract).then_inc(wd_l, 1)

            @block.tensor
            def _(pe):
                pe.wait_ge(keys_in, 16)

                def early(t):
                    pe.wait_ge(wd_l, t + 1)
                    if t >= 2:
                        pe.wait_ge(gelued, t - 1)
                    for k in range(KD):
                        hi, lo = tile(wd_hi, t)[:, k, :], tile(wd_lo, t)[:, k, :]
                        pe.matmul(H[:, t % 2, :], hi, c.x_hi[:, k, :], start=(k == 0), stop=False)
                        pe.matmul(H[:, t % 2, :], hi, c.x_lo[:, k, :], start=False, stop=False)
                        mm = pe.matmul(H[:, t % 2, :], lo, c.x_hi[:, k, :], start=False, stop=(k == KD - 1))
                    mm.then_inc(h_done, 1)

                def scores(m):
                    for b in range(4):
                        if m >= 1:
                            pe.wait_ge(s_taken, 4 * (m - 1) + b + 1)
                        for j in range(4):
                            n = 4 * b + j
                            mm = pe.matmul(s_ps[:, b, j, :], c.qT[:, n, m * P:m * P + P], keysT[:, n, :],
                                           start=True, stop=True)
                        mm.then_inc(s_done, 1)

                scores(0)
                scores(1)
                for m in range(M):
                    for t in range(PER * m, PER * m + PER):
                        early(t)
                    pe.wait_ge(picks, m + 1)
                    if m >= 1:
                        pe.wait_ge(copied, m)
                    for j in range(3):
                        t = pe.transpose(t_ps[:, j, :], pick[:, j, :], c.ident[:])
                    t.then_inc(turned, 1)
                    if m + 2 < M:
                        scores(m + 2)

            @block.scalar
            def _(act):
                def split(t):
                    act.wait_ge(wd_in, 16 * (t // G + 1))
                    act.activation(tile(wd_hi, t), tile(wd, t), ACT.Copy).then_inc(wd_h, 1)

                def early(t):
                    g = t // G
                    if g >= 2 and t % G == 0:
                        act.wait_ge(stashed[g % 2], 16 * (g // 2))
                    act.wait_ge(h_done, t + 1)
                    act.activation(stash[:, g % 2, t % G, :], H[:, t % 2, :], ACT.Gelu).then_inc(gelued, 1)
                    if t + G < EARLY * G:
                        split(t + G)

                def take(m):
                    if m >= 2:
                        act.wait_ge(s_used, m - 1)
                    for b in range(4):
                        act.wait_ge(s_done, 4 * m + b + 1)
                        act.activation(S[:, m % 2, 4 * b:4 * b + 4, :], s_ps[:, b, :, :], ACT.Copy).then_inc(s_taken, 1)

                take(0)
                for t in range(G):
                    split(t)
                for m in range(M):
                    if m + 1 < M:
                        take(m + 1)
                    for t in range(PER * m, PER * m + PER - 2):
                        early(t)
                    act.wait_ge(centred, m + 1)
                    act.activation(gate[:], gate[:], ACT.Exp).then_inc(exped, 1)
                    for t in range(PER * m + PER - 2, PER * m + PER):
                        early(t)
                    act.wait_ge(turned, m + 1)
                    act.activation(c.idxT[:, :, m * P:m * P + P], t_ps[:, 0:3, :], ACT.Copy).then_inc(copied, 1)

            @block.vector
            def _(dve):
                step = chained(dve, chain)

                def top16(values, vals, idx, n):
                    for half in range(2):
                        o = slice(8 * half, 8 * half + 8)
                        for r in range(n):
                            ins = dve.max(vals[:, r, o], values[:, r, :])
                        step(ins)
                        for r in range(n):
                            ins = dve.max_index(idx[:, r, o], vals[:, r, o], values[:, r, :])
                        step(ins)
                        if half == 0:
                            for r in range(n):
                                ins = dve.match_replace(out=values[:, r, :], in_to_replace=vals[:, r, o],
                                                        in_values=values[:, r, :], imm_value=LOW)
                            step(ins)

                for m in range(M):
                    dve.wait_ge(s_taken, 4 * m + 4)
                    top16(S[:, m % 2, :, :], v, iu, NQ)
                    dve.tensor_copy(fi[:], iu[:]).then_inc(s_used, 1)
                    dve.wait_ge(s_used, m + 1)
                    halves = v[:].rearrange("p (h two) k -> p h two k", two=2)
                    step(dve.tensor_tensor(cand[:].rearrange("p h (i j) -> p h i j", i=TOPK),
                                           halves[:, :, 0, :].unsqueeze(3).to_broadcast([P, PH, TOPK, TOPK]),
                                           halves[:, :, 1, :].unsqueeze(2).to_broadcast([P, PH, TOPK, TOPK]), ALU.add))
                    top16(cand, best, pos, PH)
                    dve.tensor_tensor(gate[:], best[:], best[:, :, 0:1].to_broadcast([P, PH, TOPK]),
                                      ALU.subtract).then_inc(centred, 1)
                    step(dve.tensor_scalar(hi[:], pos[:], 4, None, ALU.logical_shift_right))
                    step(dve.tensor_copy(posf[:, 0, :, :], hi[:]))
                    step(dve.tensor_scalar(hi[:], pos[:], 15, None, ALU.bitwise_and))
                    step(dve.tensor_copy(posf[:, 1, :, :], hi[:]))
                    fih = fi[:].rearrange("p (h two) k -> p h two k", two=2)
                    if m >= 1:
                        dve.wait_ge(turned, m)
                    for half in range(2):
                        step(dve.tensor_tensor(eq[:].rearrange("p h k i -> p (h k) i"),
                                               posf[:, half, :, :].rearrange("p h k -> p (h k)").unsqueeze(2).to_broadcast([P, PH * TOPK, TOPK]),
                                               c.count[:, 0:TOPK].unsqueeze(1).to_broadcast([P, PH * TOPK, TOPK]),
                                               ALU.is_equal))
                        step(dve.tensor_tensor(eq[:], eq[:],
                                               fih[:, :, half, :].unsqueeze(2).to_broadcast([P, PH, TOPK, TOPK]), ALU.mult))
                        step(dve.tensor_reduce(pick[:, half, :], eq[:].rearrange("p h k i -> p (h k) i"), AX.X, ALU.add))
                    dve.wait_ge(exped, m + 1)
                    step(dve.tensor_reduce(total[:], gate[:], AX.X, ALU.add))
                    step(dve.reciprocal(total[:], total[:]))
                    dve.tensor_tensor(pick[:, 2, :].rearrange("p (h k) -> p h k", h=PH), gate[:],
                                      total[:].unsqueeze(2).to_broadcast([P, PH, TOPK]), ALU.mult).then_inc(picks, 1)
                    dve.wait_ge(picks, m + 1)


TB = 64
BATCHES = T // TB


def stage_gate_matrix(nc, c, a):
    U = 4
    R = 4
    with Stage(nc, "gates") as s:
        hot = s.sb("hot", [P, R, 2, U, NK])
        out = s.sb("out", [P, 2, NK, TB])
        ps = s.ps("ps", [P, R, U, NK])
        (marked, weighed, g_done, taken) = (s.sem(n) for n in ("marked", "weighed", "g_done", "taken"))
        saved = [s.sem(f"saved{b}") for b in range(2)]
        per = TB // (R * U)
        with s.block() as block:

            @block.vector
            def _(dve):
                shape = [P, 2, U, NK]
                with dve.Fori(0, T // (R * U)) as it:
                    for u in range(R):
                        dve.wait_ge(g_done, it * R + (u + 1))
                        dve.tensor_tensor(hot[:, u, :, :, :], c.count[:].unsqueeze(1).unsqueeze(1).to_broadcast(shape),
                                          c.idxT[:, 0:2, ds(it * (R * U) + u * U, U)].unsqueeze(3).to_broadcast(shape),
                                          ALU.is_equal).then_inc(marked, 1)

            @block.gpsimd
            def _(pool):
                with pool.Fori(0, T // (R * U)) as it:
                    for u in range(R):
                        at = pool.snap(it * (R * U) + u * U)
                        pool.wait_ge(marked, it * R + (u + 1))
                        pool.tensor_tensor(hot[:, u, 0, :, :], hot[:, u, 0, :, :],
                                           c.idxT[:, 2, ds(at, U)].unsqueeze(2).to_broadcast([P, U, NK]),
                                           ALU.mult).then_inc(weighed, 1)

            @block.tensor
            def _(pe):
                pe.sem_inc(g_done, R)
                with pe.Fori(0, T // (R * U)) as it:
                    for u in range(R):
                        pe.wait_ge(weighed, it * R + (u + 1))
                        pe.wait_ge(taken, it * R + (u + 1))
                        for j in range(U):
                            mm = pe.matmul(ps[:, u, j, :], hot[:, u, 1, j, :], hot[:, u, 0, j, :], start=True, stop=True)
                        mm.then_inc(g_done, 1)

            @block.scalar
            def _(act):
                act.sem_inc(taken, R)
                for b in range(BATCHES):
                    if b >= 2:
                        act.wait_ge(saved[b % 2], 16 * (b // 2))
                    with act.Fori(0, per) as q:
                        for u in range(R):
                            act.wait_ge(g_done, q * R + (R * per * b + u + R + 1))
                            act.activation(out[:, b % 2, :, ds(q * (R * U) + u * U, U)],
                                           ps[:, u, :, :].rearrange("p t i -> p i t"), ACT.Copy).then_inc(taken, 1)

            @block.sync
            def _(sp):
                for b in range(BATCHES):
                    sp.wait_ge(taken, R * per * (b + 1) + R)
                    sp.dma_start(c.gates[b], out[:, b % 2, :, :].rearrange("p i t -> p (i t)")).then_inc(saved[b % 2], 16)
                for b in range(2):
                    sp.wait_ge(saved[b], 16 * (BATCHES // 2))


def stage_peer_experts(nc, c, a):
    N = GROUPS_ALL - EARLY
    STARTED = 1
    wd_d = rows(a["peer_w_downT"])
    wu_d = a["peer_w_up"][0].rearrange("(k p) n -> p k n", p=P)
    g_d = c.gates.rearrange("b p (i t) -> p b i t", t=TB)
    with Stage(nc, "experts") as s:
        wd = s.sb("wd", [P, KD, G * P])
        wd_hi = s.sb("wd_hi", [P, KD, G * P], F32R)
        wd_lo = s.sb("wd_lo", [P, KD, G * P], F32R)
        wu = s.sb("wu", [P, G, D])
        wu_hi = s.sb("wu_hi", [P, G, D], F32R)
        wu_lo = s.sb("wu_lo", [P, G, D], F32R)
        gt = s.sb("gt", [P, BATCHES, G * TB])
        hid = s.sb("hid", [P, G, T])
        hid_hi = s.sb("hid_hi", [P, G, T], F32R)
        hid_lo = s.sb("hid_lo", [P, G, T], F32R)
        H = s.ps("H", [P, G, T])
        Y = s.ps("Y", [P, 4, 512])
        hid_in, tile_done = s.sem("hid_in"), s.sem("tile_done")
        (wd_in, wu_in, gt_in, wd_h, wd_l, wu_h, wu_l, h_done, gelued, gated, hid_h, hid_l, y_done, added) = (
            s.sem(n) for n in ("wd_in", "wu_in", "gt_in", "wd_h", "wd_l", "wu_h", "wu_l", "h_done", "gelued",
                               "gated", "hid_h", "hid_l", "y_done", "added"))

        def tile(w, j):
            return w[:, :, j * P:(j + 1) * P]

        with s.block() as block:

            @block.sync
            def _(sp):
                def load_wd(e0):
                    sp.dma_start(wd[:], wd_d[:, :, ds(e0, G * P)]).then_inc(wd_in, 16)

                def load_gt(k0):
                    sp.dma_start(gt[:].rearrange("p b (i t) -> p b i t", t=TB), g_d[:, :, ds(k0, G), :]).then_inc(gt_in, 16)

                def load_wu(k0):
                    sp.dma_start(wu[:], wu_d[:, ds(k0, G), :]).then_inc(wu_in, 16)

                def load_hid(g):
                    sp.dma_start(hid[:].rearrange("p j t -> p (j t)"), c.early[ds(g, 1)].rearrange("o p n -> p (o n)")).then_inc(hid_in, 16)

                load_wu(0)
                load_hid(0)
                load_gt(0)
                load_wd(EARLY * G * P)
                with sp.Fori(0, EARLY - 1) as it:
                    g = sp.snap(it + 1)
                    k0 = sp.snap(it * G + G)
                    sp.wait_ge(gated, it * G + G)
                    load_gt(k0)
                    sp.wait_ge(wu_l, it * G + G)
                    load_wu(k0)
                    sp.wait_ge(hid_l, it * G + G)
                    load_hid(g)
                sp.wait_ge(gated, EARLY * G)
                load_gt(EARLY * G)
                sp.wait_ge(wu_l, EARLY * G)
                load_wu(EARLY * G)
                with sp.Fori(0, N - 1) as it:
                    e0 = sp.snap(it * (G * P) + (EARLY + 1) * G * P)
                    k0 = sp.snap(it * G + (EARLY + 1) * G)
                    sp.wait_ge(wd_l, it * G + G)
                    load_wd(e0)
                    sp.wait_ge(gated, it * G + (EARLY + 1) * G)
                    load_gt(k0)
                    sp.wait_ge(wu_l, it * G + (EARLY + 1) * G)
                    load_wu(k0)

            @block.tensor
            def _(pe):
                def early(it, first, last):
                    for j in range(G):
                        pe.wait_ge(wu_l, it * G + (j + 1))
                        pe.wait_ge(hid_l, it * G + (j + 1))
                        for y in range(8):
                            m, w = y // 2, slice(y % 2 * 512, y % 2 * 512 + 512)
                            out = Y[:, y, :] if y < 4 else H[:, y - 4, :]
                            hi, lo = hid_hi[:, j, m * P:m * P + P], hid_lo[:, j, m * P:m * P + P]
                            pe.matmul(out, hi, wu_hi[:, j, w], start=(first and j == 0), stop=False)
                            pe.matmul(out, hi, wu_lo[:, j, w], start=False, stop=False)
                            mm = pe.matmul(out, lo, wu_hi[:, j, w], start=False, stop=(last and j == G - 1))
                        mm.then_inc(tile_done, 1)

                pe.sem_inc(tile_done, G)
                early(0, True, False)
                with pe.Fori(1, EARLY - 1) as it:
                    early(it, False, False)
                early(EARLY - 1, False, True)
                with pe.Fori(0, N) as it:
                    for j in range(G):
                        pe.wait_ge(added, j + 2)
                        pe.wait_ge(wd_h, it * G + (j + 1))
                        pe.wait_ge(wd_l, it * G + (j + 1))
                        for k in range(KD):
                            hi, lo = tile(wd_hi, j)[:, k, :], tile(wd_lo, j)[:, k, :]
                            pe.matmul(H[:, j, :], hi, c.x_hi[:, k, :], start=(k == 0), stop=False)
                            pe.matmul(H[:, j, :], hi, c.x_lo[:, k, :], start=False, stop=False)
                            mm = pe.matmul(H[:, j, :], lo, c.x_hi[:, k, :], start=False, stop=(k == KD - 1))
                        mm.then_inc(h_done, 1)
                    pe.wait_ge(added, it * 8 + 9)
                    for y in range(8):
                        m, n = y // 2, y % 2
                        if y >= 4:
                            pe.wait_ge(added, it * 8 + (y + 6))
                        for j in range(G):
                            if y == 0:
                                pe.wait_ge(wu_l, it * G + (EARLY * G + j + 1))
                                pe.wait_ge(hid_l, it * G + (EARLY * G + j + 1))
                            hi, lo = hid_hi[:, j, m * P:m * P + P], hid_lo[:, j, m * P:m * P + P]
                            w = slice(n * 512, n * 512 + 512)
                            pe.matmul(Y[:, y % 4, :], hi, wu_hi[:, j, w], start=(j == 0), stop=False)
                            pe.matmul(Y[:, y % 4, :], hi, wu_lo[:, j, w], start=False, stop=False)
                            mm = pe.matmul(Y[:, y % 4, :], lo, wu_hi[:, j, w], start=False, stop=(j == G - 1))
                        mm.then_inc(y_done, 1)

            @block.scalar
            def _(act):
                def split_wd(nth, j):
                    act.wait_ge(wd_in, nth * 16 + 16)
                    act.activation(tile(wd_hi, j), tile(wd, j), ACT.Copy).then_inc(wd_h, 1)

                def group(it, last):
                    for j in range(G):
                        act.wait_ge(h_done, it * G + (j + 1))
                        act.activation(hid[:, j, :], H[:, j, :], ACT.Gelu).then_inc(gelued, 1)
                        act.wait_ge(wu_in, it * 16 + 16 * (EARLY + 1))
                        act.activation(wu_hi[:, j, :], wu[:, j, :], ACT.Copy).then_inc(wu_h, 1)
                        act.wait_ge(gated, it * G + (EARLY * G + j + 1))
                        act.activation(hid_hi[:, j, :], hid[:, j, :], ACT.Copy).then_inc(hid_h, 1)
                    if not last:
                        for j in range(G):
                            split_wd(it + 1, j)

                def early(it):
                    for j in range(G):
                        act.wait_ge(tile_done, it * G + (j + 1))
                        act.wait_ge(wu_in, it * 16 + 16)
                        act.activation(wu_hi[:, j, :], wu[:, j, :], ACT.Copy).then_inc(wu_h, 1)
                        act.wait_ge(gated, it * G + (j + 1))
                        act.activation(hid_hi[:, j, :], hid[:, j, :], ACT.Copy).then_inc(hid_h, 1)

                with act.Fori(0, EARLY) as it:
                    early(it)
                for j in range(G):
                    split_wd(0, j)
                with act.Fori(0, N - 1) as it:
                    group(it, False)
                group(N - 1, True)

            @block.vector
            def _(dve):
                def split_wd(nth, j):
                    dve.wait_ge(wd_h, nth * G + (j + 1))
                    dve.tensor_tensor(tile(wd_lo, j), tile(wd, j), tile(wd_hi, j).bitcast(F32),
                                      ALU.subtract).then_inc(wd_l, 1)

                def group(it, last):
                    dve.wait_ge(gt_in, it * 16 + 16 * (EARLY + 1))
                    for j in range(G):
                        dve.wait_ge(gelued, it * G + (j + 1))
                        h = hid[:, j, :].rearrange("p (b t) -> p b t", b=BATCHES)
                        dve.tensor_tensor(h, h, gt[:, :, j * TB:(j + 1) * TB], ALU.mult).then_inc(gated, 1)
                        dve.wait_ge(wu_h, it * G + (EARLY * G + j + 1))
                        dve.tensor_tensor(wu_lo[:, j, :], wu[:, j, :], wu_hi[:, j, :].bitcast(F32),
                                          ALU.subtract).then_inc(wu_l, 1)
                        dve.wait_ge(hid_h, it * G + (EARLY * G + j + 1))
                        dve.tensor_tensor(hid_lo[:, j, :], hid[:, j, :], hid_hi[:, j, :].bitcast(F32),
                                          ALU.subtract).then_inc(hid_l, 1)
                    for y in range(8):
                        m, n = y // 2, y % 2
                        if y % 2 == 0 and not last:
                            split_wd(it + 1, y // 2)
                        dve.wait_ge(y_done, it * 8 + (y + 1))
                        out = c.h[:, m, n * 512:n * 512 + 512]
                        if y == 0:
                            dve.wait_ge(added, it * 8 + 9)
                        dve.tensor_tensor(out, out, Y[:, y % 4, :], ALU.add).then_inc(added, 1)

                dve.sem_inc(added, 1)
                with dve.Fori(0, EARLY) as it:
                    dve.wait_ge(gt_in, it * 16 + 16)
                    dve.wait_ge(hid_in, it * 16 + 16)
                    for j in range(G):
                        h = hid[:, j, :].rearrange("p (b t) -> p b t", b=BATCHES)
                        dve.tensor_tensor(h, h, gt[:, :, j * TB:(j + 1) * TB], ALU.mult).then_inc(gated, 1)
                        dve.wait_ge(wu_h, it * G + (j + 1))
                        dve.tensor_tensor(wu_lo[:, j, :], wu[:, j, :], wu_hi[:, j, :].bitcast(F32),
                                          ALU.subtract).then_inc(wu_l, 1)
                        dve.wait_ge(hid_h, it * G + (j + 1))
                        dve.tensor_tensor(hid_lo[:, j, :], hid[:, j, :], hid_hi[:, j, :].bitcast(F32),
                                          ALU.subtract).then_inc(hid_l, 1)
                for j in range(G):
                    split_wd(0, j)
                dve.wait_ge(tile_done, (EARLY + 1) * G)
                for y in (4, 5, 6, 7, 0, 1, 2, 3):
                    m, n = y // 2, y % 2
                    out = c.h[:, m, n * 512:n * 512 + 512]
                    dve.tensor_tensor(out, out, Y[:, y, :] if y < 4 else H[:, y - 4, :], ALU.add).then_inc(added, 1)
                with dve.Fori(0, N - 1) as it:
                    group(it, False)
                group(N - 1, True)


def stage_split_x(nc, c):
    with Stage(nc, "splitx") as s:
        high, low = s.sem("high"), s.sem("low")
        with s.block() as block:

            @block.scalar
            def _(act):
                for k in range(KD):
                    act.activation(c.x_hi[:, k, :], c.hT[:, k, :], ACT.Copy).then_inc(high, 1)

            @block.vector
            def _(dve):
                for k in range(KD):
                    dve.wait_ge(high, k + 1)
                    dve.tensor_tensor(c.x_lo[:, k, :], c.hT[:, k, :], c.x_hi[:, k, :].bitcast(F32),
                                      ALU.subtract).then_inc(low, 1)


AH = 8
AJ = 4
GG = 8
ALPHA = 2.0 ** 0.25
NEG = -1e30
COL_K, COL_V, COL_U, COL_S = 512, 640, 768, 1280
EXPERTS = 32
EK = 4
BLOCKS = (T * EK) // P + EXPERTS - 1
NBLK = BLOCKS + 1
LIMIT, SWIGLU = 7.0, 1.702
ROWS = T * EK


def stage_project2(nc, c, a):
    w_d = rows(a["w_in_2"])
    with Stage(nc, "proj2") as s:
        w = s.sb("w", [P, KD, 1792])
        cb = s.sb("cb", [P, 14])
        rb = s.sb("rb", [P, P + 512])
        lg = s.sb("lg", [P, 512])
        lb = s.sb("lb", [P, 512])
        sq = s.sb("sq", [P, M, GG, 64])
        stat = s.sb("stat", [P, 2, M, GG])
        ps = s.ps("ps", [P, 8, 512])
        parts = ((COL_V, COL_U), (COL_S, 1792), (0, COL_V), (COL_U, COL_S))
        w_in = [s.sem(f"w_in{i}") for i in range(len(parts))]
        (cb_in, rb_in, done, taken, added, gelued, chain, root, var) = (
            s.sem(n) for n in ("cb_in", "rb_in", "done", "taken", "added", "gelued", "chain", "root", "var"))
        chans = [(c.qT[:, j, :], j) for j in range(AJ)] + [(c.kT[:], 4)] + [(c.uT2[:, j, :], 6 + j) for j in range(4)]
        with s.block() as block:

            @block.sync
            def _(sp):
                sp.dma_start(rb[:], a["b_in_2_row"].to_broadcast([P, P + 512])).then_inc(rb_in, 16)
                for i, (lo, hi) in enumerate(parts):
                    sp.dma_start(w[:, :, lo:hi], w_d[:, :, lo:hi]).then_inc(w_in[i], 16)
                sp.dma_start(lg[:], a["ln_v_g_2"].to_broadcast([P, 512])).then_inc(rb_in, 16)
                sp.dma_start(lb[:], a["ln_v_b_2"].to_broadcast([P, 512])).then_inc(rb_in, 16)
                sp.dma_start(cb[:], a["b_in_2_col"]).then_inc(cb_in, 16)

            @block.tensor
            def _(pe):
                pe.wait_ge(w_in[0], 16)
                for m in range(M):
                    for k in range(KD):
                        mm = pe.matmul(ps[:, 4, m * P:m * P + P], c.hT[:, k, m * P:m * P + P], w[:, k, COL_V:COL_U],
                                       start=(k == 0), stop=(k == KD - 1))
                mm.then_inc(done, 1)
                pe.wait_ge(w_in[1], 16)
                for m in range(M):
                    for k in range(KD):
                        mm = pe.matmul(ps[:, m, :], c.hT[:, k, m * P:m * P + P], w[:, k, COL_S:1792],
                                       start=(k == 0), stop=(k == KD - 1))
                    mm.then_inc(done, 1)
                pe.wait_ge(w_in[2], 16)
                for i, (_, t) in enumerate(chans):
                    if i == 5:
                        pe.wait_ge(w_in[3], 16)
                    if i >= 3:
                        pe.wait_ge(taken, i - 2)
                    for k in range(KD):
                        mm = pe.matmul(ps[:, 5 + i % 3, :], w[:, k, t * P:t * P + P], c.hT[:, k, :],
                                       start=(k == 0), stop=(k == KD - 1))
                    mm.then_inc(done, 1)

            @block.scalar
            def _(act):
                for m in range(M):
                    act.wait_ge(added, m + 2)
                    act.activation(c.gtok[:, m, :], c.gtok[:, m, :], ACT.Gelu_apprx_tanh).then_inc(gelued, 1)
                act.wait_ge(cb_in, 16)
                for i, (out, t) in enumerate(chans):
                    act.wait_ge(done, 5 + i + 1)
                    act.activation(out, ps[:, 5 + i % 3, :], ACT.Identity if i < 5 else ACT.Gelu_apprx_tanh,
                                   bias=cb[:, t:t + 1]).then_inc(taken, 1)
                act.wait_ge(var, 1)
                act.activation(stat[:, 1, :, :], stat[:, 1, :, :], ACT.Sqrt).then_inc(root, 1)

            @block.vector
            def _(dve):
                step = chained(dve, chain)
                dve.wait_ge(rb_in, 48)
                dve.wait_ge(done, 1)
                dve.tensor_tensor(c.vtok[:], ps[:, 4, :].rearrange("p (m d) -> p m d", m=M),
                                  rb[:, 0:P].unsqueeze(1).to_broadcast([P, M, P]), ALU.add).then_inc(added, 1)
                for m in range(M):
                    dve.wait_ge(done, m + 2)
                    dve.tensor_tensor(c.gtok[:, m, :], ps[:, m, :], rb[:, P:P + 512], ALU.add).then_inc(added, 1)
                dve.wait_ge(gelued, M)
                g = c.gtok[:].rearrange("p m (g d) -> p m g d", g=GG)
                g3 = c.gtok[:].rearrange("p m (g d) -> p (m g) d", g=GG)
                sq3 = sq[:].rearrange("p m g d -> p (m g) d")
                mean, var_ = (stat[:, i, :, :].rearrange("p m g -> p (m g)") for i in range(2))
                step(dve.tensor_reduce(mean, g3, AX.X, ALU.add))
                step(dve.tensor_scalar(mean, mean, 1.0 / 64, None, ALU.mult))
                step(dve.tensor_tensor(g3, g3, mean.unsqueeze(2).to_broadcast([P, M * GG, 64]), ALU.subtract))
                step(dve.tensor_tensor(sq3, g3, g3, ALU.mult))
                step(dve.tensor_reduce(var_, sq3, AX.X, ALU.add))
                dve.tensor_scalar(var_, var_, 1.0 / 64, EPS, ALU.mult, ALU.add).then_inc(var, 1)
                dve.wait_ge(root, 1)
                step(dve.reciprocal(var_, var_))
                step(dve.tensor_tensor(g3, g3, var_.unsqueeze(2).to_broadcast([P, M * GG, 64]), ALU.mult))
                step(dve.tensor_tensor(c.gtok[:], c.gtok[:], lg[:].unsqueeze(1).to_broadcast([P, M, 512]), ALU.mult))
                step(dve.tensor_tensor(c.gtok[:], c.gtok[:], lb[:].unsqueeze(1).to_broadcast([P, M, 512]), ALU.add))


def stage_attention(nc, c, a):
    W2 = 2 * P
    with Stage(nc, "attn") as s:
        mask = s.sb("mask", [P, W2])
        sink = s.sb("sink", [P, 2, AJ])
        sc = s.sb("sc", [P, 2, 2, W2])
        top = s.sb("top", [P, 2, 2, 4])
        pT = s.sb("pT", [P, 2, 4, P])
        wsT = s.sb("wsT", [P, GG, P])
        bsb = s.sb("bsb", [P, 4, P])
        S = s.ps("S", [P, 2, 2, 512])
        X = s.ps("X", [P, 2, 4, P])
        O = s.ps("O", [P, 2, 512])
        (masked, sink_in, ws_in, bs_in, s_done, maxed, exped, probs, chain, turned, pt_ok, o_done, o_taken, s_read,
         g_done, g_taken, ws_ok) = (s.sem(n) for n in (
             "masked", "sink_in", "ws_in", "bs_in", "s_done", "maxed", "exped", "probs", "chain", "turned", "pt_ok",
             "o_done", "o_taken", "s_read", "g_done", "g_taken", "ws_ok"))
        PAIRS = M * AJ

        def span(n):
            return (P, P) if n == 0 else (0, W2)

        with s.block() as block:

            @block.sync
            def _(sp):
                sp.dma_start(sink[:], a["sinks_2"].to_broadcast([P, AH]).rearrange("p (t j) -> p t j", t=2)).then_inc(sink_in, 16)
                sp.dma_start(wsT[:], a["w_spatial_2T"]).then_inc(ws_in, 16)
                bs = a["b_spatial_2"][0].rearrange("(k two) t -> two k t", two=2)
                for two in range(2):
                    sp.dma_start(bsb[64 * two:64 * two + 64, :, :],
                                 bs[two:two + 1].to_broadcast([64, 4, P])).then_inc(bs_in, 16)

            @block.gpsimd
            def _(pool):
                pool.memset(mask[:], 0.0).then_inc(masked, 1)
                pool.wait_ge(masked, 1)
                pool.affine_select(out=mask[:, 0:P], in_=mask[:, 0:P], compare_op=ALU.is_gt, fill=NEG, base=0,
                                   pattern=[[1, P]], channel_multiplier=-1).then_inc(masked, 1)
                pool.affine_select(out=mask[:, P:W2], in_=mask[:, P:W2], compare_op=ALU.is_ge, fill=NEG, base=0,
                                   pattern=[[-1, P]], channel_multiplier=1).then_inc(masked, 1)
                pool.wait_ge(ws_in, 16)
                pool.affine_select(out=wsT[:], in_=wsT[:], compare_op=ALU.is_ge, fill=0.0, base=0,
                                   pattern=[[0, GG], [1, P]], channel_multiplier=-1).then_inc(ws_ok, 1)

            @block.tensor
            def _(pe):
                def scores(i):
                    n, j = i // AJ, i % AJ
                    lo, width = span(n)
                    if i >= 2:
                        pe.wait_ge(s_read, i - 1)
                    for t in range(2):
                        h = slice(64 * t, 64 * t + 64)
                        mm = pe.matmul(S[:, i % 2, t, lo:lo + width], c.qT[h, j, n * P:n * P + P],
                                       c.kT[h, (n - 1) * P + lo:(n - 1) * P + lo + width], start=True, stop=True)
                    mm.then_inc(s_done, 1)

                def turn(i):
                    n = i // AJ
                    pe.wait_ge(probs, i + 1)
                    if i >= 2:
                        pe.wait_ge(pt_ok, i - 1)
                    for t in range(2):
                        for b in range(2):
                            if n > 0 or b == 1:
                                x = pe.transpose(X[:, i % 2, 2 * t + b, :], sc[:, i % 2, t, b * P:b * P + P], c.ident[:])
                    x.then_inc(turned, 1)

                def values(i):
                    n, j = i // AJ, i % AJ
                    pe.wait_ge(pt_ok, i + 1)
                    if i >= 2:
                        pe.wait_ge(o_taken, i - 1)
                    for t in range(2):
                        for b in range(2):
                            if n > 0 or b == 1:
                                mm = pe.matmul(O[64 * t:64 * t + 64, i % 2, 0:P], c.vtok[:, n - 1 + b, 64 * t:64 * t + 64],
                                               pT[:, i % 2, 2 * t + b, :], start=(b == 0 or n == 0), stop=(b == 1))
                    mm.then_inc(o_done, 1)

                scores(0)
                for i in range(PAIRS):
                    if i + 1 < PAIRS:
                        scores(i + 1)
                    turn(i)
                    if i >= 1:
                        values(i - 1)
                values(PAIRS - 1)
                pe.wait_ge(ws_ok, 1)
                for n in range(M):
                    if n >= 2:
                        pe.wait_ge(g_taken, n - 1)
                    else:
                        pe.wait_ge(pt_ok, PAIRS)
                    for g in range(GG):
                        mm = pe.matmul(X[64 * (g % 2):64 * (g % 2) + 64, n % 2, g // 2, :],
                                       c.gtok[:, n, 64 * g:64 * g + 64], wsT[:, g, :], start=True, stop=True)
                    mm.then_inc(g_done, 1)

            @block.scalar
            def _(act):
                def exps(i):
                    lo, width = span(i // AJ)
                    b = i % 2
                    act.wait_ge(maxed, i + 1)
                    for t in range(2):
                        act.activation(sc[:, b, t, lo:lo + width], sc[:, b, t, lo:lo + width], ACT.Exp,
                                       bias=top[:, b, t, 0:1], accum_out=top[:, b, t, 2:3])
                        ins = act.activation(top[:, b, t, 1:2], sink[:, t, i % AJ:i % AJ + 1], ACT.Exp, bias=top[:, b, t, 0:1])
                    ins.then_inc(exped, 1)

                def copies(i):
                    act.wait_ge(turned, i + 1)
                    if i >= 2:
                        act.wait_ge(o_done, i - 1)
                    if i < AJ:
                        act.activation(pT[:, i % 2, 1:4:2, :], X[:, i % 2, 1:4:2, :], ACT.Copy).then_inc(pt_ok, 1)
                    else:
                        act.activation(pT[:, i % 2, :, :], X[:, i % 2, :, :], ACT.Copy).then_inc(pt_ok, 1)

                def outs(i):
                    n, j = i // AJ, i % AJ
                    act.wait_ge(o_done, i + 1)
                    act.activation(c.mixT[:, j, n * P:n * P + P], O[:, i % 2, 0:P], ACT.Copy).then_inc(o_taken, 1)

                act.wait_ge(sink_in, 16)
                exps(0)
                for i in range(PAIRS):
                    copies(i)
                    if i + 1 < PAIRS:
                        exps(i + 1)
                    if i >= 1:
                        outs(i - 1)
                outs(PAIRS - 1)

            @block.vector
            def _(dve):
                step = chained(dve, chain)

                def maxes(i):
                    n, j, b = i // AJ, i % AJ, i % 2
                    lo, width = span(n)
                    dve.wait_ge(s_done, i + 1)
                    if i >= 2:
                        dve.wait_ge(turned, i - 1)
                    x = sc[:, b, :, lo:lo + width]
                    dve.scalar_tensor_tensor(out=x, in0=S[:, b, :, lo:lo + width], scalar=64 ** -0.5,
                                             in1=mask[:, lo:lo + width].unsqueeze(1).to_broadcast([P, 2, width]),
                                             op0=ALU.mult, op1=ALU.add).then_inc(s_read, 1)
                    dve.wait_ge(s_read, i + 1)
                    step(dve.tensor_reduce(top[:, b, :, 3], x, AX.X, ALU.max))
                    step(dve.tensor_tensor(top[:, b, :, 3], top[:, b, :, 3], sink[:, :, j], ALU.max))
                    dve.tensor_scalar(top[:, b, :, 0], top[:, b, :, 3], -1.0, None, ALU.mult).then_inc(maxed, 1)

                def norms(i):
                    b = i % 2
                    lo, width = span(i // AJ)
                    dve.wait_ge(exped, i + 1)
                    step(dve.tensor_tensor(top[:, b, :, 3], top[:, b, :, 1], top[:, b, :, 2], ALU.add))
                    step(dve.reciprocal(top[:, b, :, 3], top[:, b, :, 3]))
                    for t in range(2):
                        ins = dve.tensor_scalar(sc[:, b, t, lo:lo + width], sc[:, b, t, lo:lo + width],
                                                top[:, b, t, 3:4], None, ALU.mult)
                    ins.then_inc(probs, 1)

                dve.wait_ge(sink_in, 16)
                dve.wait_ge(masked, 3)
                maxes(0)
                for i in range(PAIRS):
                    if i + 1 < PAIRS:
                        maxes(i + 1)
                    norms(i)
                dve.wait_ge(bs_in, 32)
                for n in range(M):
                    dve.wait_ge(g_done, n + 1)
                    out = c.mixT[:, AJ:, n * P:n * P + P]
                    dve.tensor_tensor(out, X[:, n % 2, :, :], bsb[:], ALU.add).then_inc(g_taken, 1)
                    dve.wait_ge(g_taken, n + 1)
                    step(dve.tensor_tensor(out, out, c.uT2[:, :, n * P:n * P + P], ALU.mult))


def stage_route(nc, c, a):
    ME = [P, M, EXPERTS]
    with Stage(nc, "route") as s:
        wr = s.sb("wr", [P, KD, EXPERTS])
        br = s.sb("br", [P, EXPERTS])
        bd = s.sb("bd", [EXPERTS, D])
        logit = s.sb("logit", ME)
        v8 = s.sb("v8", [P, M, 8])
        i8 = s.sb("i8", [P, M, 8], U32)
        i4 = s.sb("i4", [P, M, EK])
        gate = s.sb("gate", [P, M, EK])
        tot = s.sb("tot", [P, M])
        hot = s.sb("hot", [P, M * EK, EXPERTS])
        hg = s.sb("hg", [P, M * EK, EXPERTS])
        mem = s.sb("mem", ME)
        ge = s.sb("ge", ME)
        rank = s.sb("rank", ME)
        over = s.sb("over", ME)
        tmp = s.sb("tmp", ME)
        cnt = s.sb("cnt", [P, EXPERTS])
        nb = s.sb("nb", [P, EXPERTS])
        t2 = s.sb("t2", [P, EXPERTS])
        onesE = s.sb("onesE", [P, EXPERTS])
        end = s.sb("end", [P, EXPERTS])
        start = s.sb("start", [P, EXPERTS])
        dest = s.sb("dest", [P, M * EK])
        desti = s.sb("desti", [P, M * EK], U32)
        entry = s.sb("entry", [P, M * EK, 4], I32)
        blank = s.sb("blank", [P, NBLK, 4], I32)
        ecmp = s.sb("ecmp", [1, NBLK, EXPERTS])
        ownf = s.sb("ownf", [1, NBLK])
        geT = s.sb("geT", [EXPERTS, M, P])
        ps = s.ps("ps", [P, 8, 512])
        wr_in, bd_in, br_in = s.sem("wr_in"), s.sem("bd_in"), s.sem("br_in")
        (l_done, shifted, exped, chain, mem_ok, cnt_done, ge_ok, turned, gt_ok, b_done, b_taken, blanked, blank_out,
         ids, dest_ok, scattered, back) = (s.sem(n) for n in (
             "l_done", "shifted", "exped", "chain", "mem_ok", "cnt_done", "ge_ok", "turned", "gt_ok", "b_done",
             "b_taken", "blanked", "blank_out", "ids", "dest_ok", "scattered", "back"))
        table = c.table
        with s.block() as block:

            @block.sync
            def _(sp):
                sp.dma_start(wr[:], rows(a["w_router_2"][0])).then_inc(wr_in, 16)
                sp.dma_start(br[:], a["b_router_2"].to_broadcast([P, EXPERTS])).then_inc(br_in, 16)
                sp.dma_start(bd[:], a["b_down_2"][0]).then_inc(bd_in, 16)
                sp.wait_ge(blanked, 2)
                sp.dma_start(table.rearrange("(p r) w -> p r w", p=P), blank[:]).then_inc(blank_out, 16)

            @block.gpsimd
            def _(pool):
                pool.memset(blank[:], 0).then_inc(ids, 1)
                pool.wait_ge(ids, 1)
                pool.memset(blank[:, :, 1:2], 4 * ROWS).then_inc(blanked, 1)
                pool.memset(entry[:], 0).then_inc(blanked, 1)
                pool.wait_ge(blanked, 2)
                e4 = entry[:].rearrange("p (m k) w -> p m k w", m=M)
                pool.iota(e4[:, :, :, 0], pattern=[[P, M], [0, EK]], base=0, channel_multiplier=1).then_inc(ids, 1)
                pool.iota(e4[:, :, :, 1], pattern=[[P * EK, M], [1, EK]], base=0, channel_multiplier=EK).then_inc(ids, 1)
                pool.wait_ge(blank_out, 16)
                pool.wait_ge(dest_ok, 1)
                for i in range(M * EK):
                    pool.indirect_dma_start(out=table[:, :], out_offset=bass.IndirectOffsetOnAxis(ap=desti[:, i:i + 1], axis=0),
                                            in_=entry[:, i, :], in_offset=None, bounds_check=P * NBLK - 1,
                                            oob_is_err=False).then_inc(scattered, 16)
                pool.wait_ge(scattered, 16 * M * EK)
                pool.dma_start(c.slots[:, 0:NBLK, :], table.rearrange("(p r) w -> p r w", p=P)).then_inc(back, 16)
                pool.wait_ge(back, 16)

            @block.tensor
            def _(pe):
                pe.wait_ge(wr_in, 16)
                for m in range(M):
                    for k in range(KD):
                        mm = pe.matmul(ps[:, 0, m * EXPERTS:(m + 1) * EXPERTS], c.hT[:, k, m * P:m * P + P], wr[:, k, :],
                                       start=(k == 0), stop=(k == KD - 1))
                mm.then_inc(l_done, 1)
                pe.wait_ge(mem_ok, 1)
                for m in range(M):
                    for q in range(m + 1):
                        pe.matmul(ps[:, 1, m * EXPERTS:(m + 1) * EXPERTS], c.upper[:] if q == m else c.ones[:],
                                  mem[:, q, :], start=(q == 0), stop=(q == m))
                for q in range(M):
                    mm = pe.matmul(ps[:, 2, 0:EXPERTS], c.ones[:], mem[:, q, :], start=(q == 0), stop=(q == M - 1))
                mm.then_inc(cnt_done, 1)
                pe.wait_ge(ge_ok, 1)
                for m in range(M):
                    t = pe.transpose(ps[0:EXPERTS, 3, m * P:m * P + P], ge[:, m, :], c.ident[:])
                t.then_inc(turned, 1)
                pe.wait_ge(gt_ok, 1)
                pe.wait_ge(bd_in, 16)
                for i in range(2 * M):
                    m, n = i // 2, i % 2
                    if i >= 4:
                        pe.wait_ge(b_taken, i - 3)
                    pe.matmul(ps[:, 4 + i % 4, :], geT[:, m, :], bd[:, n * 512:n * 512 + 512],
                              start=True, stop=True).then_inc(b_done, 1)

            @block.scalar
            def _(act):
                act.wait_ge(shifted, 1)
                act.activation(gate[:], gate[:], ACT.Exp).then_inc(exped, 1)
                act.wait_ge(turned, 1)
                act.activation(geT[:], ps[0:EXPERTS, 3, :].rearrange("e (m t) -> e m t", m=M), ACT.Copy).then_inc(gt_ok, 1)

            @block.vector
            def _(dve):
                step = chained(dve, chain)
                step(dve.memset(onesE[:], 1.0))
                dve.wait_ge(br_in, 16)
                dve.wait_ge(l_done, 1)
                step(dve.tensor_tensor(logit[:], ps[:, 0, 0:M * EXPERTS].rearrange("p (m e) -> p m e", m=M),
                                       br[:].unsqueeze(1).to_broadcast(ME), ALU.add))
                for m in range(M):
                    ins = dve.max(v8[:, m, :], logit[:, m, :])
                step(ins)
                for m in range(M):
                    ins = dve.max_index(i8[:, m, :], v8[:, m, :], logit[:, m, :])
                step(ins)
                dve.tensor_tensor(gate[:], v8[:, :, 0:EK], v8[:, :, 0:1].to_broadcast([P, M, EK]),
                                  ALU.subtract).then_inc(shifted, 1)
                step(dve.tensor_copy(i4[:], i8[:, :, 0:EK]))
                step(dve.tensor_tensor(hot[:], i4[:].rearrange("p m k -> p (m k)").unsqueeze(2).to_broadcast([P, M * EK, EXPERTS]),
                                       c.count[:, 0:EXPERTS].unsqueeze(1).to_broadcast([P, M * EK, EXPERTS]), ALU.is_equal))
                hot4 = hot[:].rearrange("p (m k) e -> p m k e", m=M)
                by_e = "p (m k) e -> p m e k"
                for m in range(M):
                    ins = dve.tensor_reduce(mem[:, m, :], hot[:, m * EK:(m + 1) * EK, :].rearrange("p k e -> p e k"),
                                            AX.X, ALU.add)
                ins.then_inc(mem_ok, 1)
                dve.wait_ge(mem_ok, 1)
                dve.wait_ge(exped, 1)
                step(dve.tensor_reduce(tot[:], gate[:], AX.X, ALU.add))
                step(dve.reciprocal(tot[:], tot[:]))
                step(dve.tensor_tensor(gate[:], gate[:], tot[:].unsqueeze(2).to_broadcast([P, M, EK]), ALU.mult))
                step(dve.tensor_tensor(hg[:], hot[:], gate[:].rearrange("p m k -> p (m k)").unsqueeze(2)
                                       .to_broadcast([P, M * EK, EXPERTS]), ALU.mult))
                for m in range(M):
                    ins = dve.tensor_reduce(ge[:, m, :], hg[:, m * EK:(m + 1) * EK, :].rearrange("p k e -> p e k"),
                                            AX.X, ALU.add)
                ins.then_inc(ge_ok, 1)
                dve.wait_ge(cnt_done, 1)
                step(dve.tensor_copy(cnt[:], ps[:, 2, 0:EXPERTS]))
                step(dve.tensor_scalar(nb[:], cnt[:], 0.0, None, ALU.is_gt))
                for r in range(1, T // P):
                    step(dve.tensor_scalar(t2[:], cnt[:], float(P * r), None, ALU.is_gt))
                    step(dve.tensor_tensor(nb[:], nb[:], t2[:], ALU.add))
                step(dve.tensor_tensor_scan(end[:], onesE[:], nb[:], 0.0, ALU.mult, ALU.add))
                step(dve.tensor_tensor(start[:], end[:], nb[:], ALU.subtract))
                step(dve.tensor_scalar(rank[:], ps[:, 1, 0:M * EXPERTS].rearrange("p (m e) -> p m e", m=M), -1.0, None, ALU.add))
                step(dve.tensor_scalar(over[:], rank[:], float(P), None, ALU.is_ge))
                for r in range(2, T // P):
                    step(dve.tensor_scalar(tmp[:], rank[:], float(P * r), None, ALU.is_ge))
                    step(dve.tensor_tensor(over[:], over[:], tmp[:], ALU.add))
                step(dve.tensor_scalar(over[:], over[:], -float(P * NBLK - 1), None, ALU.mult))
                step(dve.scalar_tensor_tensor(out=rank[:], in0=rank[:], scalar=float(NBLK), in1=over[:],
                                              op0=ALU.mult, op1=ALU.add))
                step(dve.tensor_tensor(rank[:], rank[:], start[:].unsqueeze(1).to_broadcast(ME), ALU.add))
                step(dve.tensor_tensor(hg[:].rearrange("p (m k) e -> p m k e", m=M), hot4,
                                       rank[:].unsqueeze(2).to_broadcast([P, M, EK, EXPERTS]), ALU.mult))
                step(dve.tensor_reduce(dest[:], hg[:], AX.X, ALU.add))
                step(dve.tensor_copy(desti[:], dest[:]))
                dve.wait_ge(ids, 3)
                dve.tensor_copy(entry[:, :, 2], gate[:].rearrange("p m k -> p (m k)").bitcast(I32)).then_inc(dest_ok, 1)
                step(dve.tensor_tensor(ecmp[:], end[0:1, :].unsqueeze(1).to_broadcast([1, NBLK, EXPERTS]),
                                       c.count[0:1, 0:NBLK].unsqueeze(2).to_broadcast([1, NBLK, EXPERTS]), ALU.is_le))
                step(dve.tensor_reduce(ownf[:], ecmp[:], AX.X, ALU.add))
                step(dve.tensor_scalar(ownf[:], ownf[:], float(EXPERTS - 1), None, ALU.min))
                step(dve.tensor_copy(c.owner[0:1, 0:NBLK], ownf[:]))
                step(dve.tensor_copy(c.owner[0:1, NBLK:NBLK + 1], end[0:1, EXPERTS - 1:EXPERTS]))
                for i in range(2 * M):
                    m, n = i // 2, i % 2
                    dve.wait_ge(b_done, i + 1)
                    out = c.h[:, m, n * 512:n * 512 + 512]
                    dve.scalar_tensor_tensor(out=out, in0=out, scalar=ALPHA, in1=ps[:, 4 + i % 4, :],
                                             op0=ALU.mult, op1=ALU.add).then_inc(b_taken, 1)


def stage_experts(nc, c, a):
    CHUNK = 512
    HT = 4
    CHUNKS, PIECES = 6, 12
    RAW, RING = 4, 4
    PIECE = KD * CHUNK // 2
    STARTED = 2 * RAW
    with Stage(nc, "moe") as s:
        raw = [s.sb(f"raw{i}", [P, KD * CHUNK])[:] for i in range(RAW - 1)] + [c.hT[:].rearrange("p k t -> p (k t)")]
        w_hi = [s.sb(f"w_hi{i}", [P, PIECE], F32R) for i in range(RING)]
        w_lo = [s.sb(f"w_lo{i}", [P, PIECE], F32R) for i in range(RING)]
        bias = s.sb("bias", [2 * EXPERTS, 2 * D], F32R)
        pick = s.sb("pick", [2 * EXPERTS, P], F32R)
        slot = s.sb("slot", [P, 2, 4], I32)
        xg = s.sb("xg", [P, 2, D])
        x_hi = s.sb("x_hi", [P, KD, P], F32R)
        x_lo = s.sb("x_lo", [P, KD, P], F32R)
        ga = s.sb("ga", [P, CHUNK])
        up = s.sb("up", [P, CHUNK])
        sg = s.sb("sg", [P, CHUNK])
        hid = s.sb("hid", [P, CHUNK])
        hid_hi = s.sb("hid_hi", [P, KD, P], F32R)
        hid_lo = s.sb("hid_lo", [P, KD, P], F32R)
        y = s.sb("y", [P, 2, D])
        GU = s.ps("GU", [P, 4, CHUNK])
        Y = s.ps("Y", [P, 2, CHUNK])
        X = s.ps("X", [P, 2, 4, P])
        raw_in = [s.sem(f"raw_in{i}") for i in range(RAW)]
        bias_in = s.sem("bias_in")
        gathered = [s.sem(f"gathered{i}") for i in range(2)]
        (slotted, paced, bias_high, bias_ok, picked, x_done, x_high, x_low, w_high, w_low, piece_done,
         g_ok, sig, h_chain, h_ok, turned, h_high, h_low, y_ok, stored) = (s.sem(n) for n in (
             "slotted", "paced", "bias_high", "bias_ok", "picked", "x_done", "x_high", "x_low", "w_high",
             "w_low", "piece_done", "g_ok", "sig", "h_chain", "h_ok", "turned", "h_high", "h_low", "y_ok", "stored"))
        wg_d, wu_d, wd_d = (a[n][0] for n in ("w_gate_2", "w_up_2", "w_down_2"))

        def n_blocks(eng):
            return eng.value_load(c.owner[0:1, NBLK:NBLK + 1], min_val=1, max_val=BLOCKS)

        def owner_of(eng, j):
            return eng.value_load(c.owner[0:1, ds(j, 1)], min_val=0, max_val=EXPERTS - 1)

        def chunk_of(it, u, q):
            i = CHUNKS * u + q
            return i % RAW, it * (2 * CHUNKS // RAW) + i // RAW

        def cut(w, q):
            return w.rearrange("p (k n) -> p k n", n=CHUNK if q < 4 else D)

        def piece_of(r, p):
            return raw[r][:, p % 2 * PIECE:(p % 2 + 1) * PIECE]

        def h_turned(half):
            return GU[:, 2 * half, :].rearrange("p (f t) -> p f t", f=HT)

        def h_split(h, half):
            return h[:, HT * half:HT * half + HT, :]

        with s.block() as block:

            @block.sync
            def _(sp):
                for part in range(2):
                    sp.dma_start(y[EXPERTS * part:EXPERTS * part + EXPERTS, :, :],
                                 a["bias_gate_up"]).then_inc(bias_in, 16)
                n = n_blocks(sp)
                with sp.Fori(0, NBLK // 2) as it:
                    for u in range(2):
                        j = it * 2 + u
                        with sp.If(j < n):
                            e = owner_of(sp, j)
                            for q in range(CHUNKS):
                                r, _ = chunk_of(it, u, q)
                                if q < 4:
                                    w_d, half = (wg_d, wu_d)[q % 2], q // 2
                                    src = w_d[ds(e, 1), :, half * CHUNK:(half + 1) * CHUNK]
                                else:
                                    src = wd_d[ds(e, 1), (q - 4) * CHUNK:(q - 3) * CHUNK, :]
                                sp.wait_ge(w_low, j * PIECES + (STARTED + 2 * (q - RAW) + 2))
                                sp.dma_start(cut(raw[r], q), src.rearrange("o (k p) n -> p (o k) n", p=P)).then_inc(raw_in[r], 16)

            @block.gpsimd
            def _(pool):
                n = n_blocks(pool)

                def gather(j, b):
                    pool.tensor_copy(slot[:, b, :], c.slots[:, ds(j, 1), :].rearrange("p o w -> p (o w)")).then_inc(slotted, 1)
                    pool.wait_ge(slotted, j + 1)
                    pool.sem_inc(paced, 1)
                    pool.indirect_dma_start(out=xg[:, b, :], out_offset=None, in_=c.h_rows[:, :],
                                            in_offset=bass.IndirectOffsetOnAxis(ap=slot[:, b, 0:1].bitcast(U32), axis=0),
                                            bounds_check=T - 1, oob_is_err=False).then_inc(gathered[b], 16)

                gather(0, 0)
                with pool.Fori(0, NBLK // 2) as it:
                    for u in range(2):
                        j = it * 2 + u
                        with pool.If(j + 1 < n):
                            gather(j + 1, 1 - u)
                        with pool.If(j < n):
                            pool.wait_ge(y_ok, j + 2)
                            pool.sem_inc(paced, 1)
                            pool.indirect_dma_start(out=c.pair_rows[:, :],
                                                    out_offset=bass.IndirectOffsetOnAxis(ap=slot[:, u, 1:2].bitcast(U32), axis=0),
                                                    in_=y[:, u, :], in_offset=None, bounds_check=ROWS - 1,
                                                    oob_is_err=False).then_inc(stored, 16)
                            pool.wait_ge(stored, j * 16 + 16)

            @block.tensor
            def _(pe):
                n = n_blocks(pe)

                def turn(b, nth):
                    pe.wait_ge(gathered[b], nth * 16 + 16)
                    for h in range(2):
                        for k in range(4):
                            t = pe.transpose(X[:, h, k, :], xg[:, b, (4 * h + k) * P:(4 * h + k + 1) * P], c.ident[:])
                    t.then_inc(x_done, 1)

                def turn_hidden(j, half):
                    pe.wait_ge(h_ok, j * 2 + (half + 1))
                    for f in range(HT):
                        t = pe.transpose(h_turned(half)[:, f, :], hid[:, f * P:f * P + P], c.ident[:])
                    t.then_inc(turned, 1)

                turn(0, 0)
                pe.wait_ge(bias_ok, 1)
                with pe.Fori(0, NBLK // 2) as it:
                    for u in range(2):
                        j = it * 2 + u
                        with pe.If(j < n):
                            pe.wait_ge(x_low, j + 1)
                            pe.wait_ge(picked, j + 1)
                            for p in range(PIECES):
                                q, second = p // 2, p % 2
                                hi, lo = cut(w_hi[p % RING][:], q), cut(w_lo[p % RING][:], q)
                                if p == 8:
                                    pe.wait_ge(y_ok, j + 1)
                                    pe.wait_ge(h_low, j * 2 + 1)
                                if p == 10:
                                    pe.wait_ge(h_low, j * 2 + 2)
                                pe.wait_ge(w_low, j * PIECES + (STARTED + p + 1))
                                if q < 4:
                                    out = GU[:, q, :]
                                    if not second:
                                        o = D * (q % 2) + CHUNK * (q // 2)
                                        pe.matmul(out, pick[:], bias[:, o:o + CHUNK], start=True, stop=False)
                                    for k in range(4):
                                        kx = 4 * second + k
                                        pe.matmul(out, x_hi[:, kx, :], hi[:, k, :], start=False, stop=False)
                                        pe.matmul(out, x_hi[:, kx, :], lo[:, k, :], start=False, stop=False)
                                        mm = pe.matmul(out, x_lo[:, kx, :], hi[:, k, :], start=False, stop=(kx == KD - 1))
                                else:
                                    for f in range(2):
                                        h = HT * (q - 4) + 2 * second + f
                                        for b in range(2):
                                            cols = slice(b * CHUNK, (b + 1) * CHUNK)
                                            pe.matmul(Y[:, b, :], hid_hi[:, h, :], hi[:, f, cols], start=(h == 0), stop=False)
                                            pe.matmul(Y[:, b, :], hid_hi[:, h, :], lo[:, f, cols], start=False, stop=False)
                                            mm = pe.matmul(Y[:, b, :], hid_lo[:, h, :], hi[:, f, cols], start=False, stop=(h == KD - 1))
                                mm.then_inc(piece_done, 1)
                                if p == 5:
                                    turn_hidden(j, 0)
                                if p == 8:
                                    turn_hidden(j, 1)
                                if p == 9:
                                    with pe.If(j + 1 < n):
                                        turn(1 - u, it + u)

            @block.scalar
            def _(act):
                n = n_blocks(act)

                def high(it, u, p, first=False):
                    r, nth = chunk_of(it, u, p // 2)
                    if p % 2 == 0:
                        act.wait_ge(raw_in[r], nth * 16 + 16)
                    if not first:
                        act.wait_ge(piece_done, it * (2 * PIECES) + (PIECES * u + p + 1 - RING))
                    act.activation(w_hi[p % RING][:], piece_of(r, p), ACT.Copy).then_inc(w_high, 1)

                def x_part(nth):
                    act.wait_ge(x_done, nth + 1)
                    act.activation(x_hi[:, 0:4, :], X[:, 0, :, :], ACT.Copy)
                    act.activation(x_hi[:, 4:8, :], X[:, 1, :, :], ACT.Copy).then_inc(x_high, 1)

                def sigmoid(j, half):
                    act.wait_ge(g_ok, j * 2 + (half + 1))
                    act.activation(sg[:], ga[:], ACT.Sigmoid, scale=SWIGLU).then_inc(sig, 1)

                def hidden(j, half):
                    act.wait_ge(turned, j * 2 + (half + 1))
                    act.activation(h_split(hid_hi, half), h_turned(half), ACT.Copy).then_inc(h_high, 1)

                act.sem_inc(y_ok, 1)
                act.wait_ge(bias_in, 32)
                act.activation(bias[:].rearrange("e (g n) -> e g n", g=2), y[0:2 * EXPERTS, :, :], ACT.Copy).then_inc(bias_high, 1)
                x_part(0)
                for p in range(RING):
                    high(0, 0, p, first=True)
                with act.Fori(0, NBLK // 2) as it:
                    for u in range(2):
                        j = it * 2 + u
                        with act.If(j < n):
                            for p in (4, 5, 6):
                                high(it, u, p)
                            sigmoid(j, 0)
                            high(it, u, 7)
                            high(it, u, 8)
                            hidden(j, 0)
                            high(it, u, 9)
                            high(it, u, 10)
                            sigmoid(j, 1)
                            high(it, u, 11)
                            hidden(j, 1)
                            with act.If(j + 1 < n):
                                high(it + u, 1 - u, 0)
                                x_part(j + 1)
                                for p in range(1, RING):
                                    high(it + u, 1 - u, p)
                            act.wait_ge(piece_done, j * PIECES + PIECES)
                            for b in range(2):
                                ins = act.activation(y[:, u, b * CHUNK:(b + 1) * CHUNK], Y[:, b, :], ACT.Copy,
                                                     scale=slot[:, u, 2:3].bitcast(F32))
                            ins.then_inc(y_ok, 1)

            @block.vector
            def _(dve):
                n = n_blocks(dve)

                def low(it, u, p):
                    r, _ = chunk_of(it, u, p // 2)
                    dve.wait_ge(w_high, it * (2 * PIECES) + (PIECES * u + p + 1))
                    dve.tensor_tensor(w_lo[p % RING][:], piece_of(r, p), w_hi[p % RING][:].bitcast(F32),
                                      ALU.subtract).then_inc(w_low, 1)

                def x_part(nth):
                    dve.wait_ge(x_high, nth + 1)
                    dve.tensor_tensor(x_lo[:, 0:4, :], X[:, 0, :, :], x_hi[:, 0:4, :].bitcast(F32), ALU.subtract)
                    dve.tensor_tensor(x_lo[:, 4:8, :], X[:, 1, :, :], x_hi[:, 4:8, :].bitcast(F32), ALU.subtract).then_inc(x_low, 1)

                def pick_bias(j):
                    e = owner_of(dve, j)
                    E2 = 2 * EXPERTS
                    dve.tensor_tensor(pick[:], c.ident[0:E2, ds(e, 1)].to_broadcast([E2, P]),
                                      c.ident[0:E2, ds(e + EXPERTS, 1)].to_broadcast([E2, P]), ALU.add).then_inc(picked, 1)

                def gate(j, half):
                    dve.wait_ge(piece_done, j * PIECES + (4 * half + 2))
                    dve.tensor_scalar(ga[:], GU[:, 2 * half, :], LIMIT, None, ALU.min).then_inc(g_ok, 1)

                def unit(j, half):
                    dve.wait_ge(piece_done, j * PIECES + (4 * half + 4))
                    dve.tensor_scalar(up[:], GU[:, 2 * half + 1, :], LIMIT, -LIMIT, ALU.min, ALU.max).then_inc(h_chain, 1)
                    dve.wait_ge(sig, j * 2 + (half + 1))
                    dve.tensor_tensor(ga[:], ga[:], sg[:], ALU.mult).then_inc(h_chain, 1)
                    dve.wait_ge(h_chain, j * 4 + (2 * half + 2))
                    dve.scalar_tensor_tensor(out=hid[:], in0=up[:], scalar=1.0, in1=ga[:],
                                             op0=ALU.add, op1=ALU.mult).then_inc(h_ok, 1)

                def hidden(j, half):
                    dve.wait_ge(h_high, j * 2 + (half + 1))
                    dve.tensor_tensor(h_split(hid_lo, half), h_turned(half), h_split(hid_hi, half).bitcast(F32),
                                      ALU.subtract).then_inc(h_low, 1)

                dve.sem_inc(w_low, STARTED)
                dve.wait_ge(bias_high, 1)
                lows = slice(EXPERTS, 2 * EXPERTS)
                lo_rows = bias[lows, :].rearrange("e (g n) -> e g n", g=2)
                dve.tensor_tensor(lo_rows, y[lows, :, :], lo_rows.bitcast(F32), ALU.subtract).then_inc(bias_ok, 1)
                pick_bias(0)
                x_part(0)
                for p in range(RING):
                    low(0, 0, p)
                with dve.Fori(0, NBLK // 2) as it:
                    for u in range(2):
                        j = it * 2 + u
                        with dve.If(j < n):
                            low(it, u, 4)
                            low(it, u, 5)
                            gate(j, 0)
                            low(it, u, 6)
                            unit(j, 0)
                            low(it, u, 7)
                            low(it, u, 8)
                            hidden(j, 0)
                            low(it, u, 9)
                            gate(j, 1)
                            low(it, u, 10)
                            unit(j, 1)
                            low(it, u, 11)
                            hidden(j, 1)
                            with dve.If(j + 1 < n):
                                pick_bias(j + 1)
                                low(it + u, 1 - u, 0)
                                x_part(j + 1)
                                for p in range(1, RING):
                                    low(it + u, 1 - u, p)


def stage_combine(nc, c, a):
    with Stage(nc, "comb") as s:
        r = s.sb("r", [P, M, EK, D])
        loaded = [s.sem(f"loaded{m}") for m in range(M)]
        chain = s.sem("chain")
        src = c.pair_rows.rearrange("(m p k) d -> p m k d", p=P, k=EK)
        with s.block() as block:

            @block.sync
            def _(sp):
                for m in range(M):
                    sp.dma_start(r[:, m, :, :], src[:, m, :, :]).then_inc(loaded[m], 16)

            @block.vector
            def _(dve):
                step = chained(dve, chain)
                for m in range(M):
                    dve.wait_ge(loaded[m], 16)
                    for k in range(EK):
                        step(dve.tensor_tensor(c.h[:, m, :], c.h[:, m, :], r[:, m, k, :], ALU.add))


def program(nc, a, out):
    with ExitStack() as ctx:
        c = Common(nc, ctx)
        c.stream(ctx)
        stage_constants(nc, c)
        with ExitStack() as mixed:
            c.yT = c.sb(mixed, "yT", [P, 2 * KD, T])
            with ExitStack() as front:
                c.front(front)
                with ExitStack() as tmp:
                    c.u_hi = c.sb(tmp, "u_hi", [P, KD, TA], F32R)
                    c.u_lo = c.sb(tmp, "u_lo", [P, KD, TA], F32R)
                    stage_norm_in(nc, c, a)
                    stage_project(nc, c, a)
                stage_conf_norm(nc, c, a)
                stage_ssd(nc, c, a)
            stage_out_proj(nc, c, a, "out1", c.yT, a["w_out"][0], 2 * KD, a["x"][0], 1.0)
        with ExitStack() as peer:
            c.peer(peer)
            with ExitStack() as tmp:
                xn = c.sb(tmp, "xn", [P, M, D])
                stage_token_norm(nc, c, a, "nffn", xn, c.hT, col_w=a["norm_ffn_w"])
            c.split(peer)
            stage_split_x(nc, c)
            with ExitStack() as tmp:
                c.qT = c.sb(tmp, "queriesT", [P, NQ, T])
                stage_queries(nc, c, a)
                stage_peer_scores(nc, c, a)
            stage_gate_matrix(nc, c, a)
            stage_peer_experts(nc, c, a)
        stage_token_norm(nc, c, a, "nfin", c.h, c.hT, row_w=a["norm_final_w"])
        second_block(nc, c, a, out)


def second_block(nc, c, a, out):
    with ExitStack() as mix:
        c.second(mix)
        stage_project2(nc, c, a)
        stage_attention(nc, c, a)
        stage_out_proj(nc, c, a, "out2", c.mixT, a["w_out_2"], KD, None, ALPHA, bias=a["b_out_2"])
    with ExitStack() as moe:
        c.routed(moe)
        stage_token_norm(nc, c, a, "ln1", c.h, c.hT, centre=True, row_w=a["ln1_g_2"], row_b=a["ln1_b_2"], save=c.h_rows)
        stage_route(nc, c, a)
        stage_experts(nc, c, a)
        stage_combine(nc, c, a)
        stage_token_norm(nc, c, a, "ln2", c.h, centre=True, row_w=a["ln2_g_2"], row_b=a["ln2_b_2"], save=out[0])


class Common:

    def __init__(self, nc, ctx):
        self.nc = nc
        self.ident = self.sb(ctx, "ident", [P, P])
        self.ones = self.sb(ctx, "ones", [P, P])
        self.upper = self.sb(ctx, "upper", [P, P])
        self.count = self.sb(ctx, "count", [P, P])
        self.count_i = self.sb(ctx, "count_i", [P, P], I32)

    def sb(self, ctx, name, shape, dt=F32):
        return ctx.enter_context(self.nc.sbuf_tensor(f"all_{name}", shape, dt))

    def stream(self, ctx):
        self.h = self.sb(ctx, "h", [P, M, D])
        self.hT = self.sb(ctx, "hT", [P, KD, T])

    def peer(self, ctx):
        self.idxT = self.sb(ctx, "idxT", [P, 3, T])
        self.early = self.nc.dram_tensor("peer_early", [EARLY, P, G * T], F32, kind="Internal").ap()
        self.gates = self.nc.dram_tensor("peer_gates", [BATCHES, NK, NK * TB], F32, kind="Internal").ap()

    def split(self, ctx):
        self.x_hi = self.sb(ctx, "x_hi", [P, KD, T], F32R)
        self.x_lo = self.sb(ctx, "x_lo", [P, KD, T], F32R)

    def second(self, ctx):
        self.qT = self.sb(ctx, "qT", [P, AJ, T])
        self.kT = self.sb(ctx, "kT", [P, T])
        self.uT2 = self.sb(ctx, "uT2", [P, 4, T])
        self.vtok = self.sb(ctx, "vtok", [P, M, P])
        self.gtok = self.sb(ctx, "gtok", [P, M, 512])
        self.mixT = self.sb(ctx, "mixT", [P, KD, T])

    def routed(self, ctx):
        self.slots = self.sb(ctx, "slots", [P, NBLK + 1, 4], I32)
        self.owner = self.sb(ctx, "owner", [1, NBLK + 1], I32)
        self.table = self.nc.dram_tensor("slot_table", [P * NBLK, 4], I32, kind="Internal").ap()
        self.h_rows = self.nc.dram_tensor("h_rows", [T, D], F32, kind="Internal").ap()
        self.pair_rows = self.nc.dram_tensor("pair_rows", [ROWS, D], F32, kind="Internal").ap()

    def front(self, ctx):
        self.xbcT = self.sb(ctx, "xbcT", [P, 16, TA])
        self.zT = self.sb(ctx, "zT", [P, KD, T])
        self.dt = self.sb(ctx, "dt", [P, M + 1, HEADS])
        self.dta = self.sb(ctx, "dta", [P, M + 1, HEADS])


FRONT = ("x", "meta_tokens", "norm_mix_w", "w_in", "ssd_dt_bias", "conf_taps", "conf_conv_b", "ssd_taps",
         "ssd_conv_b", "ssd_A_log", "ssd_D", "ssd_norm_w", "conf_ln_g", "conf_ln_b")


def layout(inputs):
    import numpy as np
    v = {k: np.asarray(x) for k, x in inputs.items()}

    def channels(x):
        return np.ascontiguousarray(x.reshape(-1, P).T)

    def channel_rows(x):
        return np.ascontiguousarray(x.reshape(x.shape[0], -1, P).transpose(2, 1, 0))

    out = {k: v[k] for k in ("x", "meta_tokens", "w_in", "ssd_dt_bias", "ssd_A_log")}
    for k in ("norm_mix_w", "conf_conv_b", "ssd_conv_b", "ssd_norm_w", "conf_ln_g", "conf_ln_b"):
        out[k] = channels(v[k][0])
    out["conf_taps"] = channel_rows(v["conf_conv_w"][0])
    out["ssd_taps"] = channel_rows(v["ssd_conv_w"][0])
    out["ssd_D"] = channels(np.repeat(v["ssd_D"][0], 64))
    keys = np.stack([v["peer_sub_keys_1"][0], v["peer_sub_keys_2"][0]], 1)
    out["peer_keysT"] = np.ascontiguousarray(keys.reshape(2 * PH, NK, P).transpose(2, 0, 1))
    for k in ("w_out", "peer_w_query", "peer_w_up"):
        out[k] = v[k]
    out["peer_w_downT"] = np.ascontiguousarray(v["peer_w_down"][0].T)
    out["norm_ffn_w"] = channels(v["norm_ffn_w"][0])
    out["norm_final_w"] = v["norm_final_w"][None]
    heads = np.arange(AH * 64).reshape(2, AJ, 64).transpose(1, 0, 2).reshape(-1)
    cols = np.concatenate([heads, np.arange(AH * 64, 1792)])
    out["w_in_2"] = np.ascontiguousarray(v["w_in_2"][0][:, cols])
    out["b_in_2_col"] = channels(v["b_in_2"][0][cols])
    out["b_in_2_row"] = np.concatenate([v["b_in_2"][:, COL_V:COL_U], v["b_in_2"][:, COL_S:]], 1)
    out["w_out_2"] = np.ascontiguousarray(v["w_out_2"][0][np.concatenate([heads, np.arange(AH * 64, D)])])
    out["w_spatial_2T"] = np.ascontiguousarray(v["w_spatial_2"][0].transpose(2, 0, 1))
    bias = np.stack([v["b_gate_2"][0], v["b_up_2"][0]], 1)
    out["bias_gate_up"] = np.ascontiguousarray(bias)
    for k in ("ln_v_g_2", "ln_v_b_2", "sinks_2", "b_spatial_2", "b_out_2", "ln1_g_2", "ln1_b_2", "w_router_2",
              "b_router_2", "w_gate_2", "w_up_2", "w_down_2", "b_down_2", "ln2_g_2", "ln2_b_2"):
        out[k] = v[k]
    return out


def kernel(**inputs):
    from concourse import bacc
    from concourse.bass_utils import run_bass_kernel_spmd

    nc = bacc.Bacc("TRN2", target_bir_lowering=False, num_devices=1)
    arrays = {f"in_{k}": x for k, x in layout(inputs).items()}
    a = {k[3:]: nc.dram_tensor(k, x.shape, F32, kind="ExternalInput").ap() for k, x in arrays.items()}
    out = nc.dram_tensor("out", (1, T, D), F32, kind="ExternalOutput").ap()
    program(nc, a, out)
    r = run_bass_kernel_spmd(nc, [arrays], core_ids=[0])
    return r.results[0]["out"]
```
